# Optimizing a Trainium2 kernel written in Bass

```python
import jax, jax.numpy as jnp
from jax import lax
import numpy as np

'''Two layers of a hybrid decoder trunk with parallel head groups (Hymba-style).

Each layer:  x += W_out [ RetNet retention | MoBA block-sparse attention | chunked gMLP gate ]( W_in RMSNorm(x) )
             x += SwiGLU(RMSNorm(x))   (dense on even layers, top-2-of-8 experts on odd layers)
then a final RMSNorm.
Input x: (BATCH, SEQ, D_MODEL) float32.  Output: (BATCH, SEQ, D_MODEL).
'''

D_MODEL = 1024
BATCH = 1
SEQ = 256
DEPTH = 2

HEAD_DIM = 64
RET_HEADS = 6
MOBA_HEADS = 6
GMLP_GROUPS = 4
RET_WIDTH = RET_HEADS * HEAD_DIM
MOBA_WIDTH = MOBA_HEADS * HEAD_DIM
GMLP_WIDTH = GMLP_GROUPS * HEAD_DIM
MIX_WIDTH = RET_WIDTH + MOBA_WIDTH + GMLP_WIDTH
IN_WIDTH = 4 * RET_WIDTH + 3 * MOBA_WIDTH + 2 * GMLP_WIDTH
RET_CHUNK = 128
MOBA_BLOCK = 256
MOBA_TOPK = 3
MOBA_QBLOCK = 128
GMLP_CHUNK = 128
D_FF = 3584
N_EXPERTS = 8
TOP_K_EXPERTS = 2
NORM_EPS = 1e-6
GN_EPS = 1e-5

kernel_name = 'hybrid_retention_moba_gmlp_moe'

F32 = jnp.float32

def rmsnorm(x, g):
    xf = x.astype(F32)
    y = xf * lax.rsqrt(jnp.mean(xf * xf, axis=-1, keepdims=True) + NORM_EPS)
    return (y * g.astype(F32)).astype(x.dtype)

def retention(q, k, v):
    B, S, H, D = q.shape
    C = RET_CHUNK
    N = S // C
    dt = q.dtype
    log_g = jnp.log(1.0 - 2.0 ** (-5.0 - jnp.arange(H, dtype=F32)))
    pos = jnp.arange(C, dtype=F32)
    diff = pos[:, None] - pos[None, :]
    decay = jnp.where(diff >= 0, jnp.exp(log_g[:, None, None] * jnp.maximum(diff, 0.0)), 0.0)
    zeta = jnp.exp(log_g[:, None] * (C - 1 - pos))
    xi = jnp.exp(log_g[:, None] * (pos + 1))
    chunk_decay = jnp.exp(log_g * C)

    def to_chunks(t):
        return t.astype(F32).reshape(B, N, C, H, D).transpose(0, 3, 1, 2, 4)

    qc = to_chunks(q)
    kc = to_chunks(k) * (D ** -0.5)
    vc = to_chunks(v)
    scores = jnp.einsum('bhnid,bhnjd->bhnij', qc, kc) * decay[None, :, None]
    intra = jnp.einsum('bhnij,bhnjd->bhnid', scores, vc)
    kv = jnp.einsum('bhncd,bhnce->nbhde', kc * zeta[None, :, None, :, None], vc)

    def step(state, kv_n):
        return state * chunk_decay[None, :, None, None] + kv_n, state

    _, prev = lax.scan(step, jnp.zeros((B, H, D, D), F32), kv)
    cross = jnp.einsum('bhncd,nbhde->bhnce', qc * xi[None, :, None, :, None], prev)
    o = intra + cross
    mu = jnp.mean(o, axis=-1, keepdims=True)
    var = jnp.mean(jnp.square(o - mu), axis=-1, keepdims=True)
    o = (o - mu) * lax.rsqrt(var + GN_EPS)
    return o.transpose(0, 2, 3, 1, 4).reshape(B, S, H * D).astype(dt)

def moba_attention(q, k, v):
    B, S, H, D = q.shape
    BS = MOBA_BLOCK
    QB = MOBA_QBLOCK
    NB = -(-S // BS)
    NQ = S // QB
    TOPK = min(MOBA_TOPK, NB)
    pad = NB * BS - S
    dt = q.dtype
    slopes = 2.0 ** (-8.0 * jnp.arange(1, H + 1, dtype=F32) / H)

    def to_bh(t):
        return t.astype(F32).transpose(0, 2, 1, 3)

    kb = jnp.pad(to_bh(k), ((0, 0), (0, 0), (0, pad), (0, 0))).reshape(B, H, NB, BS, D)
    vb = jnp.pad(to_bh(v), ((0, 0), (0, 0), (0, pad), (0, 0))).reshape(B, H, NB, BS, D)
    kmean = jnp.mean(kb, axis=3)
    q_blocks = (to_bh(q) * (D ** -0.5)).reshape(B, H, NQ, QB, D).transpose(2, 0, 1, 3, 4)
    offs = jnp.arange(BS, dtype=jnp.int32)
    blk_ids = jnp.arange(NB, dtype=jnp.int32)

    def one_block(args):
        q_blk, qi = args
        ob = (qi * QB) // BS
        t = qi * QB + jnp.arange(QB, dtype=jnp.int32)
        bscore = jnp.einsum('bhqd,bhjd->bhqj', q_blk, kmean)
        bscore = jnp.where(blk_ids < ob, bscore, -jnp.inf)
        _, idx = lax.top_k(bscore, TOPK)
        valid = idx < ob
        gidx = idx.reshape(B, H, QB * TOPK)[:, :, :, None, None]
        kg = jnp.take_along_axis(kb, gidx, axis=2).reshape(B, H, QB, TOPK, BS, D)
        vg = jnp.take_along_axis(vb, gidx, axis=2).reshape(B, H, QB, TOPK, BS, D)
        s_pos = idx[..., None] * BS + offs
        dist_sel = (t[:, None, None] - s_pos).astype(F32)
        s_sel = jnp.einsum('bhqd,bhqjsd->bhqjs', q_blk, kg) - slopes[:, None, None, None] * dist_sel
        s_sel = jnp.where(valid[..., None], s_sel, -jnp.inf)
        k_own = lax.dynamic_index_in_dim(kb, ob, axis=2, keepdims=False)
        v_own = lax.dynamic_index_in_dim(vb, ob, axis=2, keepdims=False)
        own_pos = ob * BS + offs
        dist_own = (t[:, None] - own_pos[None, :]).astype(F32)
        s_own = jnp.einsum('bhqd,bhsd->bhqs', q_blk, k_own) - slopes[:, None, None] * dist_own
        s_own = jnp.where(own_pos[None, :] <= t[:, None], s_own, -jnp.inf)
        scores = jnp.concatenate([s_sel.reshape(B, H, QB, TOPK * BS), s_own], axis=-1)
        p = jax.nn.softmax(scores, axis=-1)
        p_sel = p[..., :TOPK * BS].reshape(B, H, QB, TOPK, BS)
        p_own = p[..., TOPK * BS:]
        return (jnp.einsum('bhqjs,bhqjsd->bhqd', p_sel, vg)
                + jnp.einsum('bhqs,bhsd->bhqd', p_own, v_own))

    out = lax.map(one_block, (q_blocks, jnp.arange(NQ, dtype=jnp.int32)))
    return out.transpose(1, 0, 3, 2, 4).reshape(B, S, H * D).astype(dt)

def gmlp_spatial_gate(u, v, w_s, b_s):
    B, S, W = u.shape
    C = GMLP_CHUNK
    N = S // C
    G = GMLP_GROUPS
    Dg = W // G
    u = jax.nn.gelu(u)
    vf = jax.nn.gelu(v).astype(F32)
    mu = jnp.mean(vf, axis=-1, keepdims=True)
    var = jnp.mean(jnp.square(vf - mu), axis=-1, keepdims=True)
    vn = ((vf - mu) * lax.rsqrt(var + GN_EPS)).reshape(B, N, C, G, Dg)
    w = w_s.astype(F32) * jnp.tril(jnp.ones((C, C), F32))[None]
    mixed = jnp.einsum('gij,bnjgd->bnigd', w, vn) + b_s.astype(F32).T[None, None, :, :, None]
    return u * mixed.reshape(B, S, W).astype(u.dtype)

def mixer_block(x, norm_g, w_in, w_out, gmlp_w, gmlp_b):
    B, S, _ = x.shape
    h = rmsnorm(x, norm_g)
    proj = h @ w_in
    cuts = np.cumsum([RET_WIDTH] * 4 + [MOBA_WIDTH] * 3 + [GMLP_WIDTH] * 2)[:-1].tolist()
    rq, rk, rv, rg, mq, mk, mv, gu, gv = jnp.split(proj, cuts, axis=-1)
    heads = lambda t, n: t.reshape(B, S, n, HEAD_DIM)
    ret = retention(heads(rq, RET_HEADS), heads(rk, RET_HEADS), heads(rv, RET_HEADS)) * jax.nn.silu(rg)
    moba = moba_attention(heads(mq, MOBA_HEADS), heads(mk, MOBA_HEADS), heads(mv, MOBA_HEADS))
    gm = gmlp_spatial_gate(gu, gv, gmlp_w, gmlp_b)
    y = jnp.concatenate([ret, moba, gm], axis=-1) @ w_out
    return x + y

def swiglu(h, w_gate, w_up, w_down):
    return (jax.nn.silu(h @ w_gate) * (h @ w_up)) @ w_down

def moe_swiglu(h, router, we_gate, we_up, we_down):
    logits = (h @ router).astype(F32)
    top_val, top_idx = lax.top_k(logits, TOP_K_EXPERTS)
    gates = jax.nn.softmax(top_val, axis=-1)
    dense_gate = jnp.sum(jax.nn.one_hot(top_idx, N_EXPERTS, dtype=F32) * gates[..., None], axis=-2)
    out = jnp.zeros_like(h)
    for e in range(N_EXPERTS):
        out = out + dense_gate[..., e:e + 1].astype(h.dtype) * swiglu(h, we_gate[e], we_up[e], we_down[e])
    return out

def setup_inputs(seed: int = 0) -> dict:
    key = jax.random.key(seed)
    keys = jax.random.split(key, 24)

    def nrm(i, shape, scale):
        return jax.random.normal(keys[i], shape, F32) * scale

    d = D_MODEL ** -0.5
    f = D_FF ** -0.5
    c = 0.5 * GMLP_CHUNK ** -0.5
    return {
        'x': nrm(0, (BATCH, SEQ, D_MODEL), 1.0),
        'l0_mix_norm': 1.0 + nrm(1, (D_MODEL,), 0.05),
        'l0_w_in': nrm(2, (D_MODEL, IN_WIDTH), d),
        'l0_w_out': nrm(3, (MIX_WIDTH, D_MODEL), MIX_WIDTH ** -0.5),
        'l0_gmlp_w': nrm(4, (GMLP_GROUPS, GMLP_CHUNK, GMLP_CHUNK), c),
        'l0_gmlp_b': 1.0 + nrm(5, (GMLP_GROUPS, GMLP_CHUNK), 0.1),
        'l0_ffn_norm': 1.0 + nrm(6, (D_MODEL,), 0.05),
        'l0_w_gate': nrm(7, (D_MODEL, D_FF), d),
        'l0_w_up': nrm(8, (D_MODEL, D_FF), d),
        'l0_w_down': nrm(9, (D_FF, D_MODEL), f),
        'l1_mix_norm': 1.0 + nrm(10, (D_MODEL,), 0.05),
        'l1_w_in': nrm(11, (D_MODEL, IN_WIDTH), d),
        'l1_w_out': nrm(12, (MIX_WIDTH, D_MODEL), MIX_WIDTH ** -0.5),
        'l1_gmlp_w': nrm(13, (GMLP_GROUPS, GMLP_CHUNK, GMLP_CHUNK), c),
        'l1_gmlp_b': 1.0 + nrm(14, (GMLP_GROUPS, GMLP_CHUNK), 0.1),
        'l1_ffn_norm': 1.0 + nrm(15, (D_MODEL,), 0.05),
        'l1_router': nrm(16, (D_MODEL, N_EXPERTS), d),
        'l1_we_gate': nrm(17, (N_EXPERTS, D_MODEL, D_FF), d),
        'l1_we_up': nrm(18, (N_EXPERTS, D_MODEL, D_FF), d),
        'l1_we_down': nrm(19, (N_EXPERTS, D_FF, D_MODEL), f),
        'final_norm': 1.0 + nrm(20, (D_MODEL,), 0.05),
    }

def reference(x, l0_mix_norm, l0_w_in, l0_w_out, l0_gmlp_w, l0_gmlp_b, l0_ffn_norm,
              l0_w_gate, l0_w_up, l0_w_down,
              l1_mix_norm, l1_w_in, l1_w_out, l1_gmlp_w, l1_gmlp_b, l1_ffn_norm,
              l1_router, l1_we_gate, l1_we_up, l1_we_down, final_norm):
    mix_params = [(l0_mix_norm, l0_w_in, l0_w_out, l0_gmlp_w, l0_gmlp_b),
                  (l1_mix_norm, l1_w_in, l1_w_out, l1_gmlp_w, l1_gmlp_b)]
    ffn_norms = [l0_ffn_norm, l1_ffn_norm]
    ffn_params = [(l0_w_gate, l0_w_up, l0_w_down),
                  (l1_router, l1_we_gate, l1_we_up, l1_we_down)]
    for layer in range(DEPTH):
        x = mixer_block(x, *mix_params[layer])
        h = rmsnorm(x, ffn_norms[layer])
        if layer % 2 == 0:
            x = x + swiglu(h, *ffn_params[layer])
        else:
            x = x + moe_swiglu(h, *ffn_params[layer])
    return rmsnorm(x, final_norm)


_drawn_inputs = setup_inputs


def setup_inputs(seed=0):
    import zlib

    import numpy as np

    out = dict(_drawn_inputs(seed))
    spreads = {}
    factors = {}
    for name, (base, spread) in spreads.items():
        noise = np.random.default_rng([zlib.crc32(name.encode()), seed]).standard_normal(out[name].shape)
        drawn = base * np.exp(spread * noise) if base else spread * noise
        out[name] = __import__('jax').numpy.asarray(drawn.astype(out[name].dtype))
    for name, factor in factors.items():
        out[name] = (out[name] * factor).astype(out[name].dtype)
    return out
```

```python
import numpy as np
import concourse.bass as bass
from concourse import mybir
from contextlib import ExitStack

F32 = mybir.dt.float32
F32R = mybir.dt.float32r
I32 = mybir.dt.int32
U32 = mybir.dt.uint32
ALU = mybir.AluOpType
ACT = mybir.ActivationFunctionType
AX = mybir.AxisListType

P = 128
BANK = 512
D_MODEL, SEQ, D_FF = 1024, 256, 3584
HEADS, HEAD = 6, 64
GROUPS, CHUNK = 4, 128
WIDTH = HEADS * HEAD
G_WIDTH = GROUPS * HEAD
IN_WIDTH = 7 * WIDTH + 2 * G_WIDTH
EXPERTS, MAX_JOBS = 8, 12
TT = SEQ // P
KT = D_MODEL // P
NORM_EPS, GN_EPS = 1e-6, 1e-5

C_RQ, C_RK, C_RV, C_RG = (i * WIDTH for i in range(4))
C_MQ, C_MK, C_MV = (i * WIDTH for i in range(4, 7))
C_GU = 7 * WIDTH
C_GV = C_GU + G_WIDTH

UNIT = 2048
RAW_SLOTS, SPLIT_SLOTS = 6, 3
IN_CHUNKS = -(-IN_WIDTH // BANK)
IN_UNITS = [(c, h) for c in range(IN_CHUNKS - 1) for h in range(2)] + [(IN_CHUNKS - 1, 0)]
CHUNK_END = [max(i for i, (c, _) in enumerate(IN_UNITS) if c == chunk) + 1 for chunk in range(IN_CHUNKS)]
OUT_UNITS = [(half, h) for half in range(2) for h in range(2)]
FF_CHUNKS = D_FF // BANK


def ffn_units():
    units = []
    for c in range(FF_CHUNKS):
        units += [("gate", c, 0), ("gate", c, 1), ("up", c, 0), ("up", c, 1)]
        if c >= 2:
            units += [("down", c - 2, 0), ("down", c - 2, 1)]
    return units + [("down", c, h) for c in (FF_CHUNKS - 2, FF_CHUNKS - 1) for h in range(2)]


FFN = ffn_units()
LAST_UP = {c: FFN.index(("up", c, 1)) for c in range(FF_CHUNKS)}
LAST_GATE = {c: FFN.index(("gate", c, 1)) for c in range(FF_CHUNKS)}
TRANSPOSE_AFTER = {c: LAST_UP[c + 1] for c in range(FF_CHUNKS - 1)} | {FF_CHUNKS - 1: FFN.index(("down", FF_CHUNKS - 3, 1))}
LAYER_UNITS = len(IN_UNITS) + len(OUT_UNITS)
DENSE_AT = LAYER_UNITS
IN_AT = [0, DENSE_AT + len(FFN)]
OUT_AT = [a + len(IN_UNITS) for a in IN_AT]
MOE_AT = OUT_AT[1] + len(OUT_UNITS)
assert len(FFN) % RAW_SLOTS == 0 and len(FFN) % SPLIT_SLOTS == 0


def shape_tables():
    i = np.arange(P)
    f = np.float32
    causal_t = (i[:, None] <= i[None, :]).astype(f)
    log_g = np.log(f(1.0) - f(2.0) ** (f(-5.0) - np.arange(HEADS, dtype=f))).astype(f)
    d = np.arange(SEQ)[None, :] - i[:, None]
    wide = np.where(d >= 0, np.exp(log_g[:, None, None] * np.maximum(d, 0)), 0.0)
    decay = np.concatenate([wide, wide[:, :, :P]], axis=2) * HEAD ** -0.5
    slopes = f(2.0) ** (f(-8.0) * np.arange(1, HEADS + 1, dtype=f) / f(HEADS))
    dist = (i[:, None] + P - np.arange(SEQ)[None, :])
    own = np.where(dist >= 0, -slopes[:, None, None] * dist, -1e30)
    alibi = np.concatenate([own[:, :, P:], own], axis=2)
    flat = lambda t: t.transpose(1, 0, 2).reshape(P, -1)
    iota = np.tile(np.arange(1, P + 1), (P, 1))
    return np.concatenate([np.eye(P), causal_t, np.ones((P, P)), iota, flat(decay), flat(alibi)], axis=1).astype(f)


def hybrid_trunk(nc, ins, out):
    x_d, tables_d = ins["x"][0], ins["tables"]
    norm_d = [ins[n] for n in ("l0_mix_norm", "l0_ffn_norm", "l1_mix_norm", "l1_ffn_norm", "final_norm")]
    w_in_d = [ins["l0_w_in"], ins["l1_w_in"]]
    w_out_d = [ins["l0_w_out"], ins["l1_w_out"]]

    ctx = ExitStack()
    with ctx:
        def sem(name):
            return ctx.enter_context(nc.semaphore(name))

        def sb(name, cols, dt=F32, stack=ctx):
            return stack.enter_context(nc.sbuf_tensor(name, [P, cols], dt))

        small = sb("small", 4 * P)
        identity, causal_t, ones, count_up = (small[:, k * P:(k + 1) * P] for k in range(4))
        masks = sb("masks", 2 * HEADS * 3 * P)
        decay = masks[:, 0:HEADS * 3 * P].rearrange("p (h n) -> p h n", h=HEADS)
        alibi = masks[:, HEADS * 3 * P:].rearrange("p (h n) -> p h n", h=HEADS)
        x_sb = sb("x_sb", TT * D_MODEL)
        x_res = x_sb[:, :].rearrange("p (t n) -> p t n", t=TT)
        rows_sb = sb("rows_sb", TT * D_MODEL)
        rows = rows_sb[:, :].rearrange("p (t n) -> p t n", t=TT)
        gain = sb("gain", D_MODEL)
        h_hi = sb("h_hi", KT * SEQ, F32R)
        h_lo = sb("h_lo", KT * SEQ, F32R)
        raw = sb("raw", RAW_SLOTS * UNIT)
        w_hi = sb("w_hi", SPLIT_SLOTS * UNIT, F32R)
        w_lo = sb("w_lo", SPLIT_SLOTS * UNIT, F32R)
        stat = sb("stat", 128)
        gmlp_bias = sb("gmlp_bias", 2 * GROUPS)
        exponent = sb("exponent", 2 * HEADS)
        router_w = sb("router_w", KT * EXPERTS)
        router_hi = sb("router_hi", KT * EXPERTS, F32R)
        router_lo = sb("router_lo", KT * EXPERTS, F32R)
        jobs_i = sb("jobs_i", 16, I32)

        with ExitStack() as mixer:
            proj_sb = sb("proj_sb", TT * IN_WIDTH, stack=mixer)
            qk_sb = sb("qk_sb", 12 * SEQ, stack=mixer)
            ret_w = sb("ret_w", 2 * 3 * P, stack=mixer)
            att_p = sb("att_p", 2 * 3 * P, stack=mixer)
            att_pt = sb("att_pt", 2 * 3 * P, stack=mixer)
            gmlp_w = sb("gmlp_w", 2 * GROUPS * CHUNK, stack=mixer)
        proj = proj_sb[:, :].rearrange("p (t n) -> p t n", t=TT)
        qk_t = qk_sb[:, :].rearrange("p (m n) -> p m n", m=12)

        ffn = ctx.enter_context(ExitStack())
        gate_s = sb("gate_s", TT * BANK, stack=ffn)
        act_s = sb("act_s", TT * BANK, stack=ffn)
        actt_hi = sb("actt_hi", 2 * TT * BANK, F32R, stack=ffn)
        actt_lo = sb("actt_lo", 2 * TT * BANK, F32R, stack=ffn)
        rows_hi = sb("rows_hi", TT * D_MODEL, F32R, stack=ffn)
        rows_lo = sb("rows_lo", TT * D_MODEL, F32R, stack=ffn)
        y_hi = sb("y_hi", D_MODEL, F32R, stack=ffn)
        y_lo = sb("y_lo", D_MODEL, F32R, stack=ffn)
        slots = sb("slots", TT * P, F32R, stack=ffn)
        slots_t = sb("slots_t", TT * P, F32R, stack=ffn)
        route = sb("route", 320, stack=ffn)
        index_u = sb("index_u", TT * EXPERTS, U32, stack=ffn)

        ps_all = ctx.enter_context(nc.psum_tensor("ps_all", [P, 8 * BANK], F32))
        ps = ps_all[:, :].rearrange("p (b n) -> p b n", b=8)

        unit_landed = [sem(f"unit_landed{s}") for s in range(RAW_SLOTS)]
        hi_ready, lo_ready, unit_used = sem("hi_ready"), sem("lo_ready"), sem("unit_used")
        x_landed, tables_landed, masks_landed, bias_landed = (sem(n) for n in ("x_landed", "tables_landed", "masks_landed", "bias_landed"))
        router_landed, out_landed = sem("router_landed"), sem("out_landed")
        gmlp_w_landed = [sem("gmlp_w_landed0"), sem("gmlp_w_landed1")]
        gain_landed, exponent_set = sem("gain_landed"), sem("exponent_set")
        x_written, sumsq_ready, meansq_ready, rstd_ready, rows_ready = (sem(n) for n in ("x_written", "sumsq_ready", "meansq_ready", "rstd_ready", "rows_ready"))
        mix_ready, rows_turned, h_hi_ready, h_ready = (sem(n) for n in ("mix_ready", "rows_turned", "h_hi_ready", "h_ready"))
        proj_act, proj_dve = sem("proj_act"), sem("proj_dve")
        qk_turned, qk_act, qk_dve = sem("qk_turned"), sem("qk_act"), sem("qk_dve")
        ret_scored, ret_decayed, ret_out = sem("ret_scored"), sem("ret_decayed"), sem("ret_out")
        att_scored, att_biased, att_exped, p_turned, pt_ready, att_out = (sem(n) for n in ("att_scored", "att_biased", "att_exped", "p_turned", "pt_ready", "att_out"))
        gelu_ready, silu_ready, gate_var, gate_rstd, gv_ready, gmlp_masked, gmlp_out, ret_var, ret_rstd = (
            sem(n) for n in ("gelu_ready", "silu_ready", "gate_var", "gate_rstd", "gv_ready", "gmlp_masked", "gmlp_out", "ret_var", "ret_rstd"))
        silu_done, act_ready, act_turned, actt_hi_ready, actt_ready = (
            sem(n) for n in ("silu_done", "act_ready", "act_turned", "actt_hi_ready", "actt_ready"))
        router_hi_ready, router_ready, rows_hi_ready, rows_split, logits_ready, gap_ready, gap_exped, mask_ready, counted, jobs_ready = (
            sem(n) for n in ("router_hi_ready", "router_ready", "rows_hi_ready", "rows_split", "logits_ready", "gap_ready", "gap_exped", "mask_ready", "counted", "jobs_ready"))
        slots_ready, gathered, slots_turned, slots_t_ready, y_zeroed, y_hi_ready, y_ready, scattered, x_added = (
            sem(n) for n in ("slots_ready", "gathered", "slots_turned", "slots_t_ready", "y_zeroed", "y_hi_ready", "y_ready", "scattered", "x_added"))
        dve_step, place_copied = sem("dve_step"), sem("place_copied")

        sumsq, meansq, rstd = stat[:, 0:2], stat[:, 2:4], stat[:, 4:6]
        ret_mean, ret_sq, ret_rs = stat[:, 8:20], stat[:, 20:32], stat[:, 32:44]
        att_nmax, att_sum, att_rinv = stat[:, 44:46 + 2], stat[:, 48:60], stat[:, 60:72]
        bn6, bn2, gate_rs = stat[:, 72:84], stat[:, 84:88], stat[:, 88:90]
        scaled = stat[:, 90:102]

        logits = route[:, 0:16].rearrange("p (t e) -> p t e", t=TT)
        top = route[:, 16:32].rearrange("p (t e) -> p t e", t=TT)
        top_at = route[:, 32:48].rearrange("p (t e) -> p t e", t=TT)
        first, second, mask, gates = (route[:, 48 + 16 * k:64 + 16 * k].rearrange("p (t e) -> p t e", t=TT) for k in range(4))
        gap, gap_e, g_den, g_one, g_two = (route[:, 112 + 2 * k:114 + 2 * k] for k in range(5))
        counts = route[:, 124:148]
        over, over_rank, pick = (route[:, 148 + 8 * k:156 + 8 * k] for k in range(3))
        product = route[:, 172:188].rearrange("p (t e) -> p t e", t=TT)
        place = route[:, 188:188 + TT * MAX_JOBS].rearrange("p (t j) -> p t j", t=TT)
        weight = route[:, 212:212 + TT * MAX_JOBS].rearrange("p (t j) -> p t j", t=TT)
        jobs = route[:, 236:252]
        cur_place, cur_weight, slot_gate = route[:, 252:254], route[:, 254:256], route[:, 256:257]

        def slot(t, s, n):
            return t[:, s * UNIT:s * UNIT + n]

        def part(t, s, parts, k, lo=0, n=BANK, width=BANK):
            a = s * UNIT + k * width + lo
            return t[:, a:a + n]

        block = ctx.enter_context(nc.Block())

        @block.sync
        def _(sp):
            def load(n, s, dst_cols, parts, src):
                if not isinstance(n, int) or n >= RAW_SLOTS:
                    sp.wait_ge(lo_ready, n - RAW_SLOTS + 1)
                dst = slot(raw, s % RAW_SLOTS, dst_cols).rearrange("p (k n) -> p k n", k=parts)
                sp.dma_start(dst, src).then_inc(unit_landed[s % RAW_SLOTS], 16)

            def rows_of(w, r0, nr, c0, ncol):
                return w[r0:r0 + nr * P, c0:c0 + ncol].rearrange("(k p) n -> p k n", p=P)

            def load_mixer_in(layer):
                for i, (c, h) in enumerate(IN_UNITS):
                    n = IN_AT[layer] + i
                    if c < IN_CHUNKS - 1:
                        load(n, n, UNIT, 4, rows_of(w_in_d[layer], h * 4 * P, 4, c * BANK, BANK))
                    else:
                        load(n, n, KT * P, KT, rows_of(w_in_d[layer], 0, KT, c * BANK, P))

            def load_mixer_out(layer):
                for i, (half, h) in enumerate(OUT_UNITS):
                    n = OUT_AT[layer] + i
                    load(n, n, UNIT, 4, rows_of(w_out_d[layer], h * 4 * P, 4, half * BANK, BANK))

            def load_ffn(n0, s0, gate, up, down):
                for i, (kind, c, h) in enumerate(FFN):
                    if kind == "down":
                        src = rows_of(down, (4 * c + 2 * h) * P, 2, 0, D_MODEL)
                        load(n0 + i, s0 + i, UNIT, 2, src)
                    else:
                        src = rows_of(gate if kind == "gate" else up, h * 4 * P, 4, c * BANK, BANK)
                        load(n0 + i, s0 + i, UNIT, 4, src)

            load_mixer_in(0)
            load_mixer_out(0)
            load_ffn(DENSE_AT, DENSE_AT, ins["l0_w_gate"], ins["l0_w_up"], ins["l0_w_down"])
            load_mixer_in(1)
            load_mixer_out(1)
            load_ffn(MOE_AT, MOE_AT, ins["l1_we_gate"][0], ins["l1_we_up"][0], ins["l1_we_down"][0])
            sp.wait_ge(jobs_ready, 1)
            n_jobs = sp.value_load(jobs_i[0:1, 15:16], min_val=EXPERTS, max_val=MAX_JOBS - 1)
            with sp.Fori(1, n_jobs) as j:
                e = sp.value_load(jobs_i[0:1, bass.ds(j, 1)], min_val=0, max_val=EXPERTS - 1)
                pick_expert = lambda w: w[bass.ds(e, 1), :, :].rearrange("a r c -> (a r) c")
                load_ffn(MOE_AT + len(FFN) * j, MOE_AT, *(pick_expert(ins[w]) for w in ("l1_we_gate", "l1_we_up", "l1_we_down")))
            sp.wait_ge(rows_ready, 5)
            sp.dma_start(out[0].rearrange("(t p) n -> p t n", p=P), rows).then_inc(out_landed, 16)
            sp.wait_ge(out_landed, 16)

        @block.gpsimd
        def _(pool):
            def load_gain(n):
                pool.dma_start(gain[:, :], norm_d[n].rearrange("(a n) -> a n", a=1).to_broadcast([P, D_MODEL])).then_inc(gain_landed, 16)

            def inverse_root(dst, src, w, ready, value, done):
                pool.wait_ge(ready, value)
                nc.gpsimd.tensor_tensor(dst, src, exponent[:, 0:w], ALU.pow).then_inc(done, 1)

            load_gain(0)
            nc.gpsimd.memset(exponent[:, :], -0.5).then_inc(exponent_set, 1)
            pool.wait_ge(exponent_set, 1)
            for n in range(5):
                inverse_root(rstd, meansq, 2, meansq_ready, n + 1, rstd_ready)
                if n in (0, 2):
                    layer = n // 2
                    pool.wait_ge(rows_ready, n + 1)
                    load_gain(n + 1)
                    inverse_root(gate_rs, bn2.rearrange("p (t s) -> p s t", t=TT)[:, 1, :], 2, gate_var, layer + 1, gate_rstd)
                    inverse_root(ret_rs, ret_sq, 2 * HEADS, ret_var, layer + 1, ret_rstd)
                elif n < 4:
                    pool.wait_ge(rows_ready, n + 1)
                    load_gain(n + 1)

        @block.scalar
        def _(act):
            def split_hi(n, s, cols=UNIT, job=None):
                landed = 16 * (s // RAW_SLOTS + 1)
                act.wait_ge(unit_landed[s % RAW_SLOTS], landed if job is None else job * (16 * (len(FFN) // RAW_SLOTS)) + landed)
                if job is not None or n >= SPLIT_SLOTS:
                    act.wait_ge(unit_used, n - SPLIT_SLOTS + 1)
                nc.scalar.activation(slot(w_hi, s % SPLIT_SLOTS, cols), slot(raw, s % RAW_SLOTS, cols), ACT.Copy).then_inc(hi_ready, 1)

            def norm_sums(n, ready, value):
                act.wait_ge(ready, value)
                if n:
                    act.wait_ge(rows_ready, n)
                for t in range(TT):
                    last = nc.scalar.activation(rows[:, t, :], x_res[:, t, :], ACT.Square, accum_out=sumsq[:, t:t + 1])
                last.then_inc(sumsq_ready, 1)

            def turned_hi(r):
                for b in range(4):
                    act.wait_ge(rows_turned, 4 * r + b + 1)
                    nc.scalar.activation(h_hi[:, b * BANK:(b + 1) * BANK], ps[:, b, :], ACT.Copy).then_inc(h_hi_ready, 1)

            def mixer(layer):
                for i in range(min(2, len(IN_UNITS))):
                    split_hi(IN_AT[layer] + i, IN_AT[layer] + i)
                for c in range(IN_CHUNKS):
                    for i in (2 * c + 2, 2 * c + 3):
                        if i < len(IN_UNITS):
                            split_hi(IN_AT[layer] + i, IN_AT[layer] + i, UNIT if i < len(IN_UNITS) - 1 else KT * P)
                    width = BANK if c < IN_CHUNKS - 1 else P
                    act.wait_ge(unit_used, IN_AT[layer] + CHUNK_END[c])
                    nc.scalar.activation(proj[:, 0, c * BANK:c * BANK + width], ps[:, 2 * (c % 2), 0:width], ACT.Copy).then_inc(proj_act, 1)
                for i in range(SPLIT_SLOTS):
                    split_hi(OUT_AT[layer] + i, OUT_AT[layer] + i)
                act.wait_ge(proj_act, IN_CHUNKS * (layer + 1))
                act.wait_ge(proj_dve, IN_CHUNKS * (layer + 1))
                nc.scalar.activation(proj[:, :, C_GU:], proj[:, :, C_GU:], ACT.Gelu_apprx_tanh).then_inc(gelu_ready, 1)
                for b in (0, 2, 4):
                    act.wait_ge(qk_turned, 6 * layer + b + 1)
                    nc.scalar.activation(qk_sb[:, b * BANK:(b + 1) * BANK], ps[:, b, :], ACT.Copy).then_inc(qk_act, 1)
                nc.scalar.activation(proj[:, :, C_RG:C_RG + WIDTH], proj[:, :, C_RG:C_RG + WIDTH], ACT.Silu).then_inc(silu_ready, 1)
                for h in range(HEADS + 1):
                    if h < HEADS:
                        act.wait_ge(att_biased, HEADS * layer + h + 1)
                        a = (h % 2) * 3 * P
                        nc.scalar.activation(att_p[:, a:a + P], att_p[:, a:a + P], ACT.Exp, bias=att_nmax[:, 2 * (h % 2):2 * (h % 2) + 1], accum_out=att_sum[:, h:h + 1])
                        nc.scalar.activation(att_p[:, a + P:a + 3 * P], att_p[:, a + P:a + 3 * P], ACT.Exp, bias=att_nmax[:, 2 * (h % 2) + 1:2 * (h % 2) + 2],
                                             accum_out=att_sum[:, HEADS + h:HEADS + h + 1]).then_inc(att_exped, 1)
                    if h >= 1:
                        g = h - 1
                        act.wait_ge(p_turned, HEADS * layer + g + 1)
                        if g >= 2:
                            act.wait_ge(att_out, HEADS * layer + g - 1)
                        nc.scalar.activation(att_pt[:, (g % 2) * 3 * P:(g % 2 + 1) * 3 * P], ps[:, 2 + g % 2, 0:3 * P], ACT.Copy).then_inc(pt_ready, 1)
                turned_hi(3 * layer + 1)
                split_hi(OUT_AT[layer] + 3, OUT_AT[layer] + 3)

            def ffn_pass(n0, s0, passes, nt, job=None):
                def turned(c):
                    act.wait_ge(act_turned, passes * FF_CHUNKS + c + 1)
                    a = (c % 2) * TT * BANK
                    src = ps_all[:, 0:2 * BANK] if nt == 2 else ps[:, 6, :]
                    nc.scalar.activation(actt_hi[:, a:a + nt * BANK], src, ACT.Copy).then_inc(actt_hi_ready, 1)

                for i in range(len(FFN)):
                    split_hi(n0 + i, s0 + i, job=job)
                    if job is not None and i == 2:
                        y_high(job)
                    for c in range(FF_CHUNKS):
                        if LAST_GATE[c] == i - 2:
                            act.wait_ge(unit_used, n0 + (LAST_GATE[c] + 1))
                            if c:
                                act.wait_ge(act_ready, passes * FF_CHUNKS + c)
                            nc.scalar.activation(gate_s[:, 0:nt * BANK], ps_all[:, 0:nt * BANK], ACT.Silu).then_inc(silu_done, 1)
                        if TRANSPOSE_AFTER[c] == i - 3:
                            turned(c)
                            if c == FF_CHUNKS - 1 and job is not None:
                                gathered_high(job + 1)

            def y_high(job):
                act.wait_ge(unit_used, len(FFN) * job + MOE_AT)
                act.wait_ge(slots_t_ready, job + 1)
                nc.scalar.activation(y_hi[:, :], ps_all[:, 4 * BANK:6 * BANK], ACT.Copy, scale=slot_gate).then_inc(y_hi_ready, 1)

            def gathered_high(job):
                act.wait_ge(gathered, job + 1)
                nc.scalar.activation(h_hi[:, 0:KT * P].rearrange("p (b n) -> p b n", b=2), ps[:, 2:4, :], ACT.Copy).then_inc(h_hi_ready, 1)

            act.dma_start(x_res, x_d.rearrange("(t p) n -> p t n", p=P)).then_inc(x_landed, 16)
            act.dma_start(small[:, :], tables_d[:, 0:4 * P]).then_inc(tables_landed, 16)
            act.dma_start(masks[:, :], tables_d[:, 4 * P:]).then_inc(masks_landed, 16)
            act.dma_start(gmlp_bias[:, :], ins["gmlp_bias"]).then_inc(bias_landed, 16)
            act.dma_start(router_w[:, :], ins["router"]).then_inc(router_landed, 16)
            for layer in range(2):
                if layer:
                    act.wait_ge(rows_ready, 3)
                act.dma_start(gmlp_w[:, layer * GROUPS * CHUNK:(layer + 1) * GROUPS * CHUNK], ins["gmlp_w"][layer]).then_inc(gmlp_w_landed[layer], 16)
                if layer == 0:
                    norm_sums(0, x_landed, 16)
                    turned_hi(0)
                mixer(layer)
                if layer == 0:
                    norm_sums(1, x_written, 1)
                    turned_hi(2)
                    ffn_pass(DENSE_AT, DENSE_AT, 0, 2)
                    norm_sums(2, x_written, 2)
                    turned_hi(3)
            norm_sums(3, x_written, 3)
            act.wait_ge(router_landed, 16)
            nc.scalar.activation(router_hi[:, :], router_w[:, :], ACT.Copy).then_inc(router_hi_ready, 1)
            act.wait_ge(rows_ready, 4)
            turned_hi(5)
            nc.scalar.activation(rows_hi[:, :], rows_sb[:, :], ACT.Copy).then_inc(rows_hi_ready, 1)
            act.wait_ge(gap_ready, 1)
            nc.scalar.activation(gap_e, gap, ACT.Exp).then_inc(gap_exped, 1)
            act.wait_ge(gathered, 1)
            nc.scalar.activation(h_hi[:, 0:KT * P].rearrange("p (b n) -> p b n", b=2), ps[:, 2:4, :], ACT.Copy).then_inc(h_hi_ready, 1)
            act.wait_ge(jobs_ready, 1)
            n_jobs = act.value_load(jobs_i[0:1, 15:16], min_val=EXPERTS, max_val=MAX_JOBS - 1)
            act.wait_ge(y_zeroed, 1)
            with act.Fori(0, n_jobs) as j:
                ffn_pass(len(FFN) * j + MOE_AT, MOE_AT, j + 1, 1, job=j)
            y_high(n_jobs)
            norm_sums(4, x_added, n_jobs + 1)

        @block.vector
        def _(dve):
            v = nc.vector
            steps = [0]

            def then(instruction):
                steps[0] += 1
                instruction.then_inc(dve_step, 1)
                dve.wait_ge(dve_step, steps[0])

            def split_lo(n, s, cols=UNIT):
                dve.wait_ge(hi_ready, n + 1)
                v.tensor_tensor(slot(w_lo, s % SPLIT_SLOTS, cols), slot(raw, s % RAW_SLOTS, cols),
                                slot(w_hi, s % SPLIT_SLOTS, cols), ALU.subtract).then_inc(lo_ready, 1)

            def norm_rows(n):
                dve.wait_ge(sumsq_ready, n + 1)
                v.tensor_scalar(meansq, sumsq, 1.0 / D_MODEL, NORM_EPS, ALU.mult, ALU.add).then_inc(meansq_ready, 1)
                dve.wait_ge(rstd_ready, n + 1)
                dve.wait_ge(gain_landed, 16 * (n + 1))
                for t in range(TT):
                    last = v.scalar_tensor_tensor(rows[:, t, :], x_res[:, t, :], rstd[:, t:t + 1], gain[:, :], ALU.mult, ALU.mult)
                last.then_inc(rows_ready, 1)

            def turned_lo(r):
                for b in range(4):
                    dve.wait_ge(h_hi_ready, 4 * r + b + 1)
                    v.tensor_tensor(h_lo[:, b * BANK:(b + 1) * BANK], ps[:, b, :], h_hi[:, b * BANK:(b + 1) * BANK], ALU.subtract).then_inc(h_ready, 1)

            def mixer(layer):
                for i in range(2):
                    split_lo(IN_AT[layer] + i, IN_AT[layer] + i)
                for c in range(IN_CHUNKS):
                    for i in (2 * c + 2, 2 * c + 3):
                        if i < len(IN_UNITS):
                            split_lo(IN_AT[layer] + i, IN_AT[layer] + i, UNIT if i < len(IN_UNITS) - 1 else KT * P)
                    width = BANK if c < IN_CHUNKS - 1 else P
                    dve.wait_ge(unit_used, IN_AT[layer] + CHUNK_END[c])
                    v.tensor_copy(proj[:, 1, c * BANK:c * BANK + width], ps[:, 2 * (c % 2) + 1, 0:width]).then_inc(proj_dve, 1)
                for i in range(SPLIT_SLOTS):
                    split_lo(OUT_AT[layer] + i, OUT_AT[layer] + i)
                for b in (1, 3, 5):
                    dve.wait_ge(qk_turned, 6 * layer + b + 1)
                    v.tensor_copy(qk_sb[:, b * BANK:(b + 1) * BANK], ps[:, b, :]).then_inc(qk_dve, 1)
                dve.wait_ge(gmlp_w_landed[layer], 16)
                w = gmlp_w[:, layer * GROUPS * CHUNK:(layer + 1) * GROUPS * CHUNK].rearrange("p (g i) -> p g i", g=GROUPS)
                v.tensor_tensor(w, w, causal_t.unsqueeze(1).to_broadcast([P, GROUPS, CHUNK]), ALU.mult).then_inc(gmlp_masked, 1)
                dve.wait_ge(gelu_ready, layer + 1)
                for t in range(TT):
                    then(v.bn_stats(bn6[:, 6 * t:6 * t + 6], proj[:, t, C_GV:]))
                    then(v.bn_aggr(bn2[:, 2 * t:2 * t + 2], bn6[:, 6 * t:6 * t + 6]))
                var = bn2.rearrange("p (t s) -> p s t", t=TT)[:, 1, :]
                v.tensor_scalar(var, var, GN_EPS, None, ALU.add).then_inc(gate_var, 1)
                dve.wait_ge(gate_rstd, layer + 1)
                for t in range(TT):
                    last = v.tensor_scalar(proj[:, t, C_GV:], proj[:, t, C_GV:], bn2[:, 2 * t:2 * t + 1], gate_rs[:, t:t + 1], ALU.subtract, ALU.mult)
                last.then_inc(gv_ready, 1)
                if layer == 0:
                    dve.wait_ge(masks_landed, 16)
                for h in range(HEADS):
                    a = (h % 2) * 3 * P
                    dve.wait_ge(ret_scored, HEADS * layer + h + 1)
                    if h >= 2:
                        dve.wait_ge(ret_out, HEADS * layer + h - 1)
                    v.tensor_tensor(ret_w[:, a:a + 3 * P], ps[:, 0, 0:3 * P], decay[:, h, :], ALU.mult).then_inc(ret_decayed, 1)
                    dve.wait_ge(att_scored, HEADS * layer + h + 1)
                    if h >= 2:
                        dve.wait_ge(p_turned, HEADS * layer + h - 1)
                    then(v.scalar_tensor_tensor(att_p[:, a:a + 3 * P], ps[:, 1, 0:3 * P], HEAD ** -0.5, alibi[:, h, :], ALU.mult, ALU.add))
                    v.tensor_reduce(att_nmax[:, 2 * (h % 2):2 * (h % 2) + 1], att_p[:, a:a + P], AX.X, ALU.max, negate=True)
                    v.tensor_reduce(att_nmax[:, 2 * (h % 2) + 1:2 * (h % 2) + 2], att_p[:, a + P:a + 3 * P], AX.X, ALU.max, negate=True).then_inc(att_biased, 1)
                dve.wait_ge(ret_out, HEADS * (layer + 1))
                o = ps[:, 4:6, 0:WIDTH].rearrange("p t (h e) -> p t h e", h=HEADS)
                mixed = rows[:, :, 0:WIDTH].rearrange("p t (h e) -> p t h e", h=HEADS)
                square = proj[:, :, 0:WIDTH].rearrange("p t (h e) -> p t h e", h=HEADS)
                per_head = lambda s: s.rearrange("p (t h) -> p t h", t=TT)
                wide = lambda s: per_head(s).unsqueeze(3).to_broadcast([P, TT, HEADS, HEAD])
                then(v.tensor_reduce(per_head(ret_mean), o, AX.X, ALU.add))
                then(v.tensor_scalar(scaled, ret_mean, 1.0 / HEAD, None, ALU.mult))
                then(v.tensor_tensor(mixed, o, wide(scaled), ALU.subtract))
                then(v.tensor_tensor(square, mixed, mixed, ALU.mult))
                then(v.tensor_reduce(per_head(ret_mean), square, AX.X, ALU.add))
                v.tensor_scalar(ret_sq, ret_mean, 1.0 / HEAD, GN_EPS, ALU.mult, ALU.add).then_inc(ret_var, 1)
                dve.wait_ge(gmlp_out, layer + 1)
                dve.wait_ge(bias_landed, 16)
                for g in range(GROUPS):
                    v.scalar_tensor_tensor(rows[:, :, 2 * WIDTH + g * HEAD:2 * WIDTH + (g + 1) * HEAD],
                                           ps[:, 2, g * P:(g + 1) * P].rearrange("p (t e) -> p t e", t=TT),
                                           gmlp_bias[:, layer * GROUPS + g:layer * GROUPS + g + 1],
                                           proj[:, :, C_GU + g * HEAD:C_GU + (g + 1) * HEAD], ALU.add, ALU.mult)
                dve.wait_ge(att_exped, HEADS * (layer + 1))
                then(v.reciprocal(att_rinv, att_sum))
                dve.wait_ge(att_out, HEADS * (layer + 1))
                v.tensor_tensor(rows[:, :, WIDTH:2 * WIDTH].rearrange("p t (h e) -> p t h e", h=HEADS),
                                ps[:, 6:8, 0:WIDTH].rearrange("p t (h e) -> p t h e", h=HEADS), wide(att_rinv), ALU.mult)
                dve.wait_ge(ret_rstd, layer + 1)
                then(v.tensor_tensor(mixed, mixed, wide(ret_rs), ALU.mult))
                dve.wait_ge(silu_ready, layer + 1)
                v.tensor_tensor(rows[:, :, 0:WIDTH], rows[:, :, 0:WIDTH], proj[:, :, C_RG:C_RG + WIDTH], ALU.mult).then_inc(mix_ready, 1)
                turned_lo(3 * layer + 1)
                split_lo(OUT_AT[layer] + 3, OUT_AT[layer] + 3)
                for half in range(2):
                    dve.wait_ge(unit_used, OUT_AT[layer] + 2 * half + 2)
                    x_half = x_res[:, :, half * BANK:(half + 1) * BANK]
                    last = v.tensor_tensor(x_half, x_half, ps[:, 4 + 2 * half:6 + 2 * half, :], ALU.add)
                last.then_inc(x_written, 1)

            def ffn_pass(n0, s0, passes, nt, job=None):
                def turned(c):
                    dve.wait_ge(actt_hi_ready, passes * FF_CHUNKS + c + 1)
                    a = (c % 2) * TT * BANK
                    src = ps_all[:, 0:2 * BANK] if nt == 2 else ps[:, 6, :]
                    v.tensor_tensor(actt_lo[:, a:a + nt * BANK], src, actt_hi[:, a:a + nt * BANK], ALU.subtract).then_inc(actt_ready, 1)

                for i in range(len(FFN)):
                    split_lo(n0 + i, s0 + i)
                    if job is not None:
                        if i == 2:
                            y_low(job)
                        if i == 6:
                            add_scattered(job)
                        if i == 9:
                            turn_slots(job)
                        if i == 12:
                            make_slots(job + 1)
                    for c in range(FF_CHUNKS):
                        if LAST_UP[c] == i - 2:
                            dve.wait_ge(unit_used, n0 + (LAST_UP[c] + 1))
                            dve.wait_ge(silu_done, passes * FF_CHUNKS + c + 1)
                            if c:
                                dve.wait_ge(act_turned, passes * FF_CHUNKS + c)
                            v.tensor_tensor(act_s[:, 0:nt * BANK], gate_s[:, 0:nt * BANK], ps_all[:, nt * BANK:2 * nt * BANK], ALU.mult).then_inc(act_ready, 1)
                        if TRANSPOSE_AFTER[c] == i - 3:
                            turned(c)
                            if c == FF_CHUNKS - 1 and job is not None:
                                gathered_low(job + 1)

            def gathered_low(job):
                dve.wait_ge(h_hi_ready, 24 + job + 1)
                pair = lambda t: t[:, 0:KT * P].rearrange("p (b n) -> p b n", b=2)
                v.tensor_tensor(pair(h_lo), ps[:, 2:4, :], pair(h_hi), ALU.subtract).then_inc(h_ready, 1)

            def y_low(job):
                dve.wait_ge(y_hi_ready, job + 1)
                v.scalar_tensor_tensor(y_lo[:, :], ps_all[:, 4 * BANK:6 * BANK], slot_gate, y_hi[:, :], ALU.mult, ALU.subtract).then_inc(y_ready, 1)

            def add_scattered(job):
                dve.wait_ge(scattered, job + 1)
                x_two = lambda t: x_res[:, t, :].rearrange("p (h n) -> p h n", h=2)
                v.tensor_tensor(x_two(0), x_two(0), ps[:, 2:4, :], ALU.add)
                v.tensor_tensor(x_two(1), x_two(1), ps[:, 6:8, :], ALU.add).then_inc(x_added, 1)

            def turn_slots(job):
                dve.wait_ge(slots_turned, job + 1)
                v.tensor_copy(slots_t[:, :], ps[:, 2, 0:TT * P])
                v.tensor_copy(slot_gate, ps[:, 2, TT * P:TT * P + 1]).then_inc(slots_t_ready, 1)

            def make_slots(job):
                if not isinstance(job, int):
                    dve.wait_ge(slots_turned, job)
                column = bass.ds(job, 1)
                v.tensor_copy(cur_weight.rearrange("p (t a) -> p t a", t=TT), weight[:, :, column])
                v.tensor_copy(cur_place.rearrange("p (t a) -> p t a", t=TT), place[:, :, column]).then_inc(place_copied, 1)
                dve.wait_ge(place_copied, job + 1)
                for t in range(TT):
                    last = v.tensor_scalar(slots[:, t * P:(t + 1) * P], count_up, cur_place[:, t:t + 1], None, ALU.is_equal)
                last.then_inc(slots_ready, 1)

            dve.wait_ge(x_landed, 16)
            norm_rows(0)
            turned_lo(0)
            mixer(0)
            norm_rows(1)
            turned_lo(2)
            ffn_pass(DENSE_AT, DENSE_AT, 0, 2)
            for t in range(TT):
                dve.wait_ge(unit_used, DENSE_AT + len(FFN))
                last = v.tensor_tensor(x_res[:, t, :], x_res[:, t, :], ps_all[:, (4 + 2 * t) * BANK:(6 + 2 * t) * BANK], ALU.add)
            last.then_inc(x_written, 1)
            norm_rows(2)
            turned_lo(3)
            mixer(1)
            norm_rows(3)
            turned_lo(5)
            dve.wait_ge(router_hi_ready, 1)
            v.tensor_tensor(router_lo[:, :], router_w[:, :], router_hi[:, :], ALU.subtract).then_inc(router_ready, 1)
            v.memset(slots_t[:, :].bitcast(F32), 0.0)
            v.memset(slot_gate, 0.0).then_inc(slots_t_ready, 1)
            dve.wait_ge(logits_ready, 1)
            then(v.tensor_copy(logits, ps[:, 4, 0:TT * EXPERTS].rearrange("p (t e) -> p t e", t=TT)))
            for t in range(TT):
                last = v.max(top[:, t, :], logits[:, t, :])
            then(last)
            for t in range(TT):
                last = v.max_index(index_u[:, t * EXPERTS:(t + 1) * EXPERTS], top[:, t, :], logits[:, t, :])
            then(last)
            v.tensor_tensor(gap.unsqueeze(2), top[:, :, 1:2], top[:, :, 0:1], ALU.subtract).then_inc(gap_ready, 1)
            then(v.tensor_copy(top_at, index_u[:, :].rearrange("p (t e) -> p t e", t=TT)))
            then(v.tensor_scalar(top_at, top_at, 1.0, None, ALU.add))
            for t in range(TT):
                v.tensor_scalar(first[:, t, :], count_up[:, 0:EXPERTS], top_at[:, t, 0:1], None, ALU.is_equal)
                last = v.tensor_scalar(second[:, t, :], count_up[:, 0:EXPERTS], top_at[:, t, 1:2], None, ALU.is_equal)
            then(last)
            v.tensor_tensor(mask, first, second, ALU.add).then_inc(mask_ready, 1)
            dve.wait_ge(gap_exped, 1)
            then(v.tensor_scalar(g_den, gap_e, 1.0, None, ALU.add))
            then(v.reciprocal(g_one, g_den))
            then(v.tensor_tensor(g_two, gap_e, g_one, ALU.mult))
            for t in range(TT):
                last = v.tensor_scalar(second[:, t, :], second[:, t, :], g_two[:, t:t + 1], None, ALU.mult)
            then(last)
            for t in range(TT):
                last = v.scalar_tensor_tensor(gates[:, t, :], first[:, t, :], g_one[:, t:t + 1], second[:, t, :], ALU.mult, ALU.add)
            then(last)
            dve.wait_ge(counted, 1)
            then(v.tensor_copy(counts, ps[:, 5, 0:24]))
            v.tensor_copy(weight[:, :, 0:EXPERTS], gates)
            v.tensor_tensor(place[:, :, 0:EXPERTS], counts[:, 0:16].rearrange("p (t e) -> p t e", t=TT), mask, ALU.mult)
            then(v.tensor_scalar(over, counts[:, 16:24], float(P), None, ALU.is_gt))
            make_slots(0)
            then(v.tensor_copy(over_rank, over))
            for e in range(1, EXPERTS):
                then(v.tensor_tensor(over_rank[:, e:e + 1], over_rank[:, e - 1:e], over_rank[:, e:e + 1], ALU.add))
            then(v.tensor_scalar(jobs[:, 0:EXPERTS], count_up[:, 0:EXPERTS], -1.0, None, ALU.add))
            for r in range(MAX_JOBS - EXPERTS):
                then(v.scalar_tensor_tensor(pick, over_rank, float(r + 1), over, ALU.is_equal, ALU.mult))
                picked = pick.unsqueeze(1).to_broadcast([P, TT, EXPERTS])
                job = EXPERTS + r
                then(v.tensor_tensor(product, place[:, :, 0:EXPERTS], picked, ALU.mult))
                then(v.tensor_reduce(place[:, :, job:job + 1], product, AX.X, ALU.add))
                then(v.tensor_scalar(place[:, :, job:job + 1], place[:, :, job:job + 1], -float(P), None, ALU.add))
                then(v.tensor_tensor(product, gates, picked, ALU.mult))
                then(v.tensor_reduce(weight[:, :, job:job + 1], product, AX.X, ALU.add))
                then(v.tensor_tensor(product[:, 0, :], jobs[:, 0:EXPERTS], pick, ALU.mult))
                then(v.tensor_reduce(jobs[:, job:job + 1], product[:, 0, :], AX.X, ALU.add))
            v.memset(jobs[:, MAX_JOBS:15], 0.0)
            then(v.tensor_scalar(jobs[:, 15:16], over_rank[:, EXPERTS - 1:EXPERTS], float(EXPERTS), None, ALU.add))
            v.tensor_copy(jobs_i[:, :], jobs).then_inc(jobs_ready, 1)
            dve.wait_ge(jobs_ready, 1)
            dve.wait_ge(rows_hi_ready, 1)
            v.tensor_tensor(rows_lo[:, :], rows_sb[:, :], rows_hi[:, :], ALU.subtract).then_inc(rows_split, 1)
            gathered_low(0)
            n_jobs = dve.value_load(jobs_i[0:1, 15:16], min_val=EXPERTS, max_val=MAX_JOBS - 1)
            with dve.Fori(0, n_jobs) as j:
                ffn_pass(len(FFN) * j + MOE_AT, MOE_AT, j + 1, 1, job=j)
            y_low(n_jobs)
            add_scattered(n_jobs)
            norm_rows(4)

        @block.tensor
        def _(pe):
            mm = nc.tensor.matmul

            def product(dst, a_hi, a_lo, b_hi, b_lo, start, stop):
                mm(dst, a_hi, b_lo, start=start, stop=False)
                mm(dst, a_lo, b_hi, start=False, stop=False)
                return mm(dst, a_hi, b_hi, start=False, stop=stop)

            def unit_ready(n):
                pe.wait_ge(lo_ready, n + 1)

            def h_part(t, k, tile, nt=TT):
                a = (k * nt + tile) * P
                return t[:, a:a + P]

            def turn_rows(r, ready, value):
                pe.wait_ge(ready, value)
                for k in range(KT):
                    for t in range(TT):
                        a = (k % 2) * SEQ + t * P
                        last = nc.tensor.transpose(ps[:, k // 2, a:a + P], rows[:, t, k * P:(k + 1) * P], identity)
                    if k % 2:
                        last.then_inc(rows_turned, 1)

            def mixer(layer):
                pe.wait_ge(h_ready, 4 * (3 * layer + 1))
                for i, (c, h) in enumerate(IN_UNITS):
                    n = IN_AT[layer] + i
                    s = n % SPLIT_SLOTS
                    if h == 0 and c >= 2:
                        pe.wait_ge(proj_act, IN_CHUNKS * layer + c - 1)
                        pe.wait_ge(proj_dve, IN_CHUNKS * layer + c - 1)
                    unit_ready(n)
                    whole = c == IN_CHUNKS - 1
                    ks, width = (range(KT), P) if whole else (range(4 * h, 4 * h + 4), BANK)
                    for k in ks:
                        for t in range(TT):
                            w = (part(x, s, 0, k - ks[0], 0, width, width) for x in (w_hi, w_lo))
                            last = product(ps[:, 2 * (c % 2) + t, 0:width], h_part(h_hi, k, t), h_part(h_lo, k, t), *w, start=k == 0, stop=k == KT - 1)
                    last.then_inc(unit_used, 1)
                pe.wait_ge(proj_act, IN_CHUNKS * (layer + 1))
                pe.wait_ge(proj_dve, IN_CHUNKS * (layer + 1))
                columns = [c + m * P for c in (C_RQ, C_RK, C_MQ, C_MK) for m in range(3)]
                for m, c in enumerate(columns):
                    for t in range(TT):
                        a = (m % 2) * SEQ + t * P
                        last = nc.tensor.transpose(ps[:, m // 2, a:a + P], proj[:, t, c:c + P], identity)
                    if m % 2:
                        last.then_inc(qk_turned, 1)
                pe.wait_ge(qk_act, 3 * (layer + 1))
                pe.wait_ge(qk_dve, 3 * (layer + 1))

                def head_of(group, h):
                    return qk_t[(h % 2) * HEAD:(h % 2 + 1) * HEAD, 3 * group + h // 2, :]

                for h in range(HEADS + 2):
                    if h < HEADS:
                        if h:
                            pe.wait_ge(ret_decayed, HEADS * layer + h)
                        q, k = head_of(0, h), head_of(1, h)
                        mm(ps[:, 0, 0:SEQ], k[:, 0:P], q, start=True, stop=True)
                        mm(ps[:, 0, SEQ:SEQ + P], k[:, P:], q[:, P:], start=True, stop=True).then_inc(ret_scored, 1)
                        if h:
                            pe.wait_ge(att_biased, HEADS * layer + h)
                        q, k = head_of(2, h), head_of(3, h)
                        mm(ps[:, 1, 0:P], q[:, 0:P], k[:, 0:P], start=True, stop=True)
                        mm(ps[:, 1, P:3 * P], q[:, P:], k, start=True, stop=True).then_inc(att_scored, 1)
                    g = h - 1
                    if 0 <= g < HEADS:
                        a = (g % 2) * 3 * P
                        pe.wait_ge(ret_decayed, HEADS * layer + g + 1)
                        value = lambda t: proj[:, t, C_RV + g * HEAD:C_RV + (g + 1) * HEAD]
                        mm(ps[:, 4, g * HEAD:(g + 1) * HEAD], ret_w[:, a:a + P], value(0), start=True, stop=True)
                        mm(ps[:, 5, g * HEAD:(g + 1) * HEAD], ret_w[:, a + P:a + 2 * P], value(0), start=True, stop=False)
                        mm(ps[:, 5, g * HEAD:(g + 1) * HEAD], ret_w[:, a + 2 * P:a + 3 * P], value(1), start=False, stop=True).then_inc(ret_out, 1)
                        pe.wait_ge(att_exped, HEADS * layer + g + 1)
                        if g >= 2:
                            pe.wait_ge(pt_ready, HEADS * layer + g - 1)
                        for b in range(3):
                            last = nc.tensor.transpose(ps[:, 2 + g % 2, b * P:(b + 1) * P], att_p[:, a + b * P:a + (b + 1) * P], identity)
                        last.then_inc(p_turned, 1)
                    g = h - 2
                    if g >= 0:
                        a = (g % 2) * 3 * P
                        pe.wait_ge(pt_ready, HEADS * layer + g + 1)
                        value = lambda t: proj[:, t, C_MV + g * HEAD:C_MV + (g + 1) * HEAD]
                        mm(ps[:, 6, g * HEAD:(g + 1) * HEAD], att_pt[:, a:a + P], value(0), start=True, stop=True)
                        mm(ps[:, 7, g * HEAD:(g + 1) * HEAD], att_pt[:, a + P:a + 2 * P], value(0), start=True, stop=False)
                        mm(ps[:, 7, g * HEAD:(g + 1) * HEAD], att_pt[:, a + 2 * P:a + 3 * P], value(1), start=False, stop=True).then_inc(att_out, 1)
                pe.wait_ge(gmlp_masked, layer + 1)
                pe.wait_ge(gv_ready, layer + 1)
                pe.wait_ge(pt_ready, HEADS * (layer + 1))
                for g in range(GROUPS):
                    w = gmlp_w[:, (layer * GROUPS + g) * CHUNK:(layer * GROUPS + g + 1) * CHUNK]
                    last = mm(ps[:, 2, g * P:(g + 1) * P], w, proj[:, :, C_GV + g * HEAD:C_GV + (g + 1) * HEAD], start=True, stop=True)
                last.then_inc(gmlp_out, 1)
                turn_rows(3 * layer + 1, mix_ready, layer + 1)
                pe.wait_ge(h_ready, 4 * (3 * layer + 2))
                for i, (half, hh) in enumerate(OUT_UNITS):
                    n = OUT_AT[layer] + i
                    s = n % SPLIT_SLOTS
                    unit_ready(n)
                    for k in range(4 * hh, 4 * hh + 4):
                        for t in range(TT):
                            w = (part(x, s, 4, k - 4 * hh) for x in (w_hi, w_lo))
                            last = product(ps[:, 4 + 2 * half + t, :], h_part(h_hi, k, t), h_part(h_lo, k, t), *w, start=k == 0, stop=k == KT - 1)
                    last.then_inc(unit_used, 1)

            def ffn_pass(n0, s0, passes, nt, job=None):
                def turn(c):
                    pe.wait_ge(act_ready, passes * FF_CHUNKS + c + 1)
                    if nt == 2:
                        pe.wait_ge(silu_done, passes * FF_CHUNKS + min(c + 2, FF_CHUNKS))
                    if c:
                        pe.wait_ge(actt_ready, passes * FF_CHUNKS + c)
                    elif job is not None:
                        pe.wait_ge(x_added, job + 1)
                    for t in range(nt):
                        for f in range(4):
                            bank = t if nt == 2 else 6
                            last = nc.tensor.transpose(ps[:, bank, f * P:(f + 1) * P], act_s[:, t * BANK + f * P:t * BANK + (f + 1) * P], identity)
                    last.then_inc(act_turned, 1)

                for i, (kind, c, h) in enumerate(FFN):
                    n = n0 + i
                    s = (s0 + i) % SPLIT_SLOTS
                    if kind == "gate" and h == 0:
                        if nt == 2 and c >= 2:
                            pe.wait_ge(actt_ready, passes * FF_CHUNKS + c - 1)
                        elif c >= 1:
                            pe.wait_ge(silu_done, passes * FF_CHUNKS + c)
                    if kind == "up" and h == 0 and c >= 1:
                        pe.wait_ge(act_ready, passes * FF_CHUNKS + c)
                    if kind == "down" and h == 0:
                        pe.wait_ge(actt_ready, passes * FF_CHUNKS + c + 1)
                    unit_ready(n)
                    if kind == "down":
                        for f in range(2):
                            for t in range(nt):
                                a = (c % 2) * TT * BANK + t * BANK + (2 * h + f) * P
                                for half in range(2):
                                    w = (part(x, s, 2, f, half * BANK, BANK, D_MODEL) for x in (w_hi, w_lo))
                                    last = product(ps[:, 4 + 2 * t + half, :], actt_hi[:, a:a + P], actt_lo[:, a:a + P], *w,
                                                   start=c == 0 and h == 0 and f == 0, stop=c == FF_CHUNKS - 1 and h == 1 and f == 1)
                    else:
                        bank = 0 if kind == "gate" else nt
                        for k in range(4):
                            for t in range(nt):
                                w = (part(x, s, 4, k) for x in (w_hi, w_lo))
                                last = product(ps[:, bank + t, :], h_part(h_hi, 4 * h + k, t, nt), h_part(h_lo, 4 * h + k, t, nt), *w,
                                               start=h == 0 and k == 0, stop=h == 1 and k == 3)
                    last.then_inc(unit_used, 1)
                    if job is not None and i == 3:
                        scatter(job)
                    if job is not None and i == 7:
                        turn_slots(job)
                    if job is not None and i == TRANSPOSE_AFTER[FF_CHUNKS - 1]:
                        gather(job + 1)
                    for c2 in range(FF_CHUNKS):
                        if TRANSPOSE_AFTER[c2] == i:
                            turn(c2)

            def gather(job):
                pe.wait_ge(slots_ready, job + 1)
                if not isinstance(job, int):
                    pe.wait_ge(slots_t_ready, job + 1)
                for k in range(KT):
                    for step, (rows_part, t) in enumerate((r, t) for r in (rows_lo, rows_hi) for t in range(TT)):
                        a = t * D_MODEL + k * P
                        last = mm(ps[:, 2 + k // 4, (k % 4) * P:(k % 4 + 1) * P], rows_part[:, a:a + P], slots[:, t * P:(t + 1) * P],
                                  start=step == 0, stop=step == 3)
                last.then_inc(gathered, 1)

            def turn_slots(job):
                pe.wait_ge(x_added, job + 1)
                for t in range(TT):
                    nc.tensor.transpose(ps[:, 2, t * P:(t + 1) * P], slots[:, t * P:(t + 1) * P].bitcast(F32), identity)
                for t in range(TT):
                    last = mm(ps[:, 2, TT * P:TT * P + 1], slots[:, t * P:(t + 1) * P].bitcast(F32), cur_weight[:, t:t + 1], start=t == 0, stop=t == TT - 1)
                last.then_inc(slots_turned, 1)

            def scatter(job):
                pe.wait_ge(y_ready, job + 1)
                for t, half, bank in ((0, 0, 2), (0, 1, 3), (1, 0, 6), (1, 1, 7)):
                    at = slots_t[:, t * P:(t + 1) * P]
                    mm(ps[:, bank, :], at, y_lo[:, half * BANK:(half + 1) * BANK], start=True, stop=False)
                    last = mm(ps[:, bank, :], at, y_hi[:, half * BANK:(half + 1) * BANK], start=False, stop=True)
                last.then_inc(scattered, 1)

            pe.wait_ge(tables_landed, 16)
            turn_rows(0, rows_ready, 1)
            mixer(0)
            turn_rows(2, rows_ready, 2)
            pe.wait_ge(h_ready, 12)
            ffn_pass(DENSE_AT, DENSE_AT, 0, 2)
            turn_rows(3, rows_ready, 3)
            mixer(1)
            turn_rows(5, rows_ready, 4)
            pe.wait_ge(h_ready, 24)
            pe.wait_ge(router_ready, 1)
            for t in range(TT):
                pairs = [(a, b, k) for k in range(KT) for a in (h_lo, h_hi) for b in (router_lo, router_hi)]
                for step, (a, b, k) in enumerate(pairs):
                    last = mm(ps[:, 4, t * EXPERTS:(t + 1) * EXPERTS], h_part(a, k, t), b[:, k * EXPERTS:(k + 1) * EXPERTS],
                              start=step == 0, stop=step == len(pairs) - 1)
            last.then_inc(logits_ready, 1)
            pe.wait_ge(mask_ready, 1)
            mm(ps[:, 5, 0:8], causal_t, mask[:, 0, :], start=True, stop=True)
            mm(ps[:, 5, 8:16], causal_t, mask[:, 1, :], start=True, stop=False)
            mm(ps[:, 5, 8:16], ones, mask[:, 0, :], start=False, stop=True)
            mm(ps[:, 5, 16:24], ones, mask[:, 0, :], start=True, stop=False)
            mm(ps[:, 5, 16:24], ones, mask[:, 1, :], start=False, stop=True).then_inc(counted, 1)
            pe.wait_ge(rows_split, 1)
            gather(0)
            pe.wait_ge(jobs_ready, 1)
            for half in range(2):
                last = mm(ps[:, 4 + half, :], slots_t[:, 0:P], rows_hi[:, 0:BANK], start=True, stop=True)
            last.then_inc(y_zeroed, 1)
            n_jobs = pe.value_load(jobs_i[0:1, 15:16], min_val=EXPERTS, max_val=MAX_JOBS - 1)
            with pe.Fori(0, n_jobs) as j:
                pe.wait_ge(h_ready, 24 + 1 + j)
                ffn_pass(len(FFN) * j + MOE_AT, MOE_AT, j + 1, 1, job=j)
            scatter(n_jobs)


_INS = ["x", "l0_mix_norm", "l0_w_in", "l0_w_out", "l0_ffn_norm", "l0_w_gate", "l0_w_up", "l0_w_down",
        "l1_mix_norm", "l1_w_in", "l1_w_out", "l1_ffn_norm", "l1_we_gate", "l1_we_up", "l1_we_down", "final_norm"]


def kernel(**inputs):
    import concourse.bacc as bacc
    from concourse.bass_utils import run_bass_kernel_spmd

    nc = bacc.Bacc("TRN2", target_bir_lowering=False, num_devices=1)
    arrays = {n: np.ascontiguousarray(inputs[n]) for n in _INS}
    arrays["gmlp_w"] = np.ascontiguousarray(
        np.stack([np.asarray(inputs[f"l{n}_gmlp_w"]).transpose(2, 0, 1).reshape(CHUNK, -1) for n in range(2)]))
    arrays["gmlp_bias"] = np.ascontiguousarray(
        np.concatenate([np.asarray(inputs[f"l{n}_gmlp_b"]).T for n in range(2)], axis=1))
    arrays["router"] = np.ascontiguousarray(
        np.asarray(inputs["l1_router"]).reshape(KT, P, EXPERTS).transpose(1, 0, 2).reshape(P, -1))
    arrays["tables"] = shape_tables()
    ins = {n: nc.dram_tensor(f"in_{n}", a.shape, mybir.dt.from_np(a.dtype), kind="ExternalInput").ap() for n, a in arrays.items()}
    out = nc.dram_tensor("out", (1, SEQ, D_MODEL), F32, kind="ExternalOutput").ap()
    hybrid_trunk(nc, ins, out)
    got = run_bass_kernel_spmd(nc, [{f"in_{n}": a for n, a in arrays.items()}], core_ids=[0])
    return got.results[0]["out"]
```

```python
import numpy as np
import concourse.bass as bass
from concourse import mybir
from contextlib import ExitStack

F32 = mybir.dt.float32
F32R = mybir.dt.float32r
BF16 = mybir.dt.bfloat16
I32 = mybir.dt.int32
U32 = mybir.dt.uint32
ALU = mybir.AluOpType
ACT = mybir.ActivationFunctionType
AX = mybir.AxisListType

P = 128
BANK = 512
D_MODEL, SEQ, D_FF = 1024, 256, 3584
HEADS, HEAD = 6, 64
GROUPS, CHUNK = 4, 128
WIDTH = HEADS * HEAD
G_WIDTH = GROUPS * HEAD
IN_WIDTH = 7 * WIDTH + 2 * G_WIDTH
EXPERTS, MAX_JOBS = 8, 12
SECOND = MAX_JOBS - EXPERTS
TT = SEQ // P
KT = D_MODEL // P
NORM_EPS, GN_EPS = 1e-6, 1e-5

C_RQ, C_RK, C_RV, C_RG = (i * WIDTH for i in range(4))
C_MQ, C_MK, C_MV = (i * WIDTH for i in range(4, 7))
C_GU = 7 * WIDTH
C_GV = C_GU + G_WIDTH

UNIT = 2048
RAW_SLOTS, SPLIT_SLOTS = 6, 3
IN_CHUNKS = -(-IN_WIDTH // BANK)
IN_ORDER = (5, 6, 3, 4, 0, 1, 2)
IN_UNITS = [(c, h) for c in IN_ORDER for h in range(2 if c < IN_CHUNKS - 1 else 1)]
CHUNK_LAST = {IN_UNITS.index((c, 1 if c < IN_CHUNKS - 1 else 0)): q for q, c in enumerate(IN_ORDER)}
GELU_AT, GATE_NORM_AT, GMLP_AT = 3, 4, 6
ATT_TURN_AT, ATT_AT, RET_TURN_AT = 7, 8, 11
PAIRS = HEADS // 2
AHEAD = 2
RET_BUFFERS = 4
OUT_UNITS = [(6, 7), (4, 5), (0, 3), (1, 2)]
FF_CHUNKS = D_FF // BANK


def has_last(job):
    return job is not None and not isinstance(job, int)


def turned_bank(c, nt):
    if nt == 1:
        return 6
    return 0 if c else 4


def ffn_units():
    units = []
    for c in range(FF_CHUNKS):
        units += [("gate", c, 0), ("gate", c, 1), ("up", c, 0), ("up", c, 1)]
        if c >= 2:
            units += [("down", c - 2, 0), ("down", c - 2, 1)]
    return units + [("down", c, h) for c in (FF_CHUNKS - 2, FF_CHUNKS - 1) for h in range(2)]


FFN = ffn_units()
LAST_UP = {c: FFN.index(("up", c, 1)) for c in range(FF_CHUNKS)}
LAST_GATE = {c: FFN.index(("gate", c, 1)) for c in range(FF_CHUNKS)}
TRANSPOSE_AFTER = {c: LAST_UP[c + 1] for c in range(FF_CHUNKS - 1)} | {FF_CHUNKS - 1: FFN.index(("down", FF_CHUNKS - 3, 1))}
LAYER_UNITS = len(IN_UNITS) + len(OUT_UNITS)
DENSE_AT = LAYER_UNITS
IN_AT = [0, DENSE_AT + len(FFN)]
OUT_AT = [a + len(IN_UNITS) for a in IN_AT]
MOE_AT = OUT_AT[1] + len(OUT_UNITS)
NORM_TURNED, OUT_TURNED, JOBS_TURNED = (0, 9, 13, 22), (4, 17), 26
assert len(FFN) % RAW_SLOTS == 0 and len(FFN) % SPLIT_SLOTS == 0


def shape_tables():
    i = np.arange(P)
    f = np.float32
    causal_t = (i[:, None] <= i[None, :]).astype(f)
    log_g = np.log(f(1.0) - f(2.0) ** (f(-5.0) - np.arange(HEADS, dtype=f))).astype(f)
    d = np.arange(SEQ)[None, :] - i[:, None]
    wide = np.where(d >= 0, np.exp(log_g[:, None, None] * np.maximum(d, 0)), 0.0)
    decay = np.concatenate([wide, wide[:, :, :P]], axis=2) * HEAD ** -0.5
    slopes = f(2.0) ** (f(-8.0) * np.arange(1, HEADS + 1, dtype=f) / f(HEADS))
    dist = (i[:, None] + P - np.arange(SEQ)[None, :])
    own = np.where(dist >= 0, -slopes[:, None, None] * dist, -1e30)
    alibi = np.concatenate([own[:, :, P:], own], axis=2)
    flat = lambda t: t.transpose(1, 0, 2).reshape(P, -1)
    iota = np.tile(np.arange(1, P + 1), (P, 1))
    return np.concatenate([np.eye(P), causal_t, np.ones((P, P)), iota, flat(decay), flat(alibi)], axis=1).astype(f)


def hybrid_trunk(nc, ins, out):
    x_d, tables_d = ins["x"][0], ins["tables"]
    norm_d = [ins[n] for n in ("l0_mix_norm", "l0_ffn_norm", "l1_mix_norm", "l1_ffn_norm", "final_norm")]
    w_in_d = [ins["l0_w_in"], ins["l1_w_in"]]
    w_out_d = [ins["l0_w_out"], ins["l1_w_out"]]

    ctx = ExitStack()
    with ctx:
        def sem(name):
            return ctx.enter_context(nc.semaphore(name))

        def sb(name, cols, dt=F32, stack=ctx):
            return stack.enter_context(nc.sbuf_tensor(name, [P, cols], dt))

        small = sb("small", 4 * P)
        identity, causal_t, ones, count_up = (small[:, k * P:(k + 1) * P] for k in range(4))
        masks = sb("masks", 2 * HEADS * 3 * P)
        decay = masks[:, 0:HEADS * 3 * P].rearrange("p (h n) -> p h n", h=HEADS)
        alibi = masks[:, HEADS * 3 * P:].rearrange("p (h n) -> p h n", h=HEADS)
        x_sb = sb("x_sb", TT * D_MODEL)
        x_res = x_sb[:, :].rearrange("p (t n) -> p t n", t=TT)
        rows_sb = sb("rows_sb", TT * D_MODEL)
        rows = rows_sb[:, :].rearrange("p (t n) -> p t n", t=TT)
        gain = sb("gain", D_MODEL)
        h_hi = sb("h_hi", KT * SEQ, F32R)
        h_lo = sb("h_lo", KT * SEQ, F32R)
        raw = sb("raw", RAW_SLOTS * UNIT)
        w_hi = sb("w_hi", SPLIT_SLOTS * UNIT, F32R)
        w_lo = sb("w_lo", SPLIT_SLOTS * UNIT, F32R)
        stat = sb("stat", 128)
        gmlp_bias = sb("gmlp_bias", 2 * GROUPS)
        tables_b = sb("tables_b", 3 * P, BF16)
        identity_b, causal_b, ones_b = (tables_b[:, k * P:(k + 1) * P] for k in range(3))
        exponent = sb("exponent", 2 * HEADS)
        router_w = sb("router_w", KT * EXPERTS)
        router_s = sb("router_s", KT * 2 * EXPERTS, F32R)
        router_parts = router_s[:, :].rearrange("p (k s e) -> p k s e", k=KT, s=2)
        jobs_i = sb("jobs_i", 16, I32)

        with ExitStack() as mixer:
            proj_sb = sb("proj_sb", TT * IN_WIDTH, stack=mixer)
            qk_sb = sb("qk_sb", 12 * SEQ, stack=mixer)
            ret_w = sb("ret_w", RET_BUFFERS * 3 * P, stack=mixer)
            att_p = sb("att_p", 2 * 3 * P, stack=mixer)
            att_pt = sb("att_pt", 2 * 3 * P, stack=mixer)
            gmlp_w = sb("gmlp_w", 2 * GROUPS * CHUNK, stack=mixer)
        proj = proj_sb[:, :].rearrange("p (t n) -> p t n", t=TT)
        qk_t = qk_sb[:, :].rearrange("p (m s n) -> p m s n", m=2 * PAIRS, s=2)

        ffn = ctx.enter_context(ExitStack())
        gate_s = sb("gate_s", TT * BANK, stack=ffn)
        act_s = sb("act_s", TT * BANK, stack=ffn)
        actt_hi = sb("actt_hi", 2 * TT * BANK, F32R, stack=ffn)
        actt_lo = sb("actt_lo", 2 * TT * BANK, F32R, stack=ffn)
        rows_b = [sb(f"rows_b{n}", TT * D_MODEL, BF16, stack=ffn) for n in range(3)]
        y_hi = sb("y_hi", D_MODEL, F32R, stack=ffn)
        y_lo = sb("y_lo", D_MODEL, F32R, stack=ffn)
        slots = sb("slots", TT * P, BF16, stack=ffn)
        slots_t = sb("slots_t", TT * P, F32R, stack=ffn)
        route = sb("route", 512, stack=ffn)
        weight_b = sb("weight_b", TT * MAX_JOBS * 3, BF16, stack=ffn)
        cur_weight = sb("cur_weight", TT * 3, BF16, stack=ffn)
        index_u = sb("index_u", TT * EXPERTS, U32, stack=ffn)
        mask_b = sb("mask_b", TT * EXPERTS, BF16, stack=ffn)
        logits_t = sb("logits_t", TT * P, stack=ffn)
        rows_rest = (gate_s, act_s)

        ps_all = ctx.enter_context(nc.psum_tensor("ps_all", [P, 8 * BANK], F32))
        ps = ps_all[:, :].rearrange("p (b n) -> p b n", b=8)

        unit_landed = [sem(f"unit_landed{s}") for s in range(RAW_SLOTS)]
        hi_ready, lo_ready, unit_used = sem("hi_ready"), sem("lo_ready"), sem("unit_used")
        tables_landed, masks_landed, bias_landed = (sem(n) for n in ("tables_landed", "masks_landed", "bias_landed"))
        x_landed = [sem("x_landed0"), sem("x_landed1")]
        router_landed, out_landed = sem("router_landed"), sem("out_landed")
        gmlp_w_landed = [sem("gmlp_w_landed0"), sem("gmlp_w_landed1")]
        gain_landed, exponent_set = sem("gain_landed"), sem("exponent_set")
        x_written, sumsq_ready, meansq_ready, rstd_ready, rows_ready = (sem(n) for n in ("x_written", "sumsq_ready", "meansq_ready", "rstd_ready", "rows_ready"))
        mix_ready, rows_turned, h_hi_ready, h_ready = (sem(n) for n in ("mix_ready", "rows_turned", "h_hi_ready", "h_ready"))
        proj_act, proj_dve = sem("proj_act"), sem("proj_dve")
        qk_turned, qk_act, qk_dve = sem("qk_turned"), sem("qk_act"), sem("qk_dve")
        ret_scored, ret_decayed, ret_out = sem("ret_scored"), sem("ret_decayed"), sem("ret_out")
        att_scored, att_biased, att_exped, p_turned, pt_ready, att_out, att_stored = (sem(n) for n in ("att_scored", "att_biased", "att_exped", "p_turned", "pt_ready", "att_out", "att_stored"))
        gelu_ready, silu_ready, gate_var, gate_rstd, gv_ready, gmlp_masked, gmlp_out, gmlp_stored, ret_var, ret_rstd = (
            sem(n) for n in ("gelu_ready", "silu_ready", "gate_var", "gate_rstd", "gv_ready", "gmlp_masked", "gmlp_out", "gmlp_stored", "ret_var", "ret_rstd"))
        silu_done, act_ready, act_turned, actt_hi_ready, actt_ready = (
            sem(n) for n in ("silu_done", "act_ready", "act_turned", "actt_hi_ready", "actt_ready"))
        router_hi_ready, router_ready, rows_b_ready, rows_rest_ready, rows_b_done, logits_summed, logits_copied, logits_ready, gap_ready, gap_exped, mask_ready, counted, jobs_ready = (
            sem(n) for n in ("router_hi_ready", "router_ready", "rows_b_ready", "rows_rest_ready", "rows_b_done", "logits_summed", "logits_copied", "logits_ready", "gap_ready", "gap_exped", "mask_ready", "counted", "jobs_ready"))
        slots_ready, gathered, slots_turned, slots_t_ready, y_hi_ready, y_ready, scattered, x_added = (
            sem(n) for n in ("slots_ready", "gathered", "slots_turned", "slots_t_ready", "y_hi_ready", "y_ready", "scattered", "x_added"))
        dve_step, place_copied, tile_done, weight_copied, tables_b_ready = sem("dve_step"), sem("place_copied"), sem("tile_done"), sem("weight_copied"), sem("tables_b_ready")

        sumsq, meansq, rstd = stat[:, 0:2], stat[:, 2:4], stat[:, 4:6]
        ret_mean, ret_sq, ret_rs = stat[:, 8:20], stat[:, 20:32], stat[:, 32:44]
        att_nmax, att_sum, att_rinv = stat[:, 44:46 + 2], stat[:, 48:60], stat[:, 60:72]
        bn6, bn2, gate_rs = stat[:, 72:84], stat[:, 84:88], stat[:, 88:90]
        scaled = stat[:, 90:102]

        logits = route[:, 0:16].rearrange("p (t e) -> p t e", t=TT)
        top = route[:, 16:32].rearrange("p (t e) -> p t e", t=TT)
        top_at = route[:, 32:48].rearrange("p (t e) -> p t e", t=TT)
        first, second, gates = (route[:, 48 + 16 * k:64 + 16 * k].rearrange("p (t e) -> p t e", t=TT) for k in range(3))
        mask = mask_b[:, :].rearrange("p (t e) -> p t e", t=TT)
        gap, gap_e, g_den, g_one, g_two = (route[:, 112 + 2 * k:114 + 2 * k] for k in range(5))
        counts = route[:, 124:148]
        over, over_rank = route[:, 148:156], route[:, 156:164]
        pick = route[:, 300:300 + SECOND * EXPERTS].rearrange("p (r e) -> p r e", r=SECOND)
        product = route[:, 340:340 + TT * SECOND * EXPERTS].rearrange("p (t r e) -> p t r e", t=TT, r=SECOND)
        weight_rest = route[:, 410:410 + TT * MAX_JOBS].rearrange("p (t j) -> p t j", t=TT)
        logit_parts = route[:, 440:440 + TT * 2 * EXPERTS].rearrange("p (t s e) -> p t s e", t=TT, s=2)
        place = route[:, 188:188 + TT * MAX_JOBS].rearrange("p (t j) -> p t j", t=TT)
        weight = route[:, 212:212 + TT * MAX_JOBS].rearrange("p (t j) -> p t j", t=TT)
        jobs = route[:, 236:252]
        cur_place, slot_gate = route[:, 252:254], route[:, 256:257]
        weight_3 = weight_b[:, :].rearrange("p (t j s) -> p t j s", t=TT, s=3)

        def slot(t, s, n):
            return t[:, s * UNIT:s * UNIT + n]

        def part(t, s, parts, k, lo=0, n=BANK, width=BANK):
            a = s * UNIT + k * width + lo
            return t[:, a:a + n]

        def turned_block(b, parts):
            bank, tiles, k0, k1 = ((7, slice(0, 2), 6, 8), (6, slice(0, 1), 3, 6), (7, slice(1, 2), 3, 6),
                                   (2, slice(0, 1), 0, 3), (3, slice(1, 2), 0, 3))[b]
            n = (k1 - k0) * (tiles.stop - tiles.start) * P
            src = ps[:, bank, 0:n].rearrange("p (t n) -> p t n", t=tiles.stop - tiles.start)
            return src, [h[:, :].rearrange("p (t n) -> p t n", t=TT)[:, tiles, k0 * P:k1 * P] for h in parts]

        def pair_heads(k):
            return (2 * k, 2 * k + 1)

        block = ctx.enter_context(nc.Block())

        @block.sync
        def _(sp):
            def load(n, s, dst_cols, parts, src):
                if not isinstance(n, int) or n >= RAW_SLOTS:
                    sp.wait_ge(lo_ready, n - RAW_SLOTS + 1)
                dst = slot(raw, s % RAW_SLOTS, dst_cols).rearrange("p (k n) -> p k n", k=parts)
                sp.dma_start(dst, src).then_inc(unit_landed[s % RAW_SLOTS], 16)

            def rows_of(w, r0, nr, c0, ncol):
                return w[r0:r0 + nr * P, c0:c0 + ncol].rearrange("(k p) n -> p k n", p=P)

            def load_mixer_in(layer):
                for i, (c, h) in enumerate(IN_UNITS):
                    n = IN_AT[layer] + i
                    if layer == 0 and i == 4:
                        sp.dma_start(gmlp_w[:, 0:GROUPS * CHUNK], ins["gmlp_w"][0]).then_inc(gmlp_w_landed[0], 16)
                        sp.dma_start(gmlp_bias[:, :], ins["gmlp_bias"]).then_inc(bias_landed, 16)
                    if layer == 0 and i == 6:
                        sp.dma_start(masks[:, :], tables_d[:, 4 * P:]).then_inc(masks_landed, 16)
                        sp.dma_start(router_w[:, :], ins["router"]).then_inc(router_landed, 16)
                    if c < IN_CHUNKS - 1:
                        load(n, n, UNIT, 4, rows_of(w_in_d[layer], h * 4 * P, 4, c * BANK, BANK))
                    else:
                        load(n, n, KT * P, KT, rows_of(w_in_d[layer], 0, KT, c * BANK, P))

            def load_mixer_out(layer):
                for i, (k0, k1) in enumerate(OUT_UNITS):
                    n = OUT_AT[layer] + i
                    w = w_out_d[layer].rearrange("(k p) n -> p k n", p=P)
                    load(n, n, UNIT, 2, w[:, k0:k1 + 1:k1 - k0, :])

            def load_ffn(n0, s0, gate, up, down):
                for i, (kind, c, h) in enumerate(FFN):
                    if kind == "down":
                        src = rows_of(down, (4 * c + 2 * h) * P, 2, 0, D_MODEL)
                        load(n0 + i, s0 + i, UNIT, 2, src)
                    else:
                        src = rows_of(gate if kind == "gate" else up, h * 4 * P, 4, c * BANK, BANK)
                        load(n0 + i, s0 + i, UNIT, 4, src)

            for t in range(TT):
                sp.dma_start(x_res[:, t, :], x_d[t * P:(t + 1) * P, :]).then_inc(x_landed[t], 16)
            load_mixer_in(0)
            load_mixer_out(0)
            load_ffn(DENSE_AT, DENSE_AT, ins["l0_w_gate"], ins["l0_w_up"], ins["l0_w_down"])
            load_mixer_in(1)
            load_mixer_out(1)
            load_ffn(MOE_AT, MOE_AT, ins["l1_we_gate"][0], ins["l1_we_up"][0], ins["l1_we_down"][0])
            sp.wait_ge(jobs_ready, 1)
            n_jobs = sp.value_load(jobs_i[0:1, 15:16], min_val=EXPERTS, max_val=MAX_JOBS - 1)
            with sp.Fori(1, n_jobs) as j:
                e = sp.value_load(jobs_i[0:1, bass.ds(j, 1)], min_val=0, max_val=EXPERTS - 1)
                pick_expert = lambda w: w[bass.ds(e, 1), :, :].rearrange("a r c -> (a r) c")
                load_ffn(MOE_AT + len(FFN) * j, MOE_AT, *(pick_expert(ins[w]) for w in ("l1_we_gate", "l1_we_up", "l1_we_down")))
            for t in range(TT):
                sp.wait_ge(rows_ready, TT * 4 + t + 1)
                sp.dma_start(out[0, t * P:(t + 1) * P, :], rows[:, t, :]).then_inc(out_landed, 16)
            sp.wait_ge(out_landed, 16 * TT)

        @block.gpsimd
        def _(pool):
            def load_gain(n):
                pool.dma_start(gain[:, :], norm_d[n].rearrange("(a n) -> a n", a=1).to_broadcast([P, D_MODEL])).then_inc(gain_landed, 16)

            def inverse_root(dst, src, w, ready, value, done):
                pool.wait_ge(ready, value)
                nc.gpsimd.tensor_tensor(dst, src, exponent[:, 0:w], ALU.pow).then_inc(done, 1)

            load_gain(0)
            nc.gpsimd.memset(exponent[:, :], -0.5).then_inc(exponent_set, 1)
            pool.wait_ge(exponent_set, 1)
            for n in range(5):
                for t in range(TT):
                    inverse_root(rstd[:, t:t + 1], meansq[:, t:t + 1], 1, meansq_ready, TT * n + t + 1, rstd_ready)
                if n < 4:
                    pool.wait_ge(rows_ready, TT * (n + 1))
                    load_gain(n + 1)
                if n in (0, 2):
                    layer = n // 2
                    inverse_root(gate_rs, bn2.rearrange("p (t s) -> p s t", t=TT)[:, 1, :], 2, gate_var, layer + 1, gate_rstd)
                    for t in range(TT):
                        inverse_root(ret_rs[:, t * HEADS:(t + 1) * HEADS], ret_sq[:, t * HEADS:(t + 1) * HEADS], HEADS, ret_var, TT * layer + t + 1, ret_rstd)
                if n == 3:
                    for t in range(TT):
                        b0, b1, b2 = (b[:, t * D_MODEL:(t + 1) * D_MODEL] for b in rows_b)
                        pool.wait_ge(rows_b_ready, t + 1)
                        nc.gpsimd.tensor_tensor(rows_rest[t][:, :], rows[:, t, :], b0, ALU.subtract).then_inc(rows_rest_ready, 1)
                    for t in range(TT):
                        b0, b1, b2 = (b[:, t * D_MODEL:(t + 1) * D_MODEL] for b in rows_b)
                        pool.wait_ge(rows_b_ready, TT + t + 1)
                        nc.gpsimd.tensor_tensor(b2, rows_rest[t][:, :], b1, ALU.subtract).then_inc(rows_b_done, 1)

        @block.scalar
        def _(act):
            def split_hi(n, s, cols=UNIT, job=None):
                landed = 16 * (s // RAW_SLOTS + 1)
                act.wait_ge(unit_landed[s % RAW_SLOTS], landed if job is None else job * (16 * (len(FFN) // RAW_SLOTS)) + landed)
                if job is not None or n >= SPLIT_SLOTS:
                    act.wait_ge(unit_used, n - SPLIT_SLOTS + 1)
                nc.scalar.activation(slot(w_hi, s % SPLIT_SLOTS, cols), slot(raw, s % RAW_SLOTS, cols), ACT.Copy).then_inc(hi_ready, 1)

            def norm_sums(t, ready, value):
                act.wait_ge(ready, value)
                nc.scalar.activation(rows[:, t, :], x_res[:, t, :], ACT.Square, accum_out=sumsq[:, t:t + 1]).then_inc(sumsq_ready, 1)

            def turned_hi(r, banks=range(4)):
                for b in banks:
                    act.wait_ge(rows_turned, NORM_TURNED[r] + b + 1)
                    nc.scalar.activation(h_hi[:, b * BANK:(b + 1) * BANK], ps[:, b, :], ACT.Copy).then_inc(h_hi_ready, 1)

            def norm_between(r, n, value):
                split_hi(n, n)
                norm_sums(0, x_written, value)
                split_hi(n + 1, n + 1)
                turned_hi(r, (0,))
                norm_sums(1, x_written, value + 1)
                turned_hi(r, (1, 2, 3))

            def mixer(layer):
                first = IN_AT[layer]

                def beside(n):
                    if n in CHUNK_LAST:
                        q = CHUNK_LAST[n]
                        c = IN_ORDER[q]
                        width = BANK if c < IN_CHUNKS - 1 else P
                        act.wait_ge(unit_used, first + n + 1)
                        nc.scalar.activation(proj[:, 0, c * BANK:c * BANK + width], ps[:, 2 * (q % 2), 0:width], ACT.Copy).then_inc(proj_act, 1)
                    if n == GELU_AT:
                        act.wait_ge(proj_act, IN_CHUNKS * layer + 2)
                        act.wait_ge(proj_dve, IN_CHUNKS * layer + 2)
                        nc.scalar.activation(proj[:, :, C_GU:], proj[:, :, C_GU:], ACT.Gelu_apprx_tanh).then_inc(gelu_ready, 1)
                    if n == ATT_TURN_AT:
                        copy_turned(2, 6, 3)
                    if n - ATT_AT - 1 in range(PAIRS):
                        for h in pair_heads(n - ATT_AT - 1):
                            act.wait_ge(p_turned, HEADS * layer + h + 1)
                            if h >= 2:
                                act.wait_ge(att_out, HEADS * layer + h - 1)
                            nc.scalar.activation(att_pt[:, (h % 2) * 3 * P:(h % 2 + 1) * 3 * P], ps[:, 6 + h % 2, 0:3 * P], ACT.Copy).then_inc(pt_ready, 1)
                    if n - ATT_AT in range(PAIRS):
                        for h in pair_heads(n - ATT_AT):
                            act.wait_ge(att_biased, HEADS * layer + h + 1)
                            a = (h % 2) * 3 * P
                            low = att_nmax[:, 2 * (h % 2):2 * (h % 2) + 2]
                            nc.scalar.activation(att_p[:, a:a + P], att_p[:, a:a + P], ACT.Exp, bias=low[:, 0:1], accum_out=att_sum[:, h:h + 1])
                            nc.scalar.activation(att_p[:, a + P:a + 3 * P], att_p[:, a + P:a + 3 * P], ACT.Exp, bias=low[:, 1:2],
                                                 accum_out=att_sum[:, HEADS + h:HEADS + h + 1]).then_inc(att_exped, 1)
                    if n == RET_TURN_AT:
                        copy_turned(4, 3, 5)
                    if n == RET_TURN_AT + 1:
                        copy_turned(5, 6, 6)

                def copy_turned(pair, bank, turned):
                    act.wait_ge(qk_turned, 6 * layer + turned)
                    nc.scalar.activation(qk_sb[:, pair * BANK:(pair + 1) * BANK], ps[:, bank, :], ACT.Copy).then_inc(qk_act, 1)

                for i in range(len(IN_UNITS) + 2):
                    if i >= AHEAD:
                        split_hi(first + i, first + i, KT * P if IN_UNITS[i:i + 1] == [(IN_CHUNKS - 1, 0)] else UNIT)
                    if i >= 2:
                        beside(i - 2)
                for b in range(5):
                    if b == 2:
                        split_hi(OUT_AT[layer] + 2, OUT_AT[layer] + 2)
                    if b == 3:
                        act.wait_ge(proj_dve, IN_CHUNKS * (layer + 1))
                        act.wait_ge(proj_act, IN_CHUNKS * (layer + 1))
                        nc.scalar.activation(proj[:, :, C_RG:C_RG + WIDTH], proj[:, :, C_RG:C_RG + WIDTH], ACT.Silu).then_inc(silu_ready, 1)
                        split_hi(OUT_AT[layer] + 3, OUT_AT[layer] + 3)
                    src, (at,) = turned_block(b, (h_hi,))
                    act.wait_ge(rows_turned, OUT_TURNED[layer] + b + 1)
                    nc.scalar.activation(at, src, ACT.Copy).then_inc(h_hi_ready, 1)

            def ffn_pass(n0, s0, passes, nt, job=None, ahead=0):
                def turned(c):
                    act.wait_ge(act_turned, passes * FF_CHUNKS + c + 1)
                    a = (c % 2) * TT * BANK
                    bank = turned_bank(c, nt)
                    src = ps_all[:, bank * BANK:(bank + nt) * BANK]
                    nc.scalar.activation(actt_hi[:, a:a + nt * BANK], src, ACT.Copy).then_inc(actt_hi_ready, 1)

                for i in range(len(FFN)):
                    if i >= ahead:
                        split_hi(n0 + i, s0 + i, job=job)
                    if has_last(job) and i == 2:
                        y_high(job)
                    for c in range(FF_CHUNKS):
                        if LAST_GATE[c] == i - 2:
                            act.wait_ge(unit_used, n0 + (LAST_GATE[c] + 1))
                            if c:
                                act.wait_ge(act_ready, passes * FF_CHUNKS + c)
                            nc.scalar.activation(gate_s[:, 0:nt * BANK], ps_all[:, 0:nt * BANK], ACT.Silu).then_inc(silu_done, 1)
                        if TRANSPOSE_AFTER[c] == i - 3:
                            turned(c)
                            if c == FF_CHUNKS - 1 and job is not None:
                                gathered_high(job + 1)

            def y_high(job):
                act.wait_ge(unit_used, len(FFN) * job + MOE_AT)
                act.wait_ge(slots_t_ready, job)
                nc.scalar.activation(y_hi[:, :], ps_all[:, 4 * BANK:6 * BANK], ACT.Copy, scale=slot_gate).then_inc(y_hi_ready, 1)

            def gathered_high(job):
                for b in range(2):
                    act.wait_ge(gathered, 2 * job + (b + 1))
                    nc.scalar.activation(h_hi[:, b * BANK:(b + 1) * BANK], ps[:, 2 + b, :], ACT.Copy).then_inc(h_hi_ready, 1)

            def rows_part(n, t):
                act.wait_ge(*((rows_ready, TT * 3 + t + 1) if n == 0 else (rows_rest_ready, t + 1)))
                src = rows[:, t, :] if n == 0 else rows_rest[t][:, :]
                nc.scalar.activation(rows_b[n][:, t * D_MODEL:(t + 1) * D_MODEL], src, ACT.Copy).then_inc(rows_b_ready, 1)

            act.dma_start(small[:, :], tables_d[:, 0:4 * P]).then_inc(tables_landed, 16)
            for t in range(TT):
                norm_sums(t, x_landed[t], 16)
            turned_hi(0, (0, 1))
            split_hi(0, 0)
            split_hi(1, 1)
            turned_hi(0, (2, 3))
            mixer(0)
            norm_between(1, DENSE_AT, 1)
            ffn_pass(DENSE_AT, DENSE_AT, 0, 2, ahead=AHEAD)
            norm_between(2, IN_AT[1], TT + 1)
            act.dma_start(gmlp_w[:, GROUPS * CHUNK:], ins["gmlp_w"][1]).then_inc(gmlp_w_landed[1], 16)
            act.wait_ge(router_landed, 16)
            nc.scalar.activation(router_parts[:, :, 0, :], router_w[:, :].rearrange("p (k e) -> p k e", k=KT), ACT.Copy).then_inc(router_hi_ready, 1)
            mixer(1)
            split_hi(MOE_AT, MOE_AT)
            norm_sums(0, x_written, 2 * TT + 1)
            split_hi(MOE_AT + 1, MOE_AT + 1)
            turned_hi(3, (0,))
            norm_sums(1, x_written, 2 * TT + 2)
            turned_hi(3, (1,))
            rows_part(0, 0)
            turned_hi(3, (2, 3))
            rows_part(0, 1)
            rows_part(1, 0)
            rows_part(1, 1)
            split_hi(MOE_AT + 2, MOE_AT + 2)
            act.wait_ge(gap_ready, 1)
            nc.scalar.activation(gap_e, gap, ACT.Exp).then_inc(gap_exped, 1)
            gathered_high(0)
            ffn_pass(MOE_AT, MOE_AT, 1, 1, job=0, ahead=SPLIT_SLOTS)
            act.wait_ge(jobs_ready, 1)
            n_jobs = act.value_load(jobs_i[0:1, 15:16], min_val=EXPERTS, max_val=MAX_JOBS - 1)
            with act.Fori(1, n_jobs) as j:
                ffn_pass(len(FFN) * j + MOE_AT, MOE_AT, j + 1, 1, job=j)
            y_high(n_jobs)
            for t in range(TT):
                norm_sums(t, x_written, TT * 3 + (t + 1))

        @block.vector
        def _(dve):
            v = nc.vector
            steps = [0]

            def then(instruction):
                steps[0] += 1
                instruction.then_inc(dve_step, 1)
                dve.wait_ge(dve_step, steps[0])

            def split_lo(n, s, cols=UNIT):
                dve.wait_ge(hi_ready, n + 1)
                v.tensor_tensor(slot(w_lo, s % SPLIT_SLOTS, cols), slot(raw, s % RAW_SLOTS, cols),
                                slot(w_hi, s % SPLIT_SLOTS, cols), ALU.subtract).then_inc(lo_ready, 1)

            def mean_square(n, t):
                dve.wait_ge(sumsq_ready, TT * n + t + 1)
                v.tensor_scalar(meansq[:, t:t + 1], sumsq[:, t:t + 1], 1.0 / D_MODEL, NORM_EPS, ALU.mult, ALU.add).then_inc(meansq_ready, 1)

            def norm_rows(n, t):
                dve.wait_ge(gain_landed, 16 * (n + 1))
                dve.wait_ge(rstd_ready, TT * n + t + 1)
                v.scalar_tensor_tensor(rows[:, t, :], x_res[:, t, :], rstd[:, t:t + 1], gain[:, :], ALU.mult, ALU.mult).then_inc(rows_ready, 1)

            def turned_lo(r, banks=range(4)):
                for b in banks:
                    dve.wait_ge(h_hi_ready, NORM_TURNED[r] + b + 1)
                    v.tensor_tensor(h_lo[:, b * BANK:(b + 1) * BANK], ps[:, b, :], h_hi[:, b * BANK:(b + 1) * BANK], ALU.subtract).then_inc(h_ready, 1)

            def add_residual(t, ready, value):
                dve.wait_ge(ready, value)
                v.tensor_tensor(x_res[:, t, :], x_res[:, t, :], ps_all[:, (4 + 2 * t) * BANK:(6 + 2 * t) * BANK], ALU.add).then_inc(x_written, 1)

            def norm_between(norm, tiles_done, n):
                split_lo(n, n)
                add_residual(0, tile_done, tiles_done)
                mean_square(norm, 0)
                norm_rows(norm, 0)
                add_residual(1, unit_used, n)
                turned_lo(norm, (0,))
                mean_square(norm, 1)
                turned_lo(norm, (1,))
                split_lo(n + 1, n + 1)
                norm_rows(norm, 1)
                turned_lo(norm, (2, 3))

            def mixer(layer):
                first = IN_AT[layer]

                def beside(n):
                    if n in CHUNK_LAST:
                        q = CHUNK_LAST[n]
                        c = IN_ORDER[q]
                        width = BANK if c < IN_CHUNKS - 1 else P
                        dve.wait_ge(unit_used, first + n + 1)
                        v.tensor_copy(proj[:, 1, c * BANK:c * BANK + width], ps[:, 2 * (q % 2) + 1, 0:width]).then_inc(proj_dve, 1)
                    if n == GELU_AT:
                        dve.wait_ge(gmlp_w_landed[layer], 16)
                        w = gmlp_w[:, layer * GROUPS * CHUNK:(layer + 1) * GROUPS * CHUNK].rearrange("p (g i) -> p g i", g=GROUPS)
                        v.tensor_tensor(w, w, causal_t.unsqueeze(1).to_broadcast([P, GROUPS, CHUNK]), ALU.mult).then_inc(gmlp_masked, 1)
                    if n == GATE_NORM_AT:
                        gate_norm()
                    if n == GMLP_AT:
                        dve.wait_ge(gmlp_out, layer + 1)
                        dve.wait_ge(bias_landed, 16)
                        for g in range(GROUPS):
                            last = v.scalar_tensor_tensor(rows[:, :, 2 * WIDTH + g * HEAD:2 * WIDTH + (g + 1) * HEAD],
                                                          ps[:, 7, g * P:(g + 1) * P].rearrange("p (t e) -> p t e", t=TT),
                                                          gmlp_bias[:, layer * GROUPS + g:layer * GROUPS + g + 1],
                                                          proj[:, :, C_GU + g * HEAD:C_GU + (g + 1) * HEAD], ALU.add, ALU.mult)
                        last.then_inc(gmlp_stored, 1)
                    if n == ATT_TURN_AT:
                        copy_turned(0, 4, 1)
                        copy_turned(1, 5, 2)
                    if n - ATT_AT - 2 in range(PAIRS):
                        attention_out(n - ATT_AT - 2)
                    if n == ATT_AT:
                        dve.wait_ge(masks_landed, 16)
                    if n - ATT_AT in range(PAIRS):
                        for h in pair_heads(n - ATT_AT):
                            a = (h % 2) * 3 * P
                            dve.wait_ge(att_scored, HEADS * layer + h + 1)
                            if h >= 2:
                                dve.wait_ge(p_turned, HEADS * layer + h - 1)
                            then(v.scalar_tensor_tensor(att_p[:, a:a + 3 * P], ps[:, 4 + h % 2, 0:3 * P], HEAD ** -0.5, alibi[:, h, :], ALU.mult, ALU.add))
                            v.tensor_reduce(att_nmax[:, 2 * (h % 2):2 * (h % 2) + 1], att_p[:, a:a + P], AX.X, ALU.max, negate=True)
                            v.tensor_reduce(att_nmax[:, 2 * (h % 2) + 1:2 * (h % 2) + 2], att_p[:, a + P:a + 3 * P], AX.X, ALU.max, negate=True).then_inc(att_biased, 1)
                    if n == RET_TURN_AT:
                        copy_turned(3, 2, 4)

                def copy_turned(pair, bank, turned):
                    dve.wait_ge(qk_turned, 6 * layer + turned)
                    v.tensor_copy(qk_sb[:, pair * BANK:(pair + 1) * BANK], ps[:, bank, :]).then_inc(qk_dve, 1)

                def gate_norm():
                    dve.wait_ge(gelu_ready, layer + 1)
                    for t in range(TT):
                        last = v.bn_stats(bn6[:, 6 * t:6 * t + 6], proj[:, t, C_GV:])
                    then(last)
                    for t in range(TT):
                        last = v.bn_aggr(bn2[:, 2 * t:2 * t + 2], bn6[:, 6 * t:6 * t + 6])
                    then(last)
                    var = bn2.rearrange("p (t s) -> p s t", t=TT)[:, 1, :]
                    v.tensor_scalar(var, var, GN_EPS, None, ALU.add).then_inc(gate_var, 1)
                    dve.wait_ge(gate_rstd, layer + 1)
                    for t in range(TT):
                        last = v.tensor_scalar(proj[:, t, C_GV:], proj[:, t, C_GV:], bn2[:, 2 * t:2 * t + 1], gate_rs[:, t:t + 1], ALU.subtract, ALU.mult)
                    last.then_inc(gv_ready, 1)

                def attention_out(k):
                    a = 2 * k
                    pair_sum, pair_inverse = (s.rearrange("p (t h) -> p h t", t=TT)[:, a:a + 2, :] for s in (att_sum, att_rinv))
                    dve.wait_ge(att_exped, HEADS * layer + a + 2)
                    then(v.reciprocal(pair_inverse, pair_sum))
                    dve.wait_ge(att_out, HEADS * layer + a + 2)
                    dve.wait_ge(att_scored, HEADS * layer + min(a + 6, HEADS))
                    v.tensor_tensor(rows[:, :, WIDTH + a * HEAD:WIDTH + (a + 2) * HEAD].rearrange("p t (h e) -> p h t e", h=2),
                                    ps[:, 4:6, 3 * P:].rearrange("p h (t e) -> p h t e", t=TT),
                                    pair_inverse.unsqueeze(3).to_broadcast([P, 2, TT, HEAD]), ALU.mult).then_inc(att_stored, 2)

                def decayed(heads):
                    for h in heads:
                        a = (h % RET_BUFFERS) * 3 * P
                        dve.wait_ge(ret_scored, HEADS * layer + h + 1)
                        if h >= RET_BUFFERS:
                            dve.wait_ge(ret_out, HEADS * layer + h - RET_BUFFERS + 1)
                        v.tensor_tensor(ret_w[:, a:a + 3 * P], ps[:, 2 + h % 2, 0:3 * P], decay[:, h, :], ALU.mult).then_inc(ret_decayed, 1)

                def block_lo(b):
                    src, (hi, lo) = turned_block(b, (h_hi, h_lo))
                    dve.wait_ge(h_hi_ready, OUT_TURNED[layer] + b + 1)
                    v.tensor_tensor(lo, src, hi, ALU.subtract).then_inc(h_ready, 1)

                for i in range(len(IN_UNITS) + 2):
                    if i >= AHEAD:
                        split_lo(first + i, first + i, KT * P if IN_UNITS[i:i + 1] == [(IN_CHUNKS - 1, 0)] else UNIT)
                    if i >= 2:
                        beside(i - 2)
                decayed((0, 1))
                block_lo(0)
                decayed((2, 3))
                block_lo(1)
                decayed((4, 5))
                split_lo(OUT_AT[layer] + 2, OUT_AT[layer] + 2)
                block_lo(2)
                dve.wait_ge(ret_out, HEADS * (layer + 1))
                by_head = lambda s: s.rearrange("p (h e) -> p h e", h=HEADS)
                wide = lambda s, t: s[:, t * HEADS:(t + 1) * HEADS].unsqueeze(2).to_broadcast([P, HEADS, HEAD])
                o, mixed, square = ([by_head(s[:, t, 0:WIDTH]) for t in range(TT)] for s in (ps[:, 0:2, :], rows, proj))
                for t in range(TT):
                    last = v.tensor_reduce(ret_mean[:, t * HEADS:(t + 1) * HEADS], o[t], AX.X, ALU.add)
                then(last)
                for t in range(TT):
                    last = v.scalar_tensor_tensor(mixed[t], wide(ret_mean, t), -1.0 / HEAD, o[t], ALU.mult, ALU.add)
                then(last)
                for t in range(TT):
                    last = v.tensor_tensor(square[t], mixed[t], mixed[t], ALU.mult)
                then(last)
                for t in range(TT):
                    then(v.tensor_reduce(scaled[:, t * HEADS:(t + 1) * HEADS], square[t], AX.X, ALU.add))
                    v.tensor_scalar(ret_sq[:, t * HEADS:(t + 1) * HEADS], scaled[:, t * HEADS:(t + 1) * HEADS], 1.0 / HEAD, GN_EPS, ALU.mult, ALU.add).then_inc(ret_var, 1)
                dve.wait_ge(silu_ready, layer + 1)
                for t in range(TT):
                    dve.wait_ge(ret_rstd, TT * layer + t + 1)
                    then(v.tensor_tensor(mixed[t], mixed[t], wide(ret_rs, t), ALU.mult))
                    v.tensor_tensor(rows[:, t, 0:WIDTH], rows[:, t, 0:WIDTH], proj[:, t, C_RG:C_RG + WIDTH], ALU.mult).then_inc(mix_ready, 1)
                split_lo(OUT_AT[layer] + 3, OUT_AT[layer] + 3)
                block_lo(3)
                block_lo(4)

            def ffn_pass(n0, s0, passes, nt, job=None, ahead=0):
                def turned(c):
                    dve.wait_ge(actt_hi_ready, passes * FF_CHUNKS + c + 1)
                    a = (c % 2) * TT * BANK
                    bank = turned_bank(c, nt)
                    src = ps_all[:, bank * BANK:(bank + nt) * BANK]
                    v.tensor_tensor(actt_lo[:, a:a + nt * BANK], src, actt_hi[:, a:a + nt * BANK], ALU.subtract).then_inc(actt_ready, 1)

                for i in range(len(FFN)):
                    if i >= ahead:
                        split_lo(n0 + i, s0 + i)
                    if has_last(job):
                        if i == 2:
                            y_low(job)
                        if i == 6:
                            add_scattered(job)
                    if job is not None:
                        if i == 9:
                            turn_slots(job)
                        if i == 12:
                            make_slots(job + 1)
                    for c in range(FF_CHUNKS):
                        if LAST_UP[c] == i - 2:
                            dve.wait_ge(unit_used, n0 + (LAST_UP[c] + 1))
                            dve.wait_ge(silu_done, passes * FF_CHUNKS + c + 1)
                            if c:
                                dve.wait_ge(act_turned, passes * FF_CHUNKS + c)
                            v.tensor_tensor(act_s[:, 0:nt * BANK], gate_s[:, 0:nt * BANK], ps_all[:, nt * BANK:2 * nt * BANK], ALU.mult).then_inc(act_ready, 1)
                        if TRANSPOSE_AFTER[c] == i - 3:
                            turned(c)
                            if c == FF_CHUNKS - 1 and job is not None:
                                gathered_low(job + 1)

            def gathered_low(job, banks=range(2)):
                for b in banks:
                    dve.wait_ge(h_hi_ready, JOBS_TURNED + 2 * job + (b + 1))
                    v.tensor_tensor(h_lo[:, b * BANK:(b + 1) * BANK], ps[:, 2 + b, :], h_hi[:, b * BANK:(b + 1) * BANK], ALU.subtract).then_inc(h_ready, 1)

            def y_low(job):
                dve.wait_ge(y_hi_ready, job)
                v.scalar_tensor_tensor(y_lo[:, :], ps_all[:, 4 * BANK:6 * BANK], slot_gate, y_hi[:, :], ALU.mult, ALU.subtract).then_inc(y_ready, 1)

            def add_scattered(job, done=x_added):
                dve.wait_ge(scattered, job)
                x_two = lambda t: x_res[:, t, :].rearrange("p (h n) -> p h n", h=2)
                v.tensor_tensor(x_two(0), x_two(0), ps[:, 2:4, :], ALU.add).then_inc(done, 1)
                v.tensor_tensor(x_two(1), x_two(1), ps[:, 6:8, :], ALU.add).then_inc(done, 1)

            def turn_slots(job):
                dve.wait_ge(slots_turned, job + 1)
                v.tensor_copy(slots_t[:, :], ps[:, 2, 0:P].bitcast(BF16))
                v.tensor_reduce(slot_gate, ps[:, 2, P:P + 3], AX.X, ALU.add).then_inc(slots_t_ready, 1)

            def make_place(job):
                if not isinstance(job, int):
                    v.tensor_copy(cur_place.rearrange("p (t a) -> p t a", t=TT), place[:, :, bass.ds(job, 1)]).then_inc(place_copied, 1)
                    dve.wait_ge(place_copied, job - 1)
                for t in range(TT):
                    at = place[:, t, job:job + 1] if isinstance(job, int) else cur_place[:, t:t + 1]
                    last = v.tensor_scalar(slots[:, t * P:(t + 1) * P], count_up, at, None, ALU.is_equal)
                last.then_inc(slots_ready, 1)

            def make_weight(job):
                its = slice(job, job + 1) if isinstance(job, int) else bass.ds(job, 1)
                v.tensor_copy(cur_weight[:, :].rearrange("p (t a s) -> p t a s", t=TT, a=1), weight_3[:, :, its, :]).then_inc(weight_copied, 1)

            def make_slots(job):
                dve.wait_ge(slots_turned, job)
                make_place(job)
                make_weight(job)

            def second_jobs():
                then(v.tensor_scalar(over, counts[:, 16:24], float(P), None, ALU.is_gt))
                then(v.tensor_tensor_scan(over_rank, ones[:, 0:EXPERTS], over, 0.0, ALU.mult, ALU.add))
                by_rank = lambda row: row.unsqueeze(1).to_broadcast([P, SECOND, EXPERTS])
                by_tile = lambda rows_: rows_.unsqueeze(1).to_broadcast([P, TT, SECOND, EXPERTS])
                then(v.tensor_tensor(pick, by_rank(over_rank), count_up[:, 0:SECOND].unsqueeze(2).to_broadcast([P, SECOND, EXPERTS]), ALU.is_equal))
                then(v.tensor_tensor(pick, pick, by_rank(over), ALU.mult))
                for table, source in ((place, place[:, :, 0:EXPERTS]), (weight, gates)):
                    then(v.tensor_tensor(product, source.unsqueeze(2).to_broadcast([P, TT, SECOND, EXPERTS]), by_tile(pick), ALU.mult))
                    then(v.tensor_reduce(table[:, :, EXPERTS:], product, AX.X, ALU.add))
                v.tensor_scalar(place[:, :, EXPERTS:], place[:, :, EXPERTS:], -float(P), None, ALU.add)
                gates_in_parts(EXPERTS, MAX_JOBS)
                then(v.tensor_scalar(jobs[:, 0:EXPERTS], count_up[:, 0:EXPERTS], -1.0, None, ALU.add))
                then(v.tensor_tensor(product[:, 0, :, :], pick, by_rank(jobs[:, 0:EXPERTS]), ALU.mult))
                v.tensor_reduce(jobs[:, EXPERTS:MAX_JOBS], product[:, 0, :, :], AX.X, ALU.add)
                v.memset(jobs[:, MAX_JOBS:15], 0.0)
                then(v.tensor_scalar(jobs[:, 15:16], over_rank[:, EXPERTS - 1:EXPERTS], float(EXPERTS), None, ALU.add))
                v.tensor_copy(jobs_i[:, :], jobs).then_inc(jobs_ready, 1)

            def gates_in_parts(a, b):
                rest = weight_rest[:, :, a:b]
                part_of = lambda n: weight_3[:, :, a:b, n:n + 1].rearrange("p t j s -> p t (j s)")
                then(v.tensor_copy(part_of(0), weight[:, :, a:b]))
                then(v.tensor_tensor(rest, weight[:, :, a:b], part_of(0), ALU.subtract))
                then(v.tensor_copy(part_of(1), rest))
                then(v.tensor_tensor(part_of(2), rest, part_of(1), ALU.subtract))

            for t in range(TT):
                dve.wait_ge(x_landed[t], 16)
                mean_square(0, t)
                norm_rows(0, t)
            dve.wait_ge(tables_landed, 16)
            turned_lo(0, (0, 1))
            split_lo(0, 0)
            split_lo(1, 1)
            turned_lo(0, (2, 3))
            v.tensor_copy(tables_b[:, :], small[:, 0:3 * P]).then_inc(tables_b_ready, 1)
            mixer(0)
            norm_between(1, 1, DENSE_AT)
            ffn_pass(DENSE_AT, DENSE_AT, 0, 2, ahead=AHEAD)
            norm_between(2, 2, IN_AT[1])
            dve.wait_ge(router_hi_ready, 1)
            v.tensor_tensor(router_parts[:, :, 1, :], router_w[:, :].rearrange("p (k e) -> p k e", k=KT), router_parts[:, :, 0, :], ALU.subtract).then_inc(router_ready, 1)
            mixer(1)
            split_lo(MOE_AT, MOE_AT)
            add_residual(0, tile_done, 3)
            mean_square(3, 0)
            norm_rows(3, 0)
            add_residual(1, unit_used, MOE_AT)
            turned_lo(3, (0,))
            mean_square(3, 1)
            turned_lo(3, (1,))
            norm_rows(3, 1)
            split_lo(MOE_AT + 1, MOE_AT + 1)
            turned_lo(3, (2, 3))
            for t in range(TT):
                dve.wait_ge(logits_summed, t + 1)
                v.tensor_copy(logits_t[0:2 * EXPERTS, t * P:(t + 1) * P], ps[0:2 * EXPERTS, 4 + t, 0:P]).then_inc(logits_copied, 1)
            dve.wait_ge(logits_ready, 1)
            then(v.tensor_copy(logit_parts, ps[:, 2, 0:TT * 2 * EXPERTS].rearrange("p (t s e) -> p t s e", t=TT, s=2)))
            then(v.tensor_tensor(logits, logit_parts[:, :, 1, :], logit_parts[:, :, 0, :], ALU.add))
            for t in range(TT):
                last = v.max(top[:, t, :], logits[:, t, :])
            then(last)
            for t in range(TT):
                last = v.max_index(index_u[:, t * EXPERTS:(t + 1) * EXPERTS], top[:, t, :], logits[:, t, :])
            then(last)
            v.tensor_tensor(gap.unsqueeze(2), top[:, :, 1:2], top[:, :, 0:1], ALU.subtract).then_inc(gap_ready, 1)
            then(v.tensor_copy(top_at, index_u[:, :].rearrange("p (t e) -> p t e", t=TT)))
            then(v.tensor_scalar(top_at, top_at, 1.0, None, ALU.add))
            for t in range(TT):
                v.tensor_scalar(first[:, t, :], count_up[:, 0:EXPERTS], top_at[:, t, 0:1], None, ALU.is_equal)
                last = v.tensor_scalar(second[:, t, :], count_up[:, 0:EXPERTS], top_at[:, t, 1:2], None, ALU.is_equal)
            then(last)
            v.tensor_tensor(mask, first, second, ALU.add).then_inc(mask_ready, 1)
            dve.wait_ge(counted, 1)
            then(v.tensor_copy(counts, ps[:, 3, 0:24]))
            then(v.tensor_tensor(place[:, :, 0:EXPERTS], counts[:, 0:16].rearrange("p (t e) -> p t e", t=TT), mask, ALU.mult))
            make_place(0)
            dve.wait_ge(gap_exped, 1)
            then(v.tensor_scalar(g_den, gap_e, 1.0, None, ALU.add))
            then(v.reciprocal(g_one, g_den))
            then(v.tensor_tensor(g_two, gap_e, g_one, ALU.mult))
            for t in range(TT):
                last = v.tensor_scalar(second[:, t, :], second[:, t, :], g_two[:, t:t + 1], None, ALU.mult)
            then(last)
            for t in range(TT):
                last = v.scalar_tensor_tensor(gates[:, t, :], first[:, t, :], g_one[:, t:t + 1], second[:, t, :], ALU.mult, ALU.add)
            then(last)
            then(v.tensor_copy(weight[:, :, 0:EXPERTS], gates))
            gates_in_parts(0, EXPERTS)
            make_weight(0)
            gathered_low(0, (0,))
            second_jobs()
            gathered_low(0, (1,))
            split_lo(MOE_AT + 2, MOE_AT + 2)
            ffn_pass(MOE_AT, MOE_AT, 1, 1, job=0, ahead=SPLIT_SLOTS)
            dve.wait_ge(jobs_ready, 1)
            n_jobs = dve.value_load(jobs_i[0:1, 15:16], min_val=EXPERTS, max_val=MAX_JOBS - 1)
            with dve.Fori(1, n_jobs) as j:
                ffn_pass(len(FFN) * j + MOE_AT, MOE_AT, j + 1, 1, job=j)
            y_low(n_jobs)
            add_scattered(n_jobs, x_written)
            for t in range(TT):
                mean_square(4, t)
                norm_rows(4, t)

        @block.tensor
        def _(pe):
            mm = nc.tensor.matmul

            def product(dst, a_hi, a_lo, b_hi, b_lo, start, stop):
                mm(dst, a_hi, b_lo, start=start, stop=False)
                mm(dst, a_lo, b_hi, start=False, stop=False)
                return mm(dst, a_hi, b_hi, start=False, stop=stop)

            def unit_ready(n):
                pe.wait_ge(lo_ready, n + 1)

            def h_part(t, k, tile):
                a = (tile * KT + k) * P
                return t[:, a:a + P]

            def turn_rows(ready, value, tiles):
                for t in tiles:
                    pe.wait_ge(ready, value + t)
                    for k in range(KT):
                        a = (k % 4) * P
                        last = nc.tensor.transpose(ps[:, 2 * t + k // 4, a:a + P], rows[:, t, k * P:(k + 1) * P], identity)
                        if k % 4 == 3:
                            last.then_inc(rows_turned, 1)

            def turn_heads(layer, pair, bank, columns):
                for s, c in enumerate(columns):
                    for t in range(TT):
                        a = s * SEQ + t * P
                        last = nc.tensor.transpose(ps[:, bank, a:a + P], proj[:, t, c + pair * P:c + (pair + 1) * P], identity)
                last.then_inc(qk_turned, 1)

            def head_of(pair0, h):
                return (qk_t[(h % 2) * HEAD:(h % 2 + 1) * HEAD, pair0 + h // 2, s, :] for s in range(2))

            def beside(layer, n):
                if n == GMLP_AT:
                    pe.wait_ge(gmlp_masked, layer + 1)
                    pe.wait_ge(gv_ready, layer + 1)
                    for g in range(GROUPS):
                        w = gmlp_w[:, (layer * GROUPS + g) * CHUNK:(layer * GROUPS + g + 1) * CHUNK]
                        last = mm(ps[:, 7, g * P:(g + 1) * P], w, proj[:, :, C_GV + g * HEAD:C_GV + (g + 1) * HEAD], start=True, stop=True)
                    last.then_inc(gmlp_out, 1)
                if n == ATT_TURN_AT:
                    pe.wait_ge(proj_act, IN_CHUNKS * layer + 4)
                    pe.wait_ge(proj_dve, IN_CHUNKS * layer + 4)
                    for pair in range(PAIRS):
                        turn_heads(layer, pair, 4 + pair, (C_MQ, C_MK))
                if n - ATT_AT - 2 in range(PAIRS):
                    for h in pair_heads(n - ATT_AT - 2):
                        pe.wait_ge(att_biased, HEADS * layer + min(h + 3, HEADS))
                        if h >= 2:
                            pe.wait_ge(att_stored, HEADS * layer + 2 * (h // 2))
                        pe.wait_ge(pt_ready, HEADS * layer + h + 1)
                        weigh_values(4 + h % 2, 3 * P, 4 + h % 2, 3 * P + HEAD, att_pt, h % 2, C_MV, h).then_inc(att_out, 1)
                if n - ATT_AT in range(PAIRS):
                    for h in pair_heads(n - ATT_AT):
                        if n == ATT_AT:
                            pe.wait_ge(qk_dve, 3 * layer + 2)
                            pe.wait_ge(qk_act, 3 * layer + 1)
                        else:
                            pe.wait_ge(att_biased, HEADS * layer + h - 1)
                        q, k = head_of(0, h)
                        mm(ps[:, 4 + h % 2, 0:P], q[:, 0:P], k[:, 0:P], start=True, stop=True)
                        mm(ps[:, 4 + h % 2, P:3 * P], q[:, P:], k, start=True, stop=True).then_inc(att_scored, 1)
                if n - ATT_AT - 1 in range(PAIRS):
                    for h in pair_heads(n - ATT_AT - 1):
                        pe.wait_ge(att_exped, HEADS * layer + h + 1)
                        if h < 2:
                            pe.wait_ge(gmlp_stored, layer + 1)
                        else:
                            pe.wait_ge(pt_ready, HEADS * layer + h - 1)
                        a = (h % 2) * 3 * P
                        for b in range(3):
                            last = nc.tensor.transpose(ps[:, 6 + h % 2, b * P:(b + 1) * P], att_p[:, a + b * P:a + (b + 1) * P], identity)
                        last.then_inc(p_turned, 1)
                if n == RET_TURN_AT:
                    pe.wait_ge(proj_act, IN_CHUNKS * layer + 6)
                    pe.wait_ge(proj_dve, IN_CHUNKS * layer + 6)
                    for pair in range(2):
                        turn_heads(layer, pair, 2 + pair, (C_RQ, C_RK))
                if n == RET_TURN_AT + 1:
                    pe.wait_ge(pt_ready, HEADS * (layer + 1))
                    turn_heads(layer, 2, 6, (C_RQ, C_RK))
                    pe.wait_ge(qk_dve, 3 * (layer + 1))
                    pe.wait_ge(qk_act, 3 * layer + 2)
                    retention_scores(layer, (0, 1))

            def weigh_values(bank0, at0, bank1, at1, weights, buffer, column, h):
                a = buffer * 3 * P
                value = lambda t: proj[:, t, column + h * HEAD:column + (h + 1) * HEAD]
                mm(ps[:, bank0, at0:at0 + HEAD], weights[:, a:a + P], value(0), start=True, stop=True)
                mm(ps[:, bank1, at1:at1 + HEAD], weights[:, a + P:a + 2 * P], value(0), start=True, stop=False)
                return mm(ps[:, bank1, at1:at1 + HEAD], weights[:, a + 2 * P:a + 3 * P], value(1), start=False, stop=True)

            def retention_scores(layer, heads):
                for h in heads:
                    if h >= 2:
                        pe.wait_ge(ret_decayed, HEADS * layer + h - 1)
                    q, k = head_of(PAIRS, h)
                    mm(ps[:, 2 + h % 2, 0:SEQ], k[:, 0:P], q, start=True, stop=True)
                    mm(ps[:, 2 + h % 2, SEQ:SEQ + P], k[:, P:], q[:, P:], start=True, stop=True).then_inc(ret_scored, 1)

            def retention_outputs(layer, heads):
                for h in heads:
                    pe.wait_ge(ret_decayed, HEADS * layer + h + 1)
                    weigh_values(0, h * HEAD, 1, h * HEAD, ret_w, h % RET_BUFFERS, C_RV, h).then_inc(ret_out, 1)

            def turn_block(bank, tiles, ks):
                for i, (t, k) in enumerate((t, k) for t in tiles for k in ks):
                    last = nc.tensor.transpose(ps[:, bank, i * P:(i + 1) * P], rows[:, t, k * P:(k + 1) * P], identity)
                last.then_inc(rows_turned, 1)

            def project_out(layer, t, u, js=(0, 1)):
                n = OUT_AT[layer] + u
                unit_ready(n)
                for j in js:
                    k = OUT_UNITS[u][j]
                    for half in range(2):
                        w = (part(x, n % SPLIT_SLOTS, 2, j, half * BANK, BANK, D_MODEL) for x in (w_hi, w_lo))
                        last = product(ps[:, 4 + 2 * t + half, :], h_part(h_hi, k, t), h_part(h_lo, k, t), *w, start=k == 6, stop=k == 2)
                return last

            def mixer(layer):
                h_tile = NORM_TURNED[2 * layer]
                for t in range(TT):
                    turn_rows(rows_ready, 2 * TT * layer + 1, (t,))
                    for h in range(2):
                        n = IN_AT[layer] + h
                        pe.wait_ge(h_ready, h_tile + 2 * t + h + 1)
                        unit_ready(n)
                        for k in range(4):
                            w = (part(x, n % SPLIT_SLOTS, 4, k) for x in (w_hi, w_lo))
                            last = product(ps[:, t, :], h_part(h_hi, 4 * h + k, t), h_part(h_lo, 4 * h + k, t), *w, start=h == 0 and k == 0, stop=h == 1 and k == 3)
                        if t == TT - 1:
                            last.then_inc(unit_used, 1)
                for i, (c, h) in enumerate(IN_UNITS):
                    n = IN_AT[layer] + i
                    q = IN_ORDER.index(c)
                    if i >= 2:
                        if h == 0 and q >= 2:
                            pe.wait_ge(proj_act, IN_CHUNKS * layer + q - 1)
                            pe.wait_ge(proj_dve, IN_CHUNKS * layer + q - 1)
                        unit_ready(n)
                        whole = c == IN_CHUNKS - 1
                        ks, width = (range(KT), P) if whole else (range(4 * h, 4 * h + 4), BANK)
                        for k in ks:
                            for t in range(TT):
                                w = (part(x, n % SPLIT_SLOTS, 0, k - ks[0], 0, width, width) for x in (w_hi, w_lo))
                                last = product(ps[:, 2 * (q % 2) + t, 0:width], h_part(h_hi, k, t), h_part(h_lo, k, t), *w, start=k == 0, stop=k == KT - 1)
                        last.then_inc(unit_used, 1)
                    beside(layer, i)
                turned = OUT_TURNED[layer]
                turn_block(7, (0, 1), (6, 7))
                pe.wait_ge(att_stored, HEADS * (layer + 1))
                pe.wait_ge(qk_act, 3 * (layer + 1))
                turn_block(6, (0,), (3, 4, 5))
                retention_scores(layer, (2, 3))
                pe.wait_ge(proj_act, IN_CHUNKS * (layer + 1))
                pe.wait_ge(proj_dve, IN_CHUNKS * (layer + 1))
                retention_outputs(layer, (0, 1))
                retention_scores(layer, (4, 5))
                pe.wait_ge(h_ready, turned + 1)
                project_out(layer, 0, 0)
                retention_outputs(layer, (2, 3, 4, 5))
                turn_block(7, (1,), (3, 4, 5))
                pe.wait_ge(h_ready, turned + 2)
                project_out(layer, 0, 1)
                project_out(layer, 0, 2, (1,))
                pe.wait_ge(h_ready, turned + 3)
                project_out(layer, 1, 0).then_inc(unit_used, 1)
                project_out(layer, 1, 1).then_inc(unit_used, 1)
                for t in range(TT):
                    pe.wait_ge(mix_ready, TT * layer + t + 1)
                    turn_block(2 + t, (t,), (0, 1, 2))
                project_out(layer, 1, 2, (1,))
                for t in range(TT):
                    pe.wait_ge(h_ready, turned + 4 + t)
                    last = project_out(layer, t, 2, (0,))
                    if t == TT - 1:
                        last.then_inc(unit_used, 1)
                    project_out(layer, t, 3).then_inc(unit_used if t == TT - 1 else tile_done, 1)

            def ffn_pass(n0, s0, passes, nt, job=None):
                def turn(c):
                    pe.wait_ge(act_ready, passes * FF_CHUNKS + c + 1)
                    if nt == 2 and c:
                        pe.wait_ge(silu_done, passes * FF_CHUNKS + min(c + 2, FF_CHUNKS))
                    if c:
                        pe.wait_ge(actt_ready, passes * FF_CHUNKS + c)
                    elif has_last(job):
                        pe.wait_ge(x_added, TT * job)
                    for t in range(nt):
                        for f in range(4):
                            last = nc.tensor.transpose(ps[:, turned_bank(c, nt) + t, f * P:(f + 1) * P], act_s[:, t * BANK + f * P:t * BANK + (f + 1) * P], identity)
                    last.then_inc(act_turned, 1)

                def multiply(i, tiles):
                    kind, c, h = FFN[i]
                    s = (s0 + i) % SPLIT_SLOTS
                    unit_ready(n0 + i)
                    for k in range(2 if kind == "down" else 4):
                        for t in tiles:
                            if kind == "down":
                                a = (c % 2) * TT * BANK + t * BANK + (2 * h + k) * P
                                for half in range(2):
                                    w = (part(x, s, 2, k, half * BANK, BANK, D_MODEL) for x in (w_hi, w_lo))
                                    last = product(ps[:, 4 + 2 * t + half, :], actt_hi[:, a:a + P], actt_lo[:, a:a + P], *w,
                                                   start=c == 0 and h == 0 and k == 0, stop=c == FF_CHUNKS - 1 and h == 1 and k == 1)
                            else:
                                w = (part(x, s, 4, k) for x in (w_hi, w_lo))
                                last = product(ps[:, (0 if kind == "gate" else nt) + t, :], h_part(h_hi, 4 * h + k, t), h_part(h_lo, 4 * h + k, t), *w,
                                               start=h == 0 and k == 0, stop=h == 1 and k == 3)
                    return last

                for i, (kind, c, h) in enumerate(FFN):
                    if job is not None and i < 2:
                        pe.wait_ge(h_ready, JOBS_TURNED + 2 * job + (i + 1))
                    if kind == "gate" and h == 0:
                        if nt == 2 and c >= 3:
                            pe.wait_ge(actt_ready, passes * FF_CHUNKS + c - 1)
                        elif c >= 1:
                            pe.wait_ge(silu_done, passes * FF_CHUNKS + c)
                    if kind == "up" and h == 0 and c >= 1:
                        pe.wait_ge(act_ready, passes * FF_CHUNKS + c)
                    if kind == "down" and h == 0:
                        pe.wait_ge(actt_ready, passes * FF_CHUNKS + c + 1)
                    if nt == 2 and i in (0, len(FFN) - 2):
                        for t in range(TT):
                            if i == 0:
                                turn_rows(rows_ready, TT + 1, (t,))
                            for u in (i, i + 1):
                                if i == 0:
                                    pe.wait_ge(h_ready, NORM_TURNED[1] + 2 * t + u + 1)
                                last = multiply(u, (t,))
                                if t == TT - 1:
                                    last.then_inc(unit_used, 1)
                            if i and t == 0:
                                last.then_inc(tile_done, 1)
                    elif nt == 1 or i not in (1, len(FFN) - 1):
                        multiply(i, range(nt)).then_inc(unit_used, 1)
                    if has_last(job) and i == 3:
                        scatter(job)
                    if job is not None and i == 7:
                        turn_slots(job)
                    if job is not None and i == TRANSPOSE_AFTER[FF_CHUNKS - 1]:
                        gather(job + 1)
                    for c2 in range(FF_CHUNKS):
                        if TRANSPOSE_AFTER[c2] == i:
                            turn(c2)

            def gather(job):
                pe.wait_ge(slots_ready, job + 1)
                if has_last(job):
                    pe.wait_ge(slots_t_ready, job)
                for k in range(KT):
                    for step, (rows_part, t) in enumerate((r, t) for r in rows_b[::-1] for t in range(TT)):
                        a = t * D_MODEL + k * P
                        last = mm(ps[:, 2 + k // 4, (k % 4) * P:(k % 4 + 1) * P], rows_part[:, a:a + P], slots[:, t * P:(t + 1) * P],
                                  start=step == 0, stop=step == 3 * TT - 1)
                    if k % 4 == 3:
                        last.then_inc(gathered, 1)

            def turn_slots(job):
                if has_last(job):
                    pe.wait_ge(x_added, TT * job)
                pe.wait_ge(weight_copied, job + 1)
                for t in range(TT):
                    nc.tensor.transpose(ps[:, 2, t * P // 2:(t + 1) * P // 2].bitcast(BF16), slots[:, t * P:(t + 1) * P], identity_b)
                for t in range(TT):
                    last = mm(ps[:, 2, P:P + 3], slots[:, t * P:(t + 1) * P], cur_weight[:, 3 * t:3 * t + 3], start=t == 0, stop=t == TT - 1)
                last.then_inc(slots_turned, 1)

            def scatter(job):
                pe.wait_ge(y_ready, job)
                for t, half, bank in ((0, 0, 2), (0, 1, 3), (1, 0, 6), (1, 1, 7)):
                    at = slots_t[:, t * P:(t + 1) * P]
                    mm(ps[:, bank, :], at, y_lo[:, half * BANK:(half + 1) * BANK], start=True, stop=False)
                    last = mm(ps[:, bank, :], at, y_hi[:, half * BANK:(half + 1) * BANK], start=False, stop=True)
                last.then_inc(scattered, 1)

            pe.wait_ge(tables_landed, 16)
            mixer(0)
            ffn_pass(DENSE_AT, DENSE_AT, 0, 2)
            mixer(1)
            pe.wait_ge(router_ready, 1)
            for t in range(TT):
                turn_rows(rows_ready, 3 * TT + 1, (t,))
                for k in range(KT):
                    pe.wait_ge(h_ready, NORM_TURNED[3] + 2 * t + k // 4 + 1)
                    for a in (h_lo, h_hi):
                        last = mm(ps[0:2 * EXPERTS, 4 + t, 0:P], router_s[:, k * 2 * EXPERTS:(k + 1) * 2 * EXPERTS], h_part(a, k, t),
                                  start=k == 0 and a is h_lo, stop=k == KT - 1 and a is h_hi)
                last.then_inc(logits_summed, 1)
            for t in range(TT):
                pe.wait_ge(logits_copied, t + 1)
                last = nc.tensor.transpose(ps[:, 2, t * 2 * EXPERTS:(t + 1) * 2 * EXPERTS], logits_t[0:2 * EXPERTS, t * P:(t + 1) * P],
                                           identity[0:2 * EXPERTS, 0:2 * EXPERTS])
            last.then_inc(logits_ready, 1)
            pe.wait_ge(tables_b_ready, 1)
            pe.wait_ge(mask_ready, 1)
            mm(ps[:, 3, 0:8], causal_b, mask[:, 0, :], start=True, stop=True)
            mm(ps[:, 3, 8:16], causal_b, mask[:, 1, :], start=True, stop=False)
            mm(ps[:, 3, 8:16], ones_b, mask[:, 0, :], start=False, stop=True)
            mm(ps[:, 3, 16:24], ones_b, mask[:, 0, :], start=True, stop=False)
            mm(ps[:, 3, 16:24], ones_b, mask[:, 1, :], start=False, stop=True).then_inc(counted, 1)
            pe.wait_ge(rows_b_ready, 2 * TT)
            pe.wait_ge(rows_b_done, TT)
            gather(0)
            ffn_pass(MOE_AT, MOE_AT, 1, 1, job=0)
            pe.wait_ge(jobs_ready, 1)
            n_jobs = pe.value_load(jobs_i[0:1, 15:16], min_val=EXPERTS, max_val=MAX_JOBS - 1)
            with pe.Fori(1, n_jobs) as j:
                ffn_pass(len(FFN) * j + MOE_AT, MOE_AT, j + 1, 1, job=j)
            scatter(n_jobs)


_INS = ["x", "l0_mix_norm", "l0_w_in", "l0_w_out", "l0_ffn_norm", "l0_w_gate", "l0_w_up", "l0_w_down",
        "l1_mix_norm", "l1_w_in", "l1_w_out", "l1_ffn_norm", "l1_we_gate", "l1_we_up", "l1_we_down", "final_norm"]


def kernel(**inputs):
    import concourse.bacc as bacc
    from concourse.bass_utils import run_bass_kernel_spmd

    nc = bacc.Bacc("TRN2", target_bir_lowering=False, num_devices=1)
    arrays = {n: np.ascontiguousarray(inputs[n]) for n in _INS}
    arrays["gmlp_w"] = np.ascontiguousarray(
        np.stack([np.asarray(inputs[f"l{n}_gmlp_w"]).transpose(2, 0, 1).reshape(CHUNK, -1) for n in range(2)]))
    arrays["gmlp_bias"] = np.ascontiguousarray(
        np.concatenate([np.asarray(inputs[f"l{n}_gmlp_b"]).T for n in range(2)], axis=1))
    arrays["router"] = np.ascontiguousarray(
        np.asarray(inputs["l1_router"]).reshape(KT, P, EXPERTS).transpose(1, 0, 2).reshape(P, -1))
    arrays["tables"] = shape_tables()
    ins = {n: nc.dram_tensor(f"in_{n}", a.shape, mybir.dt.from_np(a.dtype), kind="ExternalInput").ap() for n, a in arrays.items()}
    out = nc.dram_tensor("out", (1, SEQ, D_MODEL), F32, kind="ExternalOutput").ap()
    hybrid_trunk(nc, ins, out)
    got = run_bass_kernel_spmd(nc, [{f"in_{n}": a for n, a in arrays.items()}], core_ids=[0])
    return got.results[0]["out"]
```

```python
import numpy as np
import concourse.bass as bass
from concourse import mybir
from contextlib import ExitStack

F32 = mybir.dt.float32
F32R = mybir.dt.float32r
BF16 = mybir.dt.bfloat16
I32 = mybir.dt.int32
U32 = mybir.dt.uint32
ALU = mybir.AluOpType
ACT = mybir.ActivationFunctionType
AX = mybir.AxisListType

P = 128
BANK = 512
D_MODEL, SEQ, D_FF = 1024, 256, 3584
HEADS, HEAD = 6, 64
GROUPS, CHUNK = 4, 128
WIDTH = HEADS * HEAD
G_WIDTH = GROUPS * HEAD
IN_WIDTH = 7 * WIDTH + 2 * G_WIDTH
EXPERTS, MAX_JOBS = 8, 12
SECOND = MAX_JOBS - EXPERTS
TT = SEQ // P
KT = D_MODEL // P
NORM_EPS, GN_EPS = 1e-6, 1e-5

C_RQ, C_RK, C_RV, C_RG = (i * WIDTH for i in range(4))
C_MQ, C_MK, C_MV = (i * WIDTH for i in range(4, 7))
C_GU = 7 * WIDTH
C_GV = C_GU + G_WIDTH

UNIT = 2048
RAW_SLOTS, SPLIT_SLOTS = 6, 3
IN_CHUNKS = -(-IN_WIDTH // BANK)
IN_AT_COLUMN = [c * (IN_WIDTH // (8 * IN_CHUNKS)) * 8 for c in range(IN_CHUNKS)] + [IN_WIDTH]
IN_WIDTHS = [b - a for a, b in zip(IN_AT_COLUMN, IN_AT_COLUMN[1:])]
IN_ORDER = (5, 6, 3, 4, 0, 1, 2)
IN_UNITS = [(c, h) for c in IN_ORDER for h in range(2)]
CHUNK_LAST = {IN_UNITS.index((c, 1)): q for q, c in enumerate(IN_ORDER)}
GELU_AT, GATE_NORM_AT, GMLP_AT = 4, 5, 7
ATT_TURN_AT, ATT_AT, RET_TURN_AT = 8, 9, 12
PAIRS = HEADS // 2
AHEAD = 2
RET_BUFFERS = 4
OUT_UNITS = [(6, 7), (4, 5), (0, 3), (1, 2)]
FF_CHUNKS = D_FF // BANK


def unit_columns(s):
    for first in IN_AT:
        if first <= s < first + len(IN_UNITS):
            return 4 * IN_WIDTHS[IN_UNITS[s - first][0]]
    return UNIT


def has_last(job):
    return job is not None and not isinstance(job, int)


def turned_bank(c, nt):
    if nt == 1:
        return 6
    return 0 if c else 4


def ffn_units():
    units = []
    for c in range(FF_CHUNKS):
        units += [("gate", c, 0), ("gate", c, 1), ("up", c, 0), ("up", c, 1)]
        if c >= 2:
            units += [("down", c - 2, 0), ("down", c - 2, 1)]
    return units + [("down", c, h) for c in (FF_CHUNKS - 2, FF_CHUNKS - 1) for h in range(2)]


FFN = ffn_units()
LAST_UP = {c: FFN.index(("up", c, 1)) for c in range(FF_CHUNKS)}
LAST_GATE = {c: FFN.index(("gate", c, 1)) for c in range(FF_CHUNKS)}
TRANSPOSE_AFTER = {c: LAST_UP[c + 1] for c in range(FF_CHUNKS - 1)} | {FF_CHUNKS - 1: FFN.index(("down", FF_CHUNKS - 3, 1))}
GATHER_AFTER = 20
LAYER_UNITS = len(IN_UNITS) + len(OUT_UNITS)
DENSE_AT = LAYER_UNITS
IN_AT = [0, DENSE_AT + len(FFN)]
OUT_AT = [a + len(IN_UNITS) for a in IN_AT]
MOE_AT = OUT_AT[1] + len(OUT_UNITS)
NORM_TURNED, OUT_TURNED, JOBS_TURNED = (0, 9, 13, 22), (4, 17), 26
assert len(FFN) % SPLIT_SLOTS == 0
LATE_SLOT, ROWS_SLOT = 9, 10
SLOT_ORDER = [(MOE_AT + k) % RAW_SLOTS for k in range(RAW_SLOTS)] + [6, 7, 8, LATE_SLOT, ROWS_SLOT]
JOB_SLOTS = 2 * SLOT_ORDER + 2 * SLOT_ORDER[:-1]
EARLIER_SLOTS = [n % RAW_SLOTS for n in range(MOE_AT)]
assert len(JOB_SLOTS) == len(FFN)


def shape_tables():
    i = np.arange(P)
    f = np.float32
    causal_t = (i[:, None] <= i[None, :]).astype(f)
    log_g = np.log(f(1.0) - f(2.0) ** (f(-5.0) - np.arange(HEADS, dtype=f))).astype(f)
    d = np.arange(SEQ)[None, :] - i[:, None]
    wide = np.where(d >= 0, np.exp(log_g[:, None, None] * np.maximum(d, 0)), 0.0)
    decay = np.concatenate([wide, wide[:, :, :P]], axis=2) * HEAD ** -0.5
    slopes = f(2.0) ** (f(-8.0) * np.arange(1, HEADS + 1, dtype=f) / f(HEADS))
    dist = (i[:, None] + P - np.arange(SEQ)[None, :])
    own = np.where(dist >= 0, -slopes[:, None, None] * dist, -1e30)
    alibi = np.concatenate([own[:, :, P:], own], axis=2)
    flat = lambda t: t.transpose(1, 0, 2).reshape(P, -1)
    iota = np.tile(np.arange(1, P + 1), (P, 1))
    return np.concatenate([np.eye(P), causal_t, np.ones((P, P)), iota, flat(decay), flat(alibi)], axis=1).astype(f)


def hybrid_trunk(nc, ins, out):
    x_d, tables_d = ins["x"][0], ins["tables"]
    norm_d = [ins[n] for n in ("l0_mix_norm", "l0_ffn_norm", "l1_mix_norm", "l1_ffn_norm", "final_norm")]
    w_in_d = [ins["l0_w_in"], ins["l1_w_in"]]
    w_out_d = [ins["l0_w_out"], ins["l1_w_out"]]

    ctx = ExitStack()
    with ctx:
        def sem(name):
            return ctx.enter_context(nc.semaphore(name))

        def sb(name, cols, dt=F32, stack=ctx):
            return stack.enter_context(nc.sbuf_tensor(name, [P, cols], dt))

        small = sb("small", 4 * P)
        identity, causal_t, ones, count_up = (small[:, k * P:(k + 1) * P] for k in range(4))
        masks = sb("masks", 3 * UNIT)
        assert 3 * UNIT == (2 * HEADS + 4) * 3 * P
        att_p, att_pt = (masks[:, k * 3 * P:(k + 2) * 3 * P] for k in (2 * HEADS, 2 * HEADS + 2))
        decay_t, alibi_t = (masks[:, k * HEADS * 3 * P:(k + 1) * HEADS * 3 * P] for k in range(2))
        decay, alibi = (m.rearrange("p (h n) -> p h n", h=HEADS) for m in (decay_t, alibi_t))
        x_sb = sb("x_sb", TT * D_MODEL)
        x_res = x_sb[:, :].rearrange("p (t n) -> p t n", t=TT)
        rows_sb = sb("rows_sb", TT * D_MODEL)
        rows = rows_sb[:, :].rearrange("p (t n) -> p t n", t=TT)
        gain = sb("gain", D_MODEL)
        h_hi = sb("h_hi", KT * SEQ, F32R)
        h_lo = sb("h_lo", KT * SEQ, F32R)
        raw = sb("raw", RAW_SLOTS * UNIT)
        w_hi = sb("w_hi", SPLIT_SLOTS * UNIT, F32R)
        w_lo = sb("w_lo", SPLIT_SLOTS * UNIT, F32R)
        stat = sb("stat", 128)
        gmlp_bias = sb("gmlp_bias", 2 * GROUPS)
        tables_b = sb("tables_b", 3 * P, BF16)
        identity_b, causal_b, ones_b = (tables_b[:, k * P:(k + 1) * P] for k in range(3))
        exponent = sb("exponent", 2 * HEADS)
        router_w = sb("router_w", KT * EXPERTS)
        router_s = sb("router_s", KT * 2 * EXPERTS, F32R)
        router_parts = router_s[:, :].rearrange("p (k s e) -> p k s e", k=KT, s=2)
        jobs_i = sb("jobs_i", 16, I32)

        with ExitStack() as mixer:
            proj_sb = sb("proj_sb", TT * IN_WIDTH, stack=mixer)
            qk_sb = sb("qk_sb", 12 * SEQ, stack=mixer)
            ret_w = sb("ret_w", RET_BUFFERS * 3 * P, stack=mixer)
            gmlp_w = sb("gmlp_w", 2 * GROUPS * CHUNK, stack=mixer)
        proj = proj_sb[:, :].rearrange("p (t n) -> p t n", t=TT)
        qk_t = qk_sb[:, :].rearrange("p (m s n) -> p m s n", m=2 * PAIRS, s=2)

        ffn = ctx.enter_context(ExitStack())
        gate_s = sb("gate_s", TT * BANK, stack=ffn)
        act_s = sb("act_s", TT * BANK, stack=ffn)
        act_parts = [sb("act_even", 2 * TT * BANK, F32R, stack=ffn)]
        with ExitStack() as dense:
            act_parts.append(sb("act_odd", 2 * TT * BANK, F32R, stack=dense))
        late = sb("late", UNIT, stack=ffn)
        rows_b = [sb(f"rows_b{n}", TT * D_MODEL, BF16, stack=ffn) for n in range(3)]
        y_hi = sb("y_hi", D_MODEL, F32R, stack=ffn)
        y_lo = sb("y_lo", D_MODEL, F32R, stack=ffn)
        slots = sb("slots", TT * P, BF16, stack=ffn)
        slots_t = sb("slots_t", TT * P, F32R, stack=ffn)
        route = sb("route", 472, stack=ffn)
        weight_b = sb("weight_b", TT * MAX_JOBS * 3, BF16, stack=ffn)
        cur_weight = sb("cur_weight", TT * 3, BF16, stack=ffn)
        index_u = sb("index_u", TT * EXPERTS, U32, stack=ffn)
        mask_b = sb("mask_b", TT * EXPERTS, BF16, stack=ffn)
        logits_t = gain[:, 0:TT * P]
        rows_rest = (gate_s, act_s)

        ps_all = ctx.enter_context(nc.psum_tensor("ps_all", [P, 8 * BANK], F32))
        ps = ps_all[:, :].rearrange("p (b n) -> p b n", b=8)

        unit_landed = [sem(f"unit_landed{s}") for s in range(ROWS_SLOT + 1)]
        hi_ready, lo_ready, unit_used = sem("hi_ready"), sem("lo_ready"), sem("unit_used")
        tables_landed, alibi_landed, decay_landed, bias_landed = (sem(n) for n in ("tables_landed", "alibi_landed", "decay_landed", "bias_landed"))
        x_landed = [sem("x_landed0"), sem("x_landed1")]
        router_landed, out_landed = sem("router_landed"), sem("out_landed")
        gmlp_w_landed = [sem("gmlp_w_landed0"), sem("gmlp_w_landed1")]
        gain_landed, exponent_set = sem("gain_landed"), sem("exponent_set")
        x_written, sumsq_ready, meansq_ready, rstd_ready, rows_ready = (sem(n) for n in ("x_written", "sumsq_ready", "meansq_ready", "rstd_ready", "rows_ready"))
        mix_ready, rows_turned, h_hi_ready, h_ready = (sem(n) for n in ("mix_ready", "rows_turned", "h_hi_ready", "h_ready"))
        proj_act, proj_dve = sem("proj_act"), sem("proj_dve")
        qk_turned, qk_act, qk_dve = sem("qk_turned"), sem("qk_act"), sem("qk_dve")
        ret_scored, ret_decayed, ret_out = sem("ret_scored"), sem("ret_decayed"), sem("ret_out")
        att_scored, att_biased, att_exped, p_turned, pt_ready, att_out, att_stored = (sem(n) for n in ("att_scored", "att_biased", "att_exped", "p_turned", "pt_ready", "att_out", "att_stored"))
        gelu_ready, silu_ready, gate_var, gate_rstd, gv_ready, gmlp_masked, gmlp_out, gmlp_stored, ret_var, ret_rstd = (
            sem(n) for n in ("gelu_ready", "silu_ready", "gate_var", "gate_rstd", "gv_ready", "gmlp_masked", "gmlp_out", "gmlp_stored", "ret_var", "ret_rstd"))
        silu_done, act_ready, act_turned, actt_hi_ready, actt_ready = (
            sem(n) for n in ("silu_done", "act_ready", "act_turned", "actt_hi_ready", "actt_ready"))
        router_hi_ready, router_ready, rows_b_ready, rows_rest_ready, rows_b_done, logits_summed, logits_copied, logits_ready, gap_ready, gap_exped, mask_ready, counted, jobs_ready = (
            sem(n) for n in ("router_hi_ready", "router_ready", "rows_b_ready", "rows_rest_ready", "rows_b_done", "logits_summed", "logits_copied", "logits_ready", "gap_ready", "gap_exped", "mask_ready", "counted", "jobs_ready"))
        slots_ready, gathered, slots_turned, slots_t_ready, y_hi_ready, y_ready, scattered, x_added = (
            sem(n) for n in ("slots_ready", "gathered", "slots_turned", "slots_t_ready", "y_hi_ready", "y_ready", "scattered", "x_added"))
        dve_step, place_copied, tile_done, weight_copied, tables_b_ready = sem("dve_step"), sem("place_copied"), sem("tile_done"), sem("weight_copied"), sem("tables_b_ready")

        sumsq, meansq, rstd = stat[:, 0:2], stat[:, 2:4], stat[:, 4:6]
        ret_mean, ret_sq, ret_rs = stat[:, 8:20], stat[:, 20:32], stat[:, 32:44]
        att_nmax, att_sum, att_rinv = stat[:, 44:46 + 2], stat[:, 48:60], stat[:, 60:72]
        bn6, bn2, gate_rs = stat[:, 72:84], stat[:, 84:88], stat[:, 88:90]
        scaled = stat[:, 90:102]

        logits = route[:, 0:16].rearrange("p (t e) -> p t e", t=TT)
        top = route[:, 16:32].rearrange("p (t e) -> p t e", t=TT)
        top_at = route[:, 32:48].rearrange("p (t e) -> p t e", t=TT)
        first, second, gates = (route[:, 48 + 16 * k:64 + 16 * k].rearrange("p (t e) -> p t e", t=TT) for k in range(3))
        mask = mask_b[:, :].rearrange("p (t e) -> p t e", t=TT)
        gap, gap_e, g_den, g_one, g_two = (route[:, 112 + 2 * k:114 + 2 * k] for k in range(5))
        counts = route[:, 124:148]
        over, over_rank = route[:, 148:156], route[:, 156:164]
        pick = route[:, 300:300 + SECOND * EXPERTS].rearrange("p (r e) -> p r e", r=SECOND)
        product = route[:, 340:340 + TT * SECOND * EXPERTS].rearrange("p (t r e) -> p t r e", t=TT, r=SECOND)
        weight_rest = route[:, 410:410 + TT * MAX_JOBS].rearrange("p (t j) -> p t j", t=TT)
        logit_parts = route[:, 440:440 + TT * 2 * EXPERTS].rearrange("p (t s e) -> p t s e", t=TT, s=2)
        place = route[:, 188:188 + TT * MAX_JOBS].rearrange("p (t j) -> p t j", t=TT)
        weight = route[:, 212:212 + TT * MAX_JOBS].rearrange("p (t j) -> p t j", t=TT)
        jobs = route[:, 236:252]
        cur_place, slot_gate = route[:, 252:254], route[:, 256:257]
        weight_3 = weight_b[:, :].rearrange("p (t j s) -> p t j s", t=TT, s=3)

        def slot(t, s, n):
            return t[:, s * UNIT:s * UNIT + n]

        def raw_place(s, job=None):
            before = EARLIER_SLOTS + JOB_SLOTS
            i = s - MOE_AT
            p = before[s] if job is None else JOB_SLOTS[i]
            if p < LATE_SLOT:
                place = slot(raw, p, UNIT) if p < RAW_SLOTS else slot(masks, p - RAW_SLOTS, UNIT)
            else:
                place = (late if p == LATE_SLOT else rows_sb)[:, :]
            if job is None:
                count = 16 * before[:s + 1].count(p)
            else:
                each = JOB_SLOTS.count(p)
                count = job * (16 * each) + 16 * (before.count(p) - each + JOB_SLOTS[:i + 1].count(p))
            return place, unit_landed[p], count

        def part(t, s, parts, k, lo=0, n=BANK, width=BANK):
            a = s * UNIT + k * width + lo
            return t[:, a:a + n]

        def turned_block(b, parts):
            bank, tiles, k0, k1 = ((7, slice(0, 2), 6, 8), (6, slice(0, 1), 3, 6), (7, slice(1, 2), 3, 6),
                                   (2, slice(0, 1), 0, 3), (3, slice(1, 2), 0, 3))[b]
            n = (k1 - k0) * (tiles.stop - tiles.start) * P
            src = ps[:, bank, 0:n].rearrange("p (t n) -> p t n", t=tiles.stop - tiles.start)
            return src, [h[:, :].rearrange("p (t n) -> p t n", t=TT)[:, tiles, k0 * P:k1 * P] for h in parts]

        def turned_activations(c, nt):
            n = nt * BANK
            if nt == TT:
                return [act_parts[c % 2][:, h * n:(h + 1) * n] for h in range(2)]
            return [act_parts[0][:, (2 * h + c % 2) * n:(2 * h + c % 2 + 1) * n] for h in range(2)]

        def pair_heads(k):
            return (2 * k, 2 * k + 1)

        block = ctx.enter_context(nc.Block())

        @block.sync
        def _(sp):
            def load(n, s, dst_cols, parts, src):
                job = None if isinstance(n, int) else 1
                earlier = EARLIER_SLOTS + JOB_SLOTS if job is None else JOB_SLOTS + JOB_SLOTS
                at = s if job is None else s - MOE_AT + len(FFN)
                place, landed, _ = raw_place(s, job)
                if earlier[at] in earlier[:at]:
                    distance = earlier[:at][::-1].index(earlier[at]) + 1
                    sp.wait_ge(lo_ready, n - distance + 1)
                elif earlier[at] == RAW_SLOTS:
                    sp.wait_ge(att_out, 2 * HEADS)
                    sp.wait_ge(ret_decayed, 2 * HEADS)
                elif earlier[at] == LATE_SLOT:
                    sp.wait_ge(mix_ready, 2 * TT)
                elif earlier[at] == ROWS_SLOT:
                    sp.wait_ge(rows_turned, JOBS_TURNED)
                    sp.wait_ge(rows_b_ready, TT)
                    sp.wait_ge(rows_rest_ready, TT)
                sp.dma_start(place[:, 0:dst_cols].rearrange("p (k n) -> p k n", k=parts), src).then_inc(landed, 16)

            def rows_of(w, r0, nr, c0, ncol):
                return w[r0:r0 + nr * P, c0:c0 + ncol].rearrange("(k p) n -> p k n", p=P)

            def load_mixer_in(layer):
                for i, (c, h) in enumerate(IN_UNITS):
                    n = IN_AT[layer] + i
                    if layer == 0 and i == 1:
                        sp.dma_start(x_res[:, 1, :], x_d[P:, :]).then_inc(x_landed[1], 16)
                    if layer == 0 and i == 4:
                        sp.dma_start(gmlp_w[:, 0:GROUPS * CHUNK], ins["gmlp_w"][0]).then_inc(gmlp_w_landed[0], 16)
                        sp.dma_start(gmlp_bias[:, :], ins["gmlp_bias"]).then_inc(bias_landed, 16)
                    if layer == 0 and i == 7:
                        sp.dma_start(alibi_t, tables_d[:, 4 * P + HEADS * 3 * P:]).then_inc(alibi_landed, 16)
                    if layer == 0 and i == 10:
                        sp.dma_start(decay_t, tables_d[:, 4 * P:4 * P + HEADS * 3 * P]).then_inc(decay_landed, 16)
                        sp.dma_start(router_w[:, :], ins["router"]).then_inc(router_landed, 16)
                    load(n, n, 4 * IN_WIDTHS[c], 4, rows_of(w_in_d[layer], h * 4 * P, 4, IN_AT_COLUMN[c], IN_WIDTHS[c]))

            def load_mixer_out(layer):
                for i, (k0, k1) in enumerate(OUT_UNITS):
                    n = OUT_AT[layer] + i
                    w = w_out_d[layer].rearrange("(k p) n -> p k n", p=P)
                    load(n, n, UNIT, 2, w[:, k0:k1 + 1:k1 - k0, :])

            def load_ffn(n0, s0, gate, up, down):
                for i, (kind, c, h) in enumerate(FFN):
                    if kind == "down":
                        src = rows_of(down, (4 * c + 2 * h) * P, 2, 0, D_MODEL)
                        load(n0 + i, s0 + i, UNIT, 2, src)
                    else:
                        src = rows_of(gate if kind == "gate" else up, h * 4 * P, 4, c * BANK, BANK)
                        load(n0 + i, s0 + i, UNIT, 4, src)

            sp.dma_start(x_res[:, 0, :], x_d[0:P, :]).then_inc(x_landed[0], 16)
            load_mixer_in(0)
            load_mixer_out(0)
            load_ffn(DENSE_AT, DENSE_AT, ins["l0_w_gate"], ins["l0_w_up"], ins["l0_w_down"])
            load_mixer_in(1)
            load_mixer_out(1)
            load_ffn(MOE_AT, MOE_AT, ins["l1_we_gate"][0], ins["l1_we_up"][0], ins["l1_we_down"][0])
            sp.wait_ge(jobs_ready, 1)
            n_jobs = sp.value_load(jobs_i[0:1, 15:16], min_val=EXPERTS, max_val=MAX_JOBS - 1)
            with sp.Fori(1, n_jobs) as j:
                e = sp.value_load(jobs_i[0:1, bass.ds(j, 1)], min_val=0, max_val=EXPERTS - 1)
                pick_expert = lambda w: w[bass.ds(e, 1), :, :].rearrange("a r c -> (a r) c")
                load_ffn(MOE_AT + len(FFN) * j, MOE_AT, *(pick_expert(ins[w]) for w in ("l1_we_gate", "l1_we_up", "l1_we_down")))
            for t in range(TT):
                sp.wait_ge(rows_ready, TT * 4 + t + 1)
                sp.dma_start(out[0, t * P:(t + 1) * P, :], rows[:, t, :]).then_inc(out_landed, 16)
            sp.wait_ge(out_landed, 16 * TT)

        @block.gpsimd
        def _(pool):
            def load_gain(n):
                pool.dma_start(gain[:, :], norm_d[n].rearrange("(a n) -> a n", a=1).to_broadcast([P, D_MODEL])).then_inc(gain_landed, 16)

            def inverse_root(dst, src, w, ready, value, done):
                pool.wait_ge(ready, value)
                nc.gpsimd.tensor_tensor(dst, src, exponent[:, 0:w], ALU.pow).then_inc(done, 1)

            load_gain(0)
            nc.gpsimd.memset(exponent[:, :], -0.5).then_inc(exponent_set, 1)
            pool.wait_ge(exponent_set, 1)
            for n in range(5):
                for t in range(TT):
                    inverse_root(rstd[:, t:t + 1], meansq[:, t:t + 1], 1, meansq_ready, TT * n + t + 1, rstd_ready)
                if n < 3:
                    pool.wait_ge(rows_ready, TT * (n + 1))
                    load_gain(n + 1)
                if n in (0, 2):
                    layer = n // 2
                    inverse_root(gate_rs, bn2.rearrange("p (t s) -> p s t", t=TT)[:, 1, :], 2, gate_var, layer + 1, gate_rstd)
                    for t in range(TT):
                        inverse_root(ret_rs[:, t * HEADS:(t + 1) * HEADS], ret_sq[:, t * HEADS:(t + 1) * HEADS], HEADS, ret_var, TT * layer + t + 1, ret_rstd)
                if n == 3:
                    for t in range(TT):
                        b0, b1, b2 = (b[:, t * D_MODEL:(t + 1) * D_MODEL] for b in rows_b)
                        pool.wait_ge(rows_b_ready, t + 1)
                        nc.gpsimd.tensor_tensor(rows_rest[t][:, :], rows[:, t, :], b0, ALU.subtract).then_inc(rows_rest_ready, 1)
                    for t in range(TT):
                        b0, b1, b2 = (b[:, t * D_MODEL:(t + 1) * D_MODEL] for b in rows_b)
                        pool.wait_ge(rows_b_ready, TT + t + 1)
                        nc.gpsimd.tensor_tensor(b2, rows_rest[t][:, :], b1, ALU.subtract).then_inc(rows_b_done, 1)
                    pool.wait_ge(logits_ready, 1)
                    load_gain(n + 1)

        @block.scalar
        def _(act):
            def split_hi(n, s, job=None):
                cols = unit_columns(s)
                place, landed, count = raw_place(s, job)
                act.wait_ge(landed, count)
                if job is not None or n >= SPLIT_SLOTS:
                    act.wait_ge(unit_used, n - SPLIT_SLOTS + 1)
                nc.scalar.activation(slot(w_hi, s % SPLIT_SLOTS, cols), place[:, 0:cols], ACT.Copy).then_inc(hi_ready, 1)

            def norm_sums(t, ready, value):
                act.wait_ge(ready, value)
                nc.scalar.activation(rows[:, t, :], x_res[:, t, :], ACT.Square, accum_out=sumsq[:, t:t + 1]).then_inc(sumsq_ready, 1)

            def turned_hi(r, banks=range(4)):
                for b in banks:
                    act.wait_ge(rows_turned, NORM_TURNED[r] + b + 1)
                    nc.scalar.activation(h_hi[:, b * BANK:(b + 1) * BANK], ps[:, b, :], ACT.Copy).then_inc(h_hi_ready, 1)

            def norm_between(r, n, value):
                split_hi(n, n)
                norm_sums(0, x_written, value)
                split_hi(n + 1, n + 1)
                turned_hi(r, (0,))
                norm_sums(1, x_written, value + 1)
                turned_hi(r, (1, 2, 3))

            def mixer(layer):
                first = IN_AT[layer]

                def beside(n):
                    if n in CHUNK_LAST:
                        q = CHUNK_LAST[n]
                        c = IN_ORDER[q]
                        at, width = IN_AT_COLUMN[c], IN_WIDTHS[c]
                        act.wait_ge(unit_used, first + n + 1)
                        nc.scalar.activation(proj[:, 0, at:at + width], ps[:, 2 * (q % 2), 0:width], ACT.Copy).then_inc(proj_act, 1)
                    if n == GELU_AT:
                        act.wait_ge(proj_act, IN_CHUNKS * layer + 2)
                        act.wait_ge(proj_dve, IN_CHUNKS * layer + 2)
                        nc.scalar.activation(proj[:, :, C_GU:], proj[:, :, C_GU:], ACT.Gelu_apprx_tanh).then_inc(gelu_ready, 1)
                    if n == ATT_TURN_AT:
                        copy_turned(2, 6, 3)
                    if n - ATT_AT - 1 in range(PAIRS):
                        for h in pair_heads(n - ATT_AT - 1):
                            act.wait_ge(p_turned, HEADS * layer + h + 1)
                            if h >= 2:
                                act.wait_ge(att_out, HEADS * layer + h - 1)
                            nc.scalar.activation(att_pt[:, (h % 2) * 3 * P:(h % 2 + 1) * 3 * P], ps[:, 6 + h % 2, 0:3 * P], ACT.Copy).then_inc(pt_ready, 1)
                    if n - ATT_AT in range(PAIRS):
                        for h in pair_heads(n - ATT_AT):
                            act.wait_ge(att_biased, HEADS * layer + h + 1)
                            a = (h % 2) * 3 * P
                            low = att_nmax[:, 2 * (h % 2):2 * (h % 2) + 2]
                            nc.scalar.activation(att_p[:, a:a + P], att_p[:, a:a + P], ACT.Exp, bias=low[:, 0:1], accum_out=att_sum[:, h:h + 1])
                            nc.scalar.activation(att_p[:, a + P:a + 3 * P], att_p[:, a + P:a + 3 * P], ACT.Exp, bias=low[:, 1:2],
                                                 accum_out=att_sum[:, HEADS + h:HEADS + h + 1]).then_inc(att_exped, 1)
                    if n == RET_TURN_AT:
                        copy_turned(4, 3, 5)
                    if n == RET_TURN_AT + 1:
                        copy_turned(5, 6, 6)

                def copy_turned(pair, bank, turned):
                    act.wait_ge(qk_turned, 6 * layer + turned)
                    nc.scalar.activation(qk_sb[:, pair * BANK:(pair + 1) * BANK], ps[:, bank, :], ACT.Copy).then_inc(qk_act, 1)

                for i in range(len(IN_UNITS) + 2):
                    if i >= AHEAD:
                        split_hi(first + i, first + i)
                    if i >= 2:
                        beside(i - 2)
                for b in range(5):
                    if b == 2:
                        split_hi(OUT_AT[layer] + 2, OUT_AT[layer] + 2)
                    if b == 3:
                        act.wait_ge(proj_dve, IN_CHUNKS * (layer + 1))
                        act.wait_ge(proj_act, IN_CHUNKS * (layer + 1))
                        nc.scalar.activation(proj[:, :, C_RG:C_RG + WIDTH], proj[:, :, C_RG:C_RG + WIDTH], ACT.Silu).then_inc(silu_ready, 1)
                        split_hi(OUT_AT[layer] + 3, OUT_AT[layer] + 3)
                    src, (at,) = turned_block(b, (h_hi,))
                    act.wait_ge(rows_turned, OUT_TURNED[layer] + b + 1)
                    nc.scalar.activation(at, src, ACT.Copy).then_inc(h_hi_ready, 1)

            def ffn_pass(n0, s0, passes, nt, job=None, ahead=0):
                def turned(c):
                    act.wait_ge(act_turned, passes * FF_CHUNKS + c + 1)
                    bank = turned_bank(c, nt)
                    src = ps_all[:, bank * BANK:(bank + nt) * BANK]
                    nc.scalar.activation(turned_activations(c, nt)[0], src, ACT.Copy).then_inc(actt_hi_ready, 1)

                for i in range(len(FFN)):
                    if i >= ahead:
                        split_hi(n0 + i, s0 + i, job=job if has_last(job) else None)
                    if has_last(job) and i == 2:
                        y_high(job)
                    for c in range(FF_CHUNKS):
                        if LAST_GATE[c] == i - 2:
                            act.wait_ge(unit_used, n0 + (LAST_GATE[c] + 1))
                            if c:
                                act.wait_ge(act_ready, passes * FF_CHUNKS + c)
                            nc.scalar.activation(gate_s[:, 0:nt * BANK], ps_all[:, 0:nt * BANK], ACT.Silu).then_inc(silu_done, 1)
                        if TRANSPOSE_AFTER[c] == i - 3:
                            turned(c)
                            if c == FF_CHUNKS - 1 and job is not None:
                                gathered_high(job + 1)

            def y_high(job):
                act.wait_ge(unit_used, len(FFN) * job + MOE_AT)
                act.wait_ge(slots_t_ready, job)
                nc.scalar.activation(y_hi[:, :], ps_all[:, 4 * BANK:6 * BANK], ACT.Copy, scale=slot_gate).then_inc(y_hi_ready, 1)

            def gathered_high(job):
                for b in range(2):
                    act.wait_ge(gathered, 2 * job + (b + 1))
                    nc.scalar.activation(h_hi[:, b * BANK:(b + 1) * BANK], ps[:, 2 + b, :], ACT.Copy).then_inc(h_hi_ready, 1)

            def rows_part(n, t):
                act.wait_ge(*((rows_ready, TT * 3 + t + 1) if n == 0 else (rows_rest_ready, t + 1)))
                src = rows[:, t, :] if n == 0 else rows_rest[t][:, :]
                nc.scalar.activation(rows_b[n][:, t * D_MODEL:(t + 1) * D_MODEL], src, ACT.Copy).then_inc(rows_b_ready, 1)

            act.dma_start(small[:, :], tables_d[:, 0:4 * P]).then_inc(tables_landed, 16)
            norm_sums(0, x_landed[0], 16)
            turned_hi(0, (0,))
            split_hi(0, 0)
            turned_hi(0, (1,))
            norm_sums(1, x_landed[1], 16)
            split_hi(1, 1)
            turned_hi(0, (2, 3))
            mixer(0)
            norm_between(1, DENSE_AT, 1)
            ffn_pass(DENSE_AT, DENSE_AT, 0, 2, ahead=AHEAD)
            norm_between(2, IN_AT[1], TT + 1)
            act.dma_start(gmlp_w[:, GROUPS * CHUNK:], ins["gmlp_w"][1]).then_inc(gmlp_w_landed[1], 16)
            act.wait_ge(router_landed, 16)
            nc.scalar.activation(router_parts[:, :, 0, :], router_w[:, :].rearrange("p (k e) -> p k e", k=KT), ACT.Copy).then_inc(router_hi_ready, 1)
            mixer(1)
            split_hi(MOE_AT, MOE_AT)
            norm_sums(0, x_written, 2 * TT + 1)
            split_hi(MOE_AT + 1, MOE_AT + 1)
            rows_part(0, 0)
            turned_hi(3, (0,))
            norm_sums(1, x_written, 2 * TT + 2)
            turned_hi(3, (1,))
            split_hi(MOE_AT + 2, MOE_AT + 2)
            rows_part(0, 1)
            turned_hi(3, (2, 3))
            rows_part(1, 0)
            rows_part(1, 1)
            act.wait_ge(gap_ready, 1)
            nc.scalar.activation(gap_e, gap, ACT.Exp).then_inc(gap_exped, 1)
            gathered_high(0)
            ffn_pass(MOE_AT, MOE_AT, 1, 1, job=0, ahead=SPLIT_SLOTS)
            act.wait_ge(jobs_ready, 1)
            n_jobs = act.value_load(jobs_i[0:1, 15:16], min_val=EXPERTS, max_val=MAX_JOBS - 1)
            with act.Fori(1, n_jobs) as j:
                ffn_pass(len(FFN) * j + MOE_AT, MOE_AT, j + 1, 1, job=j)
            act.wait_ge(unit_used, len(FFN) * n_jobs + MOE_AT)
            act.wait_ge(slots_t_ready, n_jobs)
            for half in range(2):
                y = slice(half * BANK, (half + 1) * BANK)
                nc.scalar.activation(y_hi[:, y], ps[:, 4 + half, :], ACT.Copy, scale=slot_gate).then_inc(y_hi_ready, 1)
            for t in range(TT):
                norm_sums(t, x_written, TT * 3 + (t + 1))

        @block.vector
        def _(dve):
            v = nc.vector
            steps = [0]

            def then(instruction):
                steps[0] += 1
                instruction.then_inc(dve_step, 1)
                dve.wait_ge(dve_step, steps[0])

            def split_lo(n, s, job=None):
                cols = unit_columns(s)
                dve.wait_ge(hi_ready, n + 1)
                v.tensor_tensor(slot(w_lo, s % SPLIT_SLOTS, cols), raw_place(s, job)[0][:, 0:cols],
                                slot(w_hi, s % SPLIT_SLOTS, cols), ALU.subtract).then_inc(lo_ready, 1)

            def mean_square(n, t):
                dve.wait_ge(sumsq_ready, TT * n + t + 1)
                v.tensor_scalar(meansq[:, t:t + 1], sumsq[:, t:t + 1], 1.0 / D_MODEL, NORM_EPS, ALU.mult, ALU.add).then_inc(meansq_ready, 1)

            def norm_rows(n, t):
                dve.wait_ge(gain_landed, 16 * (n + 1))
                dve.wait_ge(rstd_ready, TT * n + t + 1)
                v.scalar_tensor_tensor(rows[:, t, :], x_res[:, t, :], rstd[:, t:t + 1], gain[:, :], ALU.mult, ALU.mult).then_inc(rows_ready, 1)

            def turned_lo(r, banks=range(4)):
                for b in banks:
                    dve.wait_ge(h_hi_ready, NORM_TURNED[r] + b + 1)
                    v.tensor_tensor(h_lo[:, b * BANK:(b + 1) * BANK], ps[:, b, :], h_hi[:, b * BANK:(b + 1) * BANK], ALU.subtract).then_inc(h_ready, 1)

            def add_residual(t, ready, value):
                dve.wait_ge(ready, value)
                v.tensor_tensor(x_res[:, t, :], x_res[:, t, :], ps_all[:, (4 + 2 * t) * BANK:(6 + 2 * t) * BANK], ALU.add).then_inc(x_written, 1)

            def norm_between(norm, tiles_done, n):
                split_lo(n, n)
                add_residual(0, tile_done, tiles_done)
                mean_square(norm, 0)
                norm_rows(norm, 0)
                add_residual(1, unit_used, n)
                turned_lo(norm, (0,))
                mean_square(norm, 1)
                turned_lo(norm, (1,))
                split_lo(n + 1, n + 1)
                norm_rows(norm, 1)
                turned_lo(norm, (2, 3))

            def mixer(layer):
                first = IN_AT[layer]

                def beside(n):
                    if n in CHUNK_LAST:
                        q = CHUNK_LAST[n]
                        c = IN_ORDER[q]
                        at, width = IN_AT_COLUMN[c], IN_WIDTHS[c]
                        dve.wait_ge(unit_used, first + n + 1)
                        v.tensor_copy(proj[:, 1, at:at + width], ps[:, 2 * (q % 2) + 1, 0:width]).then_inc(proj_dve, 1)
                    if n == GELU_AT:
                        dve.wait_ge(gmlp_w_landed[layer], 16)
                        w = gmlp_w[:, layer * GROUPS * CHUNK:(layer + 1) * GROUPS * CHUNK].rearrange("p (g i) -> p g i", g=GROUPS)
                        v.tensor_tensor(w, w, causal_t.unsqueeze(1).to_broadcast([P, GROUPS, CHUNK]), ALU.mult).then_inc(gmlp_masked, 1)
                    if n == GATE_NORM_AT:
                        gate_norm()
                    if n == GMLP_AT:
                        dve.wait_ge(gmlp_out, layer + 1)
                        dve.wait_ge(bias_landed, 16)
                        for g in range(GROUPS):
                            last = v.scalar_tensor_tensor(rows[:, :, 2 * WIDTH + g * HEAD:2 * WIDTH + (g + 1) * HEAD],
                                                          ps[:, 7, g * P:(g + 1) * P].rearrange("p (t e) -> p t e", t=TT),
                                                          gmlp_bias[:, layer * GROUPS + g:layer * GROUPS + g + 1],
                                                          proj[:, :, C_GU + g * HEAD:C_GU + (g + 1) * HEAD], ALU.add, ALU.mult)
                        last.then_inc(gmlp_stored, 1)
                    if n == ATT_TURN_AT:
                        copy_turned(0, 4, 1)
                        copy_turned(1, 5, 2)
                    if n - ATT_AT - 2 in range(PAIRS):
                        attention_out(n - ATT_AT - 2)
                    if n == ATT_AT:
                        dve.wait_ge(alibi_landed, 16)
                    if n - ATT_AT in range(PAIRS):
                        for h in pair_heads(n - ATT_AT):
                            a = (h % 2) * 3 * P
                            dve.wait_ge(att_scored, HEADS * layer + h + 1)
                            if h >= 2:
                                dve.wait_ge(p_turned, HEADS * layer + h - 1)
                            then(v.scalar_tensor_tensor(att_p[:, a:a + 3 * P], ps[:, 4 + h % 2, 0:3 * P], HEAD ** -0.5, alibi[:, h, :], ALU.mult, ALU.add))
                            v.tensor_reduce(att_nmax[:, 2 * (h % 2):2 * (h % 2) + 1], att_p[:, a:a + P], AX.X, ALU.max, negate=True)
                            v.tensor_reduce(att_nmax[:, 2 * (h % 2) + 1:2 * (h % 2) + 2], att_p[:, a + P:a + 3 * P], AX.X, ALU.max, negate=True).then_inc(att_biased, 1)
                    if n == RET_TURN_AT:
                        copy_turned(3, 2, 4)

                def copy_turned(pair, bank, turned):
                    dve.wait_ge(qk_turned, 6 * layer + turned)
                    v.tensor_copy(qk_sb[:, pair * BANK:(pair + 1) * BANK], ps[:, bank, :]).then_inc(qk_dve, 1)

                def gate_norm():
                    dve.wait_ge(gelu_ready, layer + 1)
                    for t in range(TT):
                        last = v.bn_stats(bn6[:, 6 * t:6 * t + 6], proj[:, t, C_GV:])
                    then(last)
                    for t in range(TT):
                        last = v.bn_aggr(bn2[:, 2 * t:2 * t + 2], bn6[:, 6 * t:6 * t + 6])
                    then(last)
                    var = bn2.rearrange("p (t s) -> p s t", t=TT)[:, 1, :]
                    v.tensor_scalar(var, var, GN_EPS, None, ALU.add).then_inc(gate_var, 1)
                    dve.wait_ge(gate_rstd, layer + 1)
                    for t in range(TT):
                        last = v.tensor_scalar(proj[:, t, C_GV:], proj[:, t, C_GV:], bn2[:, 2 * t:2 * t + 1], gate_rs[:, t:t + 1], ALU.subtract, ALU.mult)
                    last.then_inc(gv_ready, 1)

                def attention_out(k):
                    a = 2 * k
                    pair_sum, pair_inverse = (s.rearrange("p (t h) -> p h t", t=TT)[:, a:a + 2, :] for s in (att_sum, att_rinv))
                    dve.wait_ge(att_exped, HEADS * layer + a + 2)
                    then(v.reciprocal(pair_inverse, pair_sum))
                    dve.wait_ge(att_out, HEADS * layer + a + 2)
                    dve.wait_ge(att_scored, HEADS * layer + min(a + 6, HEADS))
                    v.tensor_tensor(rows[:, :, WIDTH + a * HEAD:WIDTH + (a + 2) * HEAD].rearrange("p t (h e) -> p h t e", h=2),
                                    ps[:, 4:6, 3 * P:].rearrange("p h (t e) -> p h t e", t=TT),
                                    pair_inverse.unsqueeze(3).to_broadcast([P, 2, TT, HEAD]), ALU.mult).then_inc(att_stored, 2)

                def decayed(heads):
                    for h in heads:
                        a = (h % RET_BUFFERS) * 3 * P
                        dve.wait_ge(ret_scored, HEADS * layer + h + 1)
                        if h >= RET_BUFFERS:
                            dve.wait_ge(ret_out, HEADS * layer + h - RET_BUFFERS + 1)
                        v.tensor_tensor(ret_w[:, a:a + 3 * P], ps[:, 2 + h % 2, 0:3 * P], decay[:, h, :], ALU.mult).then_inc(ret_decayed, 1)

                def block_lo(b):
                    src, (hi, lo) = turned_block(b, (h_hi, h_lo))
                    dve.wait_ge(h_hi_ready, OUT_TURNED[layer] + b + 1)
                    v.tensor_tensor(lo, src, hi, ALU.subtract).then_inc(h_ready, 1)

                for i in range(len(IN_UNITS) + 2):
                    if i >= AHEAD:
                        split_lo(first + i, first + i)
                    if i >= 2:
                        beside(i - 2)
                dve.wait_ge(decay_landed, 16)
                decayed((0, 1))
                block_lo(0)
                decayed((2, 3))
                block_lo(1)
                decayed((4, 5))
                split_lo(OUT_AT[layer] + 2, OUT_AT[layer] + 2)
                block_lo(2)
                dve.wait_ge(ret_out, HEADS * (layer + 1))
                by_head = lambda s: s.rearrange("p (h e) -> p h e", h=HEADS)
                wide = lambda s, t: s[:, t * HEADS:(t + 1) * HEADS].unsqueeze(2).to_broadcast([P, HEADS, HEAD])
                o, mixed, square = ([by_head(s[:, t, 0:WIDTH]) for t in range(TT)] for s in (ps[:, 0:2, :], rows, proj))
                for t in range(TT):
                    last = v.tensor_reduce(ret_mean[:, t * HEADS:(t + 1) * HEADS], o[t], AX.X, ALU.add)
                then(last)
                for t in range(TT):
                    last = v.scalar_tensor_tensor(mixed[t], wide(ret_mean, t), -1.0 / HEAD, o[t], ALU.mult, ALU.add)
                then(last)
                for t in range(TT):
                    last = v.tensor_tensor(square[t], mixed[t], mixed[t], ALU.mult)
                then(last)
                for t in range(TT):
                    then(v.tensor_reduce(scaled[:, t * HEADS:(t + 1) * HEADS], square[t], AX.X, ALU.add))
                    v.tensor_scalar(ret_sq[:, t * HEADS:(t + 1) * HEADS], scaled[:, t * HEADS:(t + 1) * HEADS], 1.0 / HEAD, GN_EPS, ALU.mult, ALU.add).then_inc(ret_var, 1)
                dve.wait_ge(silu_ready, layer + 1)
                for t in range(TT):
                    dve.wait_ge(ret_rstd, TT * layer + t + 1)
                    then(v.tensor_tensor(mixed[t], mixed[t], wide(ret_rs, t), ALU.mult))
                    v.tensor_tensor(rows[:, t, 0:WIDTH], rows[:, t, 0:WIDTH], proj[:, t, C_RG:C_RG + WIDTH], ALU.mult).then_inc(mix_ready, 1)
                split_lo(OUT_AT[layer] + 3, OUT_AT[layer] + 3)
                block_lo(3)
                block_lo(4)

            def ffn_pass(n0, s0, passes, nt, job=None, ahead=0):
                def turned(c):
                    dve.wait_ge(actt_hi_ready, passes * FF_CHUNKS + c + 1)
                    bank = turned_bank(c, nt)
                    src = ps_all[:, bank * BANK:(bank + nt) * BANK]
                    hi, lo = turned_activations(c, nt)
                    v.tensor_tensor(lo, src, hi, ALU.subtract).then_inc(actt_ready, 1)

                for i in range(len(FFN)):
                    if i >= ahead:
                        split_lo(n0 + i, s0 + i, job=job if has_last(job) else None)
                    if has_last(job):
                        if i == 2:
                            y_low(job)
                        if i == 6:
                            add_scattered(job)
                    if job is not None and not has_last(job):
                        if i == 20:
                            second_jobs()
                        if i == 26:
                            job_table()
                    if job is not None:
                        if i == 9:
                            turn_slots(job)
                        if i == 12:
                            make_slots(job + 1)
                    for c in range(FF_CHUNKS):
                        if LAST_UP[c] == i - 2:
                            dve.wait_ge(unit_used, n0 + (LAST_UP[c] + 1))
                            dve.wait_ge(silu_done, passes * FF_CHUNKS + c + 1)
                            if c:
                                dve.wait_ge(act_turned, passes * FF_CHUNKS + c)
                            v.tensor_tensor(act_s[:, 0:nt * BANK], gate_s[:, 0:nt * BANK], ps_all[:, nt * BANK:2 * nt * BANK], ALU.mult).then_inc(act_ready, 1)
                        if TRANSPOSE_AFTER[c] == i - 3:
                            turned(c)
                            if c == FF_CHUNKS - 1 and job is not None:
                                gathered_low(job + 1)

            def gathered_low(job):
                for b in range(2):
                    dve.wait_ge(h_hi_ready, JOBS_TURNED + 2 * job + (b + 1))
                    v.tensor_tensor(h_lo[:, b * BANK:(b + 1) * BANK], ps[:, 2 + b, :], h_hi[:, b * BANK:(b + 1) * BANK], ALU.subtract).then_inc(h_ready, 1)

            def y_low(job):
                dve.wait_ge(y_hi_ready, job)
                v.scalar_tensor_tensor(y_lo[:, :], ps_all[:, 4 * BANK:6 * BANK], slot_gate, y_hi[:, :], ALU.mult, ALU.subtract).then_inc(y_ready, 1)

            def add_scattered(job):
                dve.wait_ge(scattered, job)
                x_two = lambda t: x_res[:, t, :].rearrange("p (h n) -> p h n", h=2)
                v.tensor_tensor(x_two(0), x_two(0), ps[:, 2:4, :], ALU.add).then_inc(x_added, 1)
                v.tensor_tensor(x_two(1), x_two(1), ps[:, 6:8, :], ALU.add).then_inc(x_added, 1)

            def turn_slots(job):
                dve.wait_ge(slots_turned, job + 1)
                v.tensor_copy(slots_t[:, :], ps[:, 2, 0:P].bitcast(BF16))
                v.tensor_reduce(slot_gate, ps[:, 2, P:P + 3], AX.X, ALU.add).then_inc(slots_t_ready, 1)

            def make_place(job):
                if not isinstance(job, int):
                    v.tensor_copy(cur_place.rearrange("p (t a) -> p t a", t=TT), place[:, :, bass.ds(job, 1)]).then_inc(place_copied, 1)
                    dve.wait_ge(place_copied, job - 1)
                for t in range(TT):
                    at = place[:, t, job:job + 1] if isinstance(job, int) else cur_place[:, t:t + 1]
                    last = v.tensor_scalar(slots[:, t * P:(t + 1) * P], count_up, at, None, ALU.is_equal)
                last.then_inc(slots_ready, 1)

            def make_weight(job):
                its = slice(job, job + 1) if isinstance(job, int) else bass.ds(job, 1)
                v.tensor_copy(cur_weight[:, :].rearrange("p (t a s) -> p t a s", t=TT, a=1), weight_3[:, :, its, :]).then_inc(weight_copied, 1)

            def make_slots(job):
                dve.wait_ge(slots_turned, job)
                make_place(job)
                make_weight(job)

            by_rank = lambda row: row.unsqueeze(1).to_broadcast([P, SECOND, EXPERTS])

            def second_jobs():
                then(v.tensor_scalar(over, counts[:, 16:24], float(P), None, ALU.is_gt))
                then(v.tensor_tensor_scan(over_rank, ones[:, 0:EXPERTS], over, 0.0, ALU.mult, ALU.add))
                by_tile = lambda rows_: rows_.unsqueeze(1).to_broadcast([P, TT, SECOND, EXPERTS])
                then(v.tensor_tensor(pick, by_rank(over_rank), count_up[:, 0:SECOND].unsqueeze(2).to_broadcast([P, SECOND, EXPERTS]), ALU.is_equal))
                then(v.tensor_tensor(pick, pick, by_rank(over), ALU.mult))
                for table, source in ((place, place[:, :, 0:EXPERTS]), (weight, gates)):
                    then(v.tensor_tensor(product, source.unsqueeze(2).to_broadcast([P, TT, SECOND, EXPERTS]), by_tile(pick), ALU.mult))
                    then(v.tensor_reduce(table[:, :, EXPERTS:], product, AX.X, ALU.add))
                v.tensor_scalar(place[:, :, EXPERTS:], place[:, :, EXPERTS:], -float(P), None, ALU.add)
                gates_in_parts(EXPERTS, MAX_JOBS)

            def job_table():
                then(v.tensor_scalar(jobs[:, 0:EXPERTS], count_up[:, 0:EXPERTS], -1.0, None, ALU.add))
                then(v.tensor_tensor(product[:, 0, :, :], pick, by_rank(jobs[:, 0:EXPERTS]), ALU.mult))
                v.tensor_reduce(jobs[:, EXPERTS:MAX_JOBS], product[:, 0, :, :], AX.X, ALU.add)
                v.memset(jobs[:, MAX_JOBS:15], 0.0)
                then(v.tensor_scalar(jobs[:, 15:16], over_rank[:, EXPERTS - 1:EXPERTS], float(EXPERTS), None, ALU.add))
                v.tensor_copy(jobs_i[:, :], jobs).then_inc(jobs_ready, 1)

            def gates_in_parts(a, b):
                rest = weight_rest[:, :, a:b]
                part_of = lambda n: weight_3[:, :, a:b, n:n + 1].rearrange("p t j s -> p t (j s)")
                then(v.tensor_copy(part_of(0), weight[:, :, a:b]))
                then(v.tensor_tensor(rest, weight[:, :, a:b], part_of(0), ALU.subtract))
                then(v.tensor_copy(part_of(1), rest))
                then(v.tensor_tensor(part_of(2), rest, part_of(1), ALU.subtract))

            dve.wait_ge(x_landed[0], 16)
            mean_square(0, 0)
            norm_rows(0, 0)
            turned_lo(0, (0,))
            split_lo(0, 0)
            turned_lo(0, (1,))
            dve.wait_ge(x_landed[1], 16)
            mean_square(0, 1)
            split_lo(1, 1)
            norm_rows(0, 1)
            dve.wait_ge(tables_landed, 16)
            turned_lo(0, (2, 3))
            v.tensor_copy(tables_b[:, :], small[:, 0:3 * P]).then_inc(tables_b_ready, 1)
            mixer(0)
            norm_between(1, 1, DENSE_AT)
            ffn_pass(DENSE_AT, DENSE_AT, 0, 2, ahead=AHEAD)
            norm_between(2, 2, IN_AT[1])
            dve.wait_ge(router_hi_ready, 1)
            v.tensor_tensor(router_parts[:, :, 1, :], router_w[:, :].rearrange("p (k e) -> p k e", k=KT), router_parts[:, :, 0, :], ALU.subtract).then_inc(router_ready, 1)
            mixer(1)
            split_lo(MOE_AT, MOE_AT)
            add_residual(0, tile_done, 3)
            mean_square(3, 0)
            norm_rows(3, 0)
            add_residual(1, unit_used, MOE_AT)
            turned_lo(3, (0,))
            mean_square(3, 1)
            turned_lo(3, (1,))
            norm_rows(3, 1)
            split_lo(MOE_AT + 1, MOE_AT + 1)
            turned_lo(3, (2, 3))
            for t in range(TT):
                dve.wait_ge(logits_summed, t + 1)
                v.tensor_copy(logits_t[0:2 * EXPERTS, t * P:(t + 1) * P], ps[0:2 * EXPERTS, 4 + t, 0:P]).then_inc(logits_copied, 1)
            dve.wait_ge(logits_ready, 1)
            then(v.tensor_copy(logit_parts, ps[:, 2, 0:TT * 2 * EXPERTS].rearrange("p (t s e) -> p t s e", t=TT, s=2)))
            then(v.tensor_tensor(logits, logit_parts[:, :, 1, :], logit_parts[:, :, 0, :], ALU.add))
            for t in range(TT):
                last = v.max(top[:, t, :], logits[:, t, :])
            then(last)
            for t in range(TT):
                last = v.max_index(index_u[:, t * EXPERTS:(t + 1) * EXPERTS], top[:, t, :], logits[:, t, :])
            then(last)
            v.tensor_tensor(gap.unsqueeze(2), top[:, :, 1:2], top[:, :, 0:1], ALU.subtract).then_inc(gap_ready, 1)
            then(v.tensor_copy(top_at, index_u[:, :].rearrange("p (t e) -> p t e", t=TT)))
            then(v.tensor_scalar(top_at, top_at, 1.0, None, ALU.add))
            for t in range(TT):
                v.tensor_scalar(first[:, t, :], count_up[:, 0:EXPERTS], top_at[:, t, 0:1], None, ALU.is_equal)
                last = v.tensor_scalar(second[:, t, :], count_up[:, 0:EXPERTS], top_at[:, t, 1:2], None, ALU.is_equal)
            then(last)
            v.tensor_tensor(mask, first, second, ALU.add).then_inc(mask_ready, 1)
            dve.wait_ge(counted, 1)
            then(v.tensor_copy(counts, ps[:, 3, 0:24]))
            then(v.tensor_tensor(place[:, :, 0:EXPERTS], counts[:, 0:16].rearrange("p (t e) -> p t e", t=TT), mask, ALU.mult))
            make_place(0)
            dve.wait_ge(gap_exped, 1)
            then(v.tensor_scalar(g_den, gap_e, 1.0, None, ALU.add))
            then(v.reciprocal(g_one, g_den))
            then(v.tensor_tensor(g_two, gap_e, g_one, ALU.mult))
            for t in range(TT):
                last = v.tensor_scalar(second[:, t, :], second[:, t, :], g_two[:, t:t + 1], None, ALU.mult)
            then(last)
            for t in range(TT):
                last = v.scalar_tensor_tensor(gates[:, t, :], first[:, t, :], g_one[:, t:t + 1], second[:, t, :], ALU.mult, ALU.add)
            then(last)
            then(v.tensor_copy(weight[:, :, 0:EXPERTS], gates))
            gates_in_parts(0, EXPERTS)
            make_weight(0)
            split_lo(MOE_AT + 2, MOE_AT + 2)
            gathered_low(0)
            ffn_pass(MOE_AT, MOE_AT, 1, 1, job=0, ahead=SPLIT_SLOTS)
            dve.wait_ge(jobs_ready, 1)
            n_jobs = dve.value_load(jobs_i[0:1, 15:16], min_val=EXPERTS, max_val=MAX_JOBS - 1)
            with dve.Fori(1, n_jobs) as j:
                ffn_pass(len(FFN) * j + MOE_AT, MOE_AT, j + 1, 1, job=j)
            for half in range(2):
                y = slice(half * BANK, (half + 1) * BANK)
                dve.wait_ge(y_hi_ready, n_jobs + half)
                v.scalar_tensor_tensor(y_lo[:, y], ps[:, 4 + half, :], slot_gate, y_hi[:, y], ALU.mult, ALU.subtract).then_inc(y_ready, 1)
            for t in range(TT):
                dve.wait_ge(tile_done, 3 + t + 1)
                x_two = x_res[:, t, :].rearrange("p (h n) -> p h n", h=2)
                v.tensor_tensor(x_two, x_two, ps[:, 2 + 4 * t:4 + 4 * t, :], ALU.add).then_inc(x_written, 1)
            for t in range(TT):
                mean_square(4, t)
            for t in range(TT):
                norm_rows(4, t)

        @block.tensor
        def _(pe):
            mm = nc.tensor.matmul

            def product(dst, a_hi, a_lo, b_hi, b_lo, start, stop):
                mm(dst, a_hi, b_lo, start=start, stop=False)
                mm(dst, a_lo, b_hi, start=False, stop=False)
                return mm(dst, a_hi, b_hi, start=False, stop=stop)

            def unit_ready(n):
                pe.wait_ge(lo_ready, n + 1)

            def h_part(t, k, tile):
                a = (tile * KT + k) * P
                return t[:, a:a + P]

            def turn_rows(ready, value, tiles):
                for t in tiles:
                    pe.wait_ge(ready, value + t)
                    for k in range(KT):
                        a = (k % 4) * P
                        last = nc.tensor.transpose(ps[:, 2 * t + k // 4, a:a + P], rows[:, t, k * P:(k + 1) * P], identity)
                        if k % 4 == 3:
                            last.then_inc(rows_turned, 1)

            def turn_heads(layer, pair, bank, columns):
                for s, c in enumerate(columns):
                    for t in range(TT):
                        a = s * SEQ + t * P
                        last = nc.tensor.transpose(ps[:, bank, a:a + P], proj[:, t, c + pair * P:c + (pair + 1) * P], identity)
                last.then_inc(qk_turned, 1)

            def head_of(pair0, h):
                return (qk_t[(h % 2) * HEAD:(h % 2 + 1) * HEAD, pair0 + h // 2, s, :] for s in range(2))

            def beside(layer, n):
                if n == GMLP_AT:
                    pe.wait_ge(gmlp_masked, layer + 1)
                    pe.wait_ge(gv_ready, layer + 1)
                    for g in range(GROUPS):
                        w = gmlp_w[:, (layer * GROUPS + g) * CHUNK:(layer * GROUPS + g + 1) * CHUNK]
                        last = mm(ps[:, 7, g * P:(g + 1) * P], w, proj[:, :, C_GV + g * HEAD:C_GV + (g + 1) * HEAD], start=True, stop=True)
                    last.then_inc(gmlp_out, 1)
                if n == ATT_TURN_AT:
                    pe.wait_ge(proj_act, IN_CHUNKS * layer + 4)
                    pe.wait_ge(proj_dve, IN_CHUNKS * layer + 4)
                    for pair in range(PAIRS):
                        turn_heads(layer, pair, 4 + pair, (C_MQ, C_MK))
                if n - ATT_AT - 2 in range(PAIRS):
                    for h in pair_heads(n - ATT_AT - 2):
                        pe.wait_ge(att_biased, HEADS * layer + min(h + 3, HEADS))
                        if h >= 2:
                            pe.wait_ge(att_stored, HEADS * layer + 2 * (h // 2))
                        pe.wait_ge(pt_ready, HEADS * layer + h + 1)
                        weigh_values(4 + h % 2, 3 * P, 4 + h % 2, 3 * P + HEAD, att_pt, h % 2, C_MV, h).then_inc(att_out, 1)
                if n - ATT_AT in range(PAIRS):
                    for h in pair_heads(n - ATT_AT):
                        if n == ATT_AT:
                            pe.wait_ge(qk_dve, 3 * layer + 2)
                            pe.wait_ge(qk_act, 3 * layer + 1)
                        else:
                            pe.wait_ge(att_biased, HEADS * layer + h - 1)
                        q, k = head_of(0, h)
                        mm(ps[:, 4 + h % 2, 0:P], q[:, 0:P], k[:, 0:P], start=True, stop=True)
                        mm(ps[:, 4 + h % 2, P:3 * P], q[:, P:], k, start=True, stop=True).then_inc(att_scored, 1)
                if n - ATT_AT - 1 in range(PAIRS):
                    for h in pair_heads(n - ATT_AT - 1):
                        pe.wait_ge(att_exped, HEADS * layer + h + 1)
                        if h < 2:
                            pe.wait_ge(gmlp_stored, layer + 1)
                        else:
                            pe.wait_ge(pt_ready, HEADS * layer + h - 1)
                        a = (h % 2) * 3 * P
                        for b in range(3):
                            last = nc.tensor.transpose(ps[:, 6 + h % 2, b * P:(b + 1) * P], att_p[:, a + b * P:a + (b + 1) * P], identity)
                        last.then_inc(p_turned, 1)
                if n == RET_TURN_AT:
                    pe.wait_ge(proj_act, IN_CHUNKS * layer + 6)
                    pe.wait_ge(proj_dve, IN_CHUNKS * layer + 6)
                    for pair in range(2):
                        turn_heads(layer, pair, 2 + pair, (C_RQ, C_RK))
                if n == RET_TURN_AT + 1:
                    pe.wait_ge(pt_ready, HEADS * (layer + 1))
                    turn_heads(layer, 2, 6, (C_RQ, C_RK))
                    pe.wait_ge(qk_dve, 3 * (layer + 1))
                    pe.wait_ge(qk_act, 3 * layer + 2)
                    retention_scores(layer, (0, 1))

            def weigh_values(bank0, at0, bank1, at1, weights, buffer, column, h):
                a = buffer * 3 * P
                value = lambda t: proj[:, t, column + h * HEAD:column + (h + 1) * HEAD]
                mm(ps[:, bank0, at0:at0 + HEAD], weights[:, a:a + P], value(0), start=True, stop=True)
                mm(ps[:, bank1, at1:at1 + HEAD], weights[:, a + P:a + 2 * P], value(0), start=True, stop=False)
                return mm(ps[:, bank1, at1:at1 + HEAD], weights[:, a + 2 * P:a + 3 * P], value(1), start=False, stop=True)

            def retention_scores(layer, heads):
                for h in heads:
                    if h >= 2:
                        pe.wait_ge(ret_decayed, HEADS * layer + h - 1)
                    q, k = head_of(PAIRS, h)
                    mm(ps[:, 2 + h % 2, 0:SEQ], k[:, 0:P], q, start=True, stop=True)
                    mm(ps[:, 2 + h % 2, SEQ:SEQ + P], k[:, P:], q[:, P:], start=True, stop=True).then_inc(ret_scored, 1)

            def retention_outputs(layer, heads):
                for h in heads:
                    pe.wait_ge(ret_decayed, HEADS * layer + h + 1)
                    weigh_values(0, h * HEAD, 1, h * HEAD, ret_w, h % RET_BUFFERS, C_RV, h).then_inc(ret_out, 1)

            def turn_block(bank, tiles, ks):
                for i, (t, k) in enumerate((t, k) for t in tiles for k in ks):
                    last = nc.tensor.transpose(ps[:, bank, i * P:(i + 1) * P], rows[:, t, k * P:(k + 1) * P], identity)
                last.then_inc(rows_turned, 1)

            def project_out(layer, t, u, js=(0, 1)):
                n = OUT_AT[layer] + u
                unit_ready(n)
                for j in js:
                    k = OUT_UNITS[u][j]
                    for half in range(2):
                        w = (part(x, n % SPLIT_SLOTS, 2, j, half * BANK, BANK, D_MODEL) for x in (w_hi, w_lo))
                        last = product(ps[:, 4 + 2 * t + half, :], h_part(h_hi, k, t), h_part(h_lo, k, t), *w, start=k == 6, stop=k == 2)
                return last

            def mixer(layer):
                h_tile = NORM_TURNED[2 * layer]
                for t in range(TT):
                    turn_rows(rows_ready, 2 * TT * layer + 1, (t,))
                    width = IN_WIDTHS[IN_ORDER[0]]
                    for h in range(2):
                        n = IN_AT[layer] + h
                        pe.wait_ge(h_ready, h_tile + 2 * t + h + 1)
                        unit_ready(n)
                        for k in range(4):
                            w = (part(x, n % SPLIT_SLOTS, 4, k, 0, width, width) for x in (w_hi, w_lo))
                            last = product(ps[:, t, 0:width], h_part(h_hi, 4 * h + k, t), h_part(h_lo, 4 * h + k, t), *w, start=h == 0 and k == 0, stop=h == 1 and k == 3)
                        if t == TT - 1:
                            last.then_inc(unit_used, 1)
                for i, (c, h) in enumerate(IN_UNITS):
                    n = IN_AT[layer] + i
                    q = IN_ORDER.index(c)
                    if i >= 2:
                        if h == 0 and q >= 2:
                            pe.wait_ge(proj_act, IN_CHUNKS * layer + q - 1)
                            pe.wait_ge(proj_dve, IN_CHUNKS * layer + q - 1)
                        unit_ready(n)
                        width = IN_WIDTHS[c]
                        for k in range(4):
                            for t in range(TT):
                                w = (part(x, n % SPLIT_SLOTS, 4, k, 0, width, width) for x in (w_hi, w_lo))
                                last = product(ps[:, 2 * (q % 2) + t, 0:width], h_part(h_hi, 4 * h + k, t), h_part(h_lo, 4 * h + k, t), *w,
                                               start=h == 0 and k == 0, stop=h == 1 and k == 3)
                        last.then_inc(unit_used, 1)
                    beside(layer, i)
                turned = OUT_TURNED[layer]
                turn_block(7, (0, 1), (6, 7))
                pe.wait_ge(att_stored, HEADS * (layer + 1))
                pe.wait_ge(qk_act, 3 * (layer + 1))
                turn_block(6, (0,), (3, 4, 5))
                retention_scores(layer, (2, 3))
                pe.wait_ge(proj_act, IN_CHUNKS * (layer + 1))
                pe.wait_ge(proj_dve, IN_CHUNKS * (layer + 1))
                retention_outputs(layer, (0, 1))
                retention_scores(layer, (4, 5))
                pe.wait_ge(h_ready, turned + 1)
                project_out(layer, 0, 0)
                retention_outputs(layer, (2, 3, 4, 5))
                turn_block(7, (1,), (3, 4, 5))
                pe.wait_ge(h_ready, turned + 2)
                project_out(layer, 0, 1)
                project_out(layer, 0, 2, (1,))
                pe.wait_ge(h_ready, turned + 3)
                project_out(layer, 1, 0).then_inc(unit_used, 1)
                project_out(layer, 1, 1).then_inc(unit_used, 1)
                for t in range(TT):
                    pe.wait_ge(mix_ready, TT * layer + t + 1)
                    turn_block(2 + t, (t,), (0, 1, 2))
                project_out(layer, 1, 2, (1,))
                for t in range(TT):
                    pe.wait_ge(h_ready, turned + 4 + t)
                    last = project_out(layer, t, 2, (0,))
                    if t == TT - 1:
                        last.then_inc(unit_used, 1)
                    project_out(layer, t, 3).then_inc(unit_used if t == TT - 1 else tile_done, 1)

            def ffn_pass(n0, s0, passes, nt, job=None):
                def turn(c):
                    pe.wait_ge(act_ready, passes * FF_CHUNKS + c + 1)
                    if nt == 2 and c:
                        pe.wait_ge(silu_done, passes * FF_CHUNKS + min(c + 2, FF_CHUNKS))
                    if c:
                        pe.wait_ge(actt_ready, passes * FF_CHUNKS + c)
                    elif has_last(job):
                        pe.wait_ge(x_added, TT * job)
                    for t in range(nt):
                        for f in range(4):
                            last = nc.tensor.transpose(ps[:, turned_bank(c, nt) + t, f * P:(f + 1) * P], act_s[:, t * BANK + f * P:t * BANK + (f + 1) * P], identity)
                    last.then_inc(act_turned, 1)

                def multiply(i, tiles):
                    kind, c, h = FFN[i]
                    s = (s0 + i) % SPLIT_SLOTS
                    unit_ready(n0 + i)
                    for k in range(2 if kind == "down" else 4):
                        for t in tiles:
                            if kind == "down":
                                a = t * BANK + (2 * h + k) * P
                                hi, lo = (x[:, a:a + P] for x in turned_activations(c, nt))
                                for half in range(2):
                                    w = (part(x, s, 2, k, half * BANK, BANK, D_MODEL) for x in (w_hi, w_lo))
                                    last = product(ps[:, 4 + 2 * t + half, :], hi, lo, *w,
                                                   start=c == 0 and h == 0 and k == 0, stop=c == FF_CHUNKS - 1 and h == 1 and k == 1)
                            else:
                                w = (part(x, s, 4, k) for x in (w_hi, w_lo))
                                last = product(ps[:, (0 if kind == "gate" else nt) + t, :], h_part(h_hi, 4 * h + k, t), h_part(h_lo, 4 * h + k, t), *w,
                                               start=h == 0 and k == 0, stop=h == 1 and k == 3)
                    return last

                for i, (kind, c, h) in enumerate(FFN):
                    if job is not None and i < 2:
                        pe.wait_ge(h_ready, JOBS_TURNED + 2 * job + (i + 1))
                    if kind == "gate" and h == 0:
                        if nt == 2 and c >= 3:
                            pe.wait_ge(actt_ready, passes * FF_CHUNKS + c - 1)
                        elif c >= 1:
                            pe.wait_ge(silu_done, passes * FF_CHUNKS + c)
                    if kind == "up" and h == 0 and c >= 1:
                        pe.wait_ge(act_ready, passes * FF_CHUNKS + c)
                    if kind == "down" and h == 0:
                        pe.wait_ge(actt_ready, passes * FF_CHUNKS + c + 1)
                    if nt == 2 and i in (0, len(FFN) - 2):
                        for t in range(TT):
                            if i == 0:
                                turn_rows(rows_ready, TT + 1, (t,))
                            for u in (i, i + 1):
                                if i == 0:
                                    pe.wait_ge(h_ready, NORM_TURNED[1] + 2 * t + u + 1)
                                last = multiply(u, (t,))
                                if t == TT - 1:
                                    last.then_inc(unit_used, 1)
                            if i and t == 0:
                                last.then_inc(tile_done, 1)
                    elif nt == 1 or i not in (1, len(FFN) - 1):
                        multiply(i, range(nt)).then_inc(unit_used, 1)
                    if has_last(job) and i == 3:
                        scatter(job)
                    if job is not None and i == 7:
                        turn_slots(job)
                    if job is not None and i == GATHER_AFTER:
                        gather(job + 1)
                    for c2 in range(FF_CHUNKS):
                        if TRANSPOSE_AFTER[c2] == i:
                            turn(c2)

            def gather(job):
                pe.wait_ge(slots_ready, job + 1)
                if has_last(job):
                    pe.wait_ge(slots_t_ready, job)
                for k in range(KT):
                    for step, (rows_part, t) in enumerate((r, t) for r in rows_b[::-1] for t in range(TT)):
                        a = t * D_MODEL + k * P
                        last = mm(ps[:, 2 + k // 4, (k % 4) * P:(k % 4 + 1) * P], rows_part[:, a:a + P], slots[:, t * P:(t + 1) * P],
                                  start=step == 0, stop=step == 3 * TT - 1)
                    if k % 4 == 3:
                        last.then_inc(gathered, 1)

            def turn_slots(job):
                if has_last(job):
                    pe.wait_ge(x_added, TT * job)
                pe.wait_ge(weight_copied, job + 1)
                for t in range(TT):
                    nc.tensor.transpose(ps[:, 2, t * P // 2:(t + 1) * P // 2].bitcast(BF16), slots[:, t * P:(t + 1) * P], identity_b)
                for t in range(TT):
                    last = mm(ps[:, 2, P:P + 3], slots[:, t * P:(t + 1) * P], cur_weight[:, 3 * t:3 * t + 3], start=t == 0, stop=t == TT - 1)
                last.then_inc(slots_turned, 1)

            def scatter(job):
                pe.wait_ge(y_ready, job)
                for t in range(TT):
                    for half in range(2):
                        last = scatter_half(t, half)
                last.then_inc(scattered, 1)

            def scatter_half(t, half):
                at = slots_t[:, t * P:(t + 1) * P]
                dst = ps[:, 2 + 4 * t + half, :]
                mm(dst, at, y_lo[:, half * BANK:(half + 1) * BANK], start=True, stop=False)
                return mm(dst, at, y_hi[:, half * BANK:(half + 1) * BANK], start=False, stop=True)

            pe.wait_ge(tables_landed, 16)
            mixer(0)
            ffn_pass(DENSE_AT, DENSE_AT, 0, 2)
            mixer(1)
            pe.wait_ge(router_ready, 1)
            for t in range(TT):
                turn_rows(rows_ready, 3 * TT + 1, (t,))
                for k in range(KT):
                    pe.wait_ge(h_ready, NORM_TURNED[3] + 2 * t + k // 4 + 1)
                    for a in (h_lo, h_hi):
                        last = mm(ps[0:2 * EXPERTS, 4 + t, 0:P], router_s[:, k * 2 * EXPERTS:(k + 1) * 2 * EXPERTS], h_part(a, k, t),
                                  start=k == 0 and a is h_lo, stop=k == KT - 1 and a is h_hi)
                last.then_inc(logits_summed, 1)
            for t in range(TT):
                pe.wait_ge(logits_copied, t + 1)
                last = nc.tensor.transpose(ps[:, 2, t * 2 * EXPERTS:(t + 1) * 2 * EXPERTS], logits_t[0:2 * EXPERTS, t * P:(t + 1) * P],
                                           identity[0:2 * EXPERTS, 0:2 * EXPERTS])
            last.then_inc(logits_ready, 1)
            pe.wait_ge(tables_b_ready, 1)
            pe.wait_ge(mask_ready, 1)
            mm(ps[:, 3, 0:8], causal_b, mask[:, 0, :], start=True, stop=True)
            mm(ps[:, 3, 8:16], causal_b, mask[:, 1, :], start=True, stop=False)
            mm(ps[:, 3, 8:16], ones_b, mask[:, 0, :], start=False, stop=True)
            mm(ps[:, 3, 16:24], ones_b, mask[:, 0, :], start=True, stop=False)
            mm(ps[:, 3, 16:24], ones_b, mask[:, 1, :], start=False, stop=True).then_inc(counted, 1)
            pe.wait_ge(rows_b_ready, 2 * TT)
            pe.wait_ge(rows_b_done, TT)
            gather(0)
            ffn_pass(MOE_AT, MOE_AT, 1, 1, job=0)
            pe.wait_ge(jobs_ready, 1)
            n_jobs = pe.value_load(jobs_i[0:1, 15:16], min_val=EXPERTS, max_val=MAX_JOBS - 1)
            with pe.Fori(1, n_jobs) as j:
                ffn_pass(len(FFN) * j + MOE_AT, MOE_AT, j + 1, 1, job=j)
            for t in range(TT):
                for half in range(2):
                    if t == 0:
                        pe.wait_ge(y_ready, n_jobs + half)
                    last = scatter_half(t, half)
                last.then_inc(tile_done, 1)


_INS = ["x", "l0_mix_norm", "l0_w_in", "l0_w_out", "l0_ffn_norm", "l0_w_gate", "l0_w_up", "l0_w_down",
        "l1_mix_norm", "l1_w_in", "l1_w_out", "l1_ffn_norm", "l1_we_gate", "l1_we_up", "l1_we_down", "final_norm"]


def kernel(**inputs):
    import concourse.bacc as bacc
    from concourse.bass_utils import run_bass_kernel_spmd

    nc = bacc.Bacc("TRN2", target_bir_lowering=False, num_devices=1)
    arrays = {n: np.ascontiguousarray(inputs[n]) for n in _INS}
    arrays["gmlp_w"] = np.ascontiguousarray(
        np.stack([np.asarray(inputs[f"l{n}_gmlp_w"]).transpose(2, 0, 1).reshape(CHUNK, -1) for n in range(2)]))
    arrays["gmlp_bias"] = np.ascontiguousarray(
        np.concatenate([np.asarray(inputs[f"l{n}_gmlp_b"]).T for n in range(2)], axis=1))
    arrays["router"] = np.ascontiguousarray(
        np.asarray(inputs["l1_router"]).reshape(KT, P, EXPERTS).transpose(1, 0, 2).reshape(P, -1))
    arrays["tables"] = shape_tables()
    ins = {n: nc.dram_tensor(f"in_{n}", a.shape, mybir.dt.from_np(a.dtype), kind="ExternalInput").ap() for n, a in arrays.items()}
    out = nc.dram_tensor("out", (1, SEQ, D_MODEL), F32, kind="ExternalOutput").ap()
    hybrid_trunk(nc, ins, out)
    got = run_bass_kernel_spmd(nc, [{f"in_{n}": a for n, a in arrays.items()}], core_ids=[0])
    return got.results[0]["out"]
```
